# Optimizing a Trainium2 kernel written in Bass

```python
import jax, jax.numpy as jnp
from jax import lax
import numpy as np

D_MODEL = 1024
BATCH = 1
SEQ = 256
DEPTH = 2

GRID_W = 64
CTX_LEN = 256
ROPE_THETA = 10000.0
EPS = 1e-6
Q_BLOCK = 128
MLA_HEADS = 8
MLA_Q_RANK = 384
MLA_KV_RANK = 256
MLA_NOPE = 64
MLA_ROPE = 32
MLA_V = 64
GQA_HEADS = 8
GQA_KV_HEADS = 2
GQA_GROUP = GQA_HEADS // GQA_KV_HEADS
GQA_HEAD_DIM = 64
GLA_HEADS = 4
GLA_DK = D_MODEL // 2 // GLA_HEADS
GLA_DV = D_MODEL // GLA_HEADS
GLA_GATE_RANK = 16
GLA_GATE_NORM = 16.0
GLA_CHUNK = 32
FFN_DIM = 2816
N_EXPERTS = 8
TOP_K = 2
EXPERT_DIM = 3584

N_EVEN = (DEPTH + 1) // 2
N_ODD = DEPTH // 2

ATTN_WIDTHS = (MLA_Q_RANK, MLA_KV_RANK, MLA_ROPE, GQA_HEADS * GQA_HEAD_DIM,
               GQA_KV_HEADS * GQA_HEAD_DIM, GQA_KV_HEADS * GQA_HEAD_DIM)
ATTN_IN = MLA_Q_RANK + MLA_KV_RANK + MLA_ROPE + (GQA_HEADS + 2 * GQA_KV_HEADS) * GQA_HEAD_DIM
ATTN_MIX = MLA_HEADS * MLA_V + GQA_HEADS * GQA_HEAD_DIM
GLA_WIDTHS = (GLA_HEADS * GLA_DK, GLA_HEADS * GLA_DK, GLA_HEADS * GLA_DV, GLA_HEADS * GLA_DV,
              GLA_GATE_RANK, GLA_GATE_RANK)
GLA_IN = 2 * GLA_HEADS * GLA_DK + 2 * GLA_HEADS * GLA_DV + 2 * GLA_GATE_RANK
GLA_MIX = GLA_HEADS * GLA_DV

kernel_name = 'hybrid_mla_gqa_gla_moe_dit_block'

def rms_norm(x, g):
    x32 = x.astype(jnp.float32)
    y = x32 * lax.rsqrt(jnp.mean(x32 * x32, axis=-1, keepdims=True) + EPS)
    return (y * g).astype(x.dtype)

def modulate(h, shift, scale):
    return h * (1.0 + scale) + shift

def split_cols(z, widths):
    idx, acc = [], 0
    for w in widths[:-1]:
        acc += w
        idx.append(acc)
    return jnp.split(z, idx, axis=-1)

def to_heads(z, h):
    b, t, _ = z.shape
    return z.reshape(b, t, h, -1).transpose(0, 2, 1, 3)

def from_heads(o):
    b, h, t, d = o.shape
    return o.transpose(0, 2, 1, 3).reshape(b, t, h * d)

def rope_1d(x, pos):
    d = x.shape[-1]
    freqs = ROPE_THETA ** (-jnp.arange(0, d, 2, dtype=jnp.float32) / d)
    ang = pos.astype(jnp.float32)[:, None] * freqs[None, :]
    cos, sin = jnp.cos(ang), jnp.sin(ang)
    x32 = x.astype(jnp.float32)
    x1, x2 = x32[..., : d // 2], x32[..., d // 2:]
    return jnp.concatenate([x1 * cos - x2 * sin, x2 * cos + x1 * sin], axis=-1).astype(x.dtype)

def axial_rope(x, rows, cols):
    half = x.shape[-1] // 2
    return jnp.concatenate([rope_1d(x[..., :half], rows), rope_1d(x[..., half:], cols)], axis=-1)

def attend(q, k, v):
    s = jnp.einsum('bhgqd,bhkd->bhgqk', q, k, preferred_element_type=jnp.float32) * (q.shape[-1] ** -0.5)
    p = jax.nn.softmax(s, axis=-1)
    return jnp.einsum('bhgqk,bhkd->bhgqd', p.astype(v.dtype), v)

def blocked_attend(q, k, v):
    b, hk, g, t, d = q.shape
    nb = t // Q_BLOCK
    qb = jnp.moveaxis(q.reshape(b, hk, g, nb, Q_BLOCK, d), 3, 0)
    ob = lax.map(lambda qi: attend(qi, k, v), qb)
    return jnp.moveaxis(ob, 0, 3).reshape(b, hk, g, t, v.shape[-1])

def attn_project(u, w_in, q_a_norm, w_uq, kv_a_norm, w_ukv, qk_norm, rows, cols):
    b, t, _ = u.shape
    q_lat, kv_lat, k_rope, q_b, k_b, v_b = split_cols(u @ w_in, ATTN_WIDTHS)
    q_a = to_heads(rms_norm(q_lat, q_a_norm) @ w_uq, MLA_HEADS)
    kv_a = to_heads(rms_norm(kv_lat, kv_a_norm) @ w_ukv, MLA_HEADS)
    q_nope, q_rope = q_a[..., :MLA_NOPE], q_a[..., MLA_NOPE:]
    k_nope, v_a = kv_a[..., :MLA_NOPE], kv_a[..., MLA_NOPE:]
    k_rope = k_rope[:, None]
    q_b = rms_norm(to_heads(q_b, GQA_HEADS), qk_norm[0])
    k_b = rms_norm(to_heads(k_b, GQA_KV_HEADS), qk_norm[1])
    v_b = to_heads(v_b, GQA_KV_HEADS)
    if rows is not None:
        q_rope = axial_rope(q_rope, rows, cols)
        k_rope = axial_rope(k_rope, rows, cols)
        q_b = axial_rope(q_b, rows, cols)
        k_b = axial_rope(k_b, rows, cols)
    q_a = jnp.concatenate([q_nope, q_rope], axis=-1)[:, :, None]
    k_a = jnp.concatenate([k_nope, jnp.broadcast_to(k_rope, k_nope.shape[:-1] + (MLA_ROPE,))], axis=-1)
    q_b = q_b.reshape(b, GQA_KV_HEADS, GQA_GROUP, t, GQA_HEAD_DIM)
    return (q_a, k_a, v_a), (q_b, k_b, v_b)

def merge_heads(o_a, o_b):
    b, _, _, t, _ = o_a.shape
    o_a = o_a.transpose(0, 3, 1, 2, 4).reshape(b, t, -1)
    o_b = o_b.transpose(0, 3, 1, 2, 4).reshape(b, t, -1)
    return jnp.concatenate([o_a, o_b], axis=-1)

def attn_mixer(u_ctx, u_lat, w_in, q_a_norm, w_uq, kv_a_norm, w_ukv, qk_norm, w_out, rows, cols, ctx_out):
    (qa_c, ka_c, va_c), (qb_c, kb_c, vb_c) = attn_project(u_ctx, w_in, q_a_norm, w_uq, kv_a_norm, w_ukv, qk_norm, None, None)
    (qa_l, ka_l, va_l), (qb_l, kb_l, vb_l) = attn_project(u_lat, w_in, q_a_norm, w_uq, kv_a_norm, w_ukv, qk_norm, rows, cols)
    o_a = blocked_attend(qa_l, jnp.concatenate([ka_c, ka_l], axis=2), jnp.concatenate([va_c, va_l], axis=2))
    o_b = blocked_attend(qb_l, jnp.concatenate([kb_c, kb_l], axis=2), jnp.concatenate([vb_c, vb_l], axis=2))
    y_lat = merge_heads(o_a, o_b) @ w_out
    y_ctx = None
    if ctx_out:
        y_ctx = merge_heads(attend(qa_c, ka_c, va_c), attend(qb_c, kb_c, vb_c)) @ w_out
    return y_ctx, y_lat

def gla_chunked(q, k, v, log_a, s0):
    b, h, t, dk = q.shape
    dv = v.shape[-1]
    n = t // GLA_CHUNK

    def chunks(a):
        return jnp.moveaxis(a.astype(jnp.float32).reshape(b, h, n, GLA_CHUNK, a.shape[-1]), 2, 0)

    qc, kc, vc, ac = chunks(q), chunks(k), chunks(v), chunks(log_a)
    cum = jnp.cumsum(ac, axis=-2)
    cum_last = cum[..., -1:, :]
    q_dec = qc * jnp.exp(cum)
    k_intra = kc * jnp.exp(-cum)
    k_state = kc * jnp.exp(cum_last - cum)
    mask = jnp.tril(jnp.ones((GLA_CHUNK, GLA_CHUNK), jnp.float32))
    scores = jnp.einsum('nbhtk,nbhsk->nbhts', q_dec, k_intra) * mask
    o_intra = jnp.einsum('nbhts,nbhsv->nbhtv', scores, vc)

    def step(state, xs):
        q_n, k_n, v_n, cl_n = xs
        o_n = jnp.einsum('bhtk,bhkv->bhtv', q_n, state)
        state = jnp.exp(cl_n[..., 0, :])[..., None] * state + jnp.einsum('bhtk,bhtv->bhkv', k_n, v_n)
        return state, o_n

    s_final, o_inter = lax.scan(step, s0, (q_dec, k_state, vc, cum_last))
    o = jnp.moveaxis(o_intra + o_inter, 0, 2).reshape(b, h, t, dv)
    return o.astype(v.dtype), s_final

def gla_final_state(k, v, log_a):
    a = log_a.astype(jnp.float32)
    cum = jnp.cumsum(a, axis=-2)
    tail = cum[..., -1:, :] - cum
    return jnp.einsum('bhtk,bhtv->bhkv', k.astype(jnp.float32) * jnp.exp(tail), v.astype(jnp.float32))

def gla_project(u, w_in, w_gate2, b_gate):
    q, k, v, g, r_f, r_b = split_cols(u @ w_in, GLA_WIDTHS)
    q = to_heads(q, GLA_HEADS) * (GLA_DK ** -0.5)
    k = to_heads(k, GLA_HEADS)
    v = to_heads(v, GLA_HEADS)

    def log_decay(r, d):
        z = (r @ w_gate2[d] + b_gate[d]).astype(jnp.float32)
        return to_heads(jax.nn.log_sigmoid(z) / GLA_GATE_NORM, GLA_HEADS)

    return q, k, v, g, log_decay(r_f, 0), log_decay(r_b, 1)

def flip_t(a):
    return a[:, :, ::-1, :]

def gla_mixer(u_ctx, u_lat, w_in, w_gate2, b_gate, o_norm, w_out, ctx_out):
    qc, kc, vc, gc, afc, abc = gla_project(u_ctx, w_in, w_gate2, b_gate)
    ql, kl, vl, gl, afl, abl = gla_project(u_lat, w_in, w_gate2, b_gate)

    def finish(o, g):
        return (from_heads(rms_norm(o, o_norm)) * jax.nn.silu(g)) @ w_out

    y_ctx = None
    if ctx_out:
        zeros = jnp.zeros((qc.shape[0], GLA_HEADS, GLA_DK, GLA_DV), jnp.float32)
        oc_f, s_f = gla_chunked(qc, kc, vc, afc, zeros)
        oc_b, s_b = gla_chunked(flip_t(qc), flip_t(kc), flip_t(vc), flip_t(abc), zeros)
        y_ctx = finish(oc_f + flip_t(oc_b), gc)
    else:
        s_f = gla_final_state(kc, vc, afc)
        s_b = gla_final_state(flip_t(kc), flip_t(vc), flip_t(abc))
    ol_f, _ = gla_chunked(ql, kl, vl, afl, s_f)
    ol_b, _ = gla_chunked(flip_t(ql), flip_t(kl), flip_t(vl), flip_t(abl), s_b)
    y_lat = finish(ol_f + flip_t(ol_b), gl)
    return y_ctx, y_lat

def swiglu(u, w_gate, w_up, w_down):
    return (jax.nn.silu(u @ w_gate) * (u @ w_up)) @ w_down

def moe_swiglu(u, w_router, b_router, w_gate, w_up, w_down):
    logits = (u @ w_router).astype(jnp.float32) + b_router
    probs = jax.nn.softmax(logits, axis=-1)
    top_p, top_i = lax.top_k(probs, TOP_K)
    top_p = top_p / jnp.sum(top_p, axis=-1, keepdims=True)
    combine = jnp.einsum('btk,btke->bte', top_p, jax.nn.one_hot(top_i, N_EXPERTS, dtype=jnp.float32)).astype(u.dtype)
    y = jnp.zeros_like(u)
    for e in range(N_EXPERTS):
        y = y + combine[..., e:e + 1] * swiglu(u, w_gate[e], w_up[e], w_down[e])
    return y

def setup_inputs(seed: int = 0) -> dict:
    key = jax.random.key(seed)
    ks = iter(jax.random.split(key, 32))
    f32 = jnp.float32
    D = D_MODEL

    def normal(shape, scale=1.0):
        return jax.random.normal(next(ks), shape, f32) * scale

    def w(shape, fan_in, scale=1.0):
        return normal(shape, scale * fan_in ** -0.5)

    def gain(shape):
        return 1.0 + normal(shape, 0.05)

    return {
        'x': normal((BATCH, SEQ, D)),
        'c': normal((BATCH, D)),
        'ctx': normal((BATCH, CTX_LEN, D)),
        'c_ctx': normal((D,)),
        'mod_w': w((DEPTH, D, 6 * D), D, 0.5),
        'mod_b': normal((DEPTH, 6 * D), 0.02),
        'norm_g': gain((DEPTH, 4, D)),
        'attn_w_in': w((N_EVEN, D, ATTN_IN), D),
        'attn_q_norm': gain((N_EVEN, MLA_Q_RANK)),
        'attn_w_uq': w((N_EVEN, MLA_Q_RANK, MLA_HEADS * (MLA_NOPE + MLA_ROPE)), MLA_Q_RANK),
        'attn_kv_norm': gain((N_EVEN, MLA_KV_RANK)),
        'attn_w_ukv': w((N_EVEN, MLA_KV_RANK, MLA_HEADS * (MLA_NOPE + MLA_V)), MLA_KV_RANK),
        'attn_qk_norm': gain((N_EVEN, 2, GQA_HEAD_DIM)),
        'attn_w_out': w((N_EVEN, ATTN_MIX, D), ATTN_MIX),
        'gla_w_in': w((N_ODD, D, GLA_IN), D),
        'gla_w_gate2': w((N_ODD, 2, GLA_GATE_RANK, GLA_HEADS * GLA_DK), GLA_GATE_RANK),
        'gla_b_gate': normal((N_ODD, 2, GLA_HEADS * GLA_DK), 0.1),
        'gla_o_norm': gain((N_ODD, GLA_DV)),
        'gla_w_out': w((N_ODD, GLA_MIX, D), GLA_MIX),
        'ffn_w_gate': w((N_EVEN, D, FFN_DIM), D),
        'ffn_w_up': w((N_EVEN, D, FFN_DIM), D),
        'ffn_w_down': w((N_EVEN, FFN_DIM, D), FFN_DIM),
        'moe_w_router': w((N_ODD, D, N_EXPERTS), D),
        'moe_b_router': normal((N_ODD, N_EXPERTS), 0.01),
        'moe_w_gate': w((N_ODD, N_EXPERTS, D, EXPERT_DIM), D),
        'moe_w_up': w((N_ODD, N_EXPERTS, D, EXPERT_DIM), D),
        'moe_w_down': w((N_ODD, N_EXPERTS, EXPERT_DIM, D), EXPERT_DIM),
    }

def reference(x, c, ctx, c_ctx, mod_w, mod_b, norm_g, attn_w_in, attn_q_norm, attn_w_uq, attn_kv_norm,
              attn_w_ukv, attn_qk_norm, attn_w_out, gla_w_in, gla_w_gate2, gla_b_gate, gla_o_norm, gla_w_out,
              ffn_w_gate, ffn_w_up, ffn_w_down, moe_w_router, moe_b_router, moe_w_gate, moe_w_up, moe_w_down):
    t = x.shape[1]
    ROWS = t // GRID_W
    rows = jnp.repeat(jnp.arange(ROWS, dtype=jnp.int32), GRID_W)
    cols = jnp.tile(jnp.arange(GRID_W, dtype=jnp.int32), ROWS)

    def channel_mixer(u, layer):
        i = layer // 2
        if layer % 2 == 0:
            return swiglu(u, ffn_w_gate[i], ffn_w_up[i], ffn_w_down[i])
        return moe_swiglu(u, moe_w_router[i], moe_b_router[i], moe_w_gate[i], moe_w_up[i], moe_w_down[i])

    h_lat, h_ctx = x, ctx
    for layer in range(DEPTH):
        i = layer // 2
        last = layer == DEPTH - 1
        g = norm_g[layer]
        m_lat = [m[:, None, :] for m in jnp.split(jax.nn.silu(c) @ mod_w[layer] + mod_b[layer], 6, axis=-1)]
        m_ctx = jnp.split(jax.nn.silu(c_ctx) @ mod_w[layer] + mod_b[layer], 6, axis=-1)
        u_lat = modulate(rms_norm(h_lat, g[0]), m_lat[0], m_lat[1])
        u_ctx = modulate(rms_norm(h_ctx, g[0]), m_ctx[0], m_ctx[1])
        if layer % 2 == 0:
            y_ctx, y_lat = attn_mixer(u_ctx, u_lat, attn_w_in[i], attn_q_norm[i], attn_w_uq[i], attn_kv_norm[i],
                                      attn_w_ukv[i], attn_qk_norm[i], attn_w_out[i], rows, cols, not last)
        else:
            y_ctx, y_lat = gla_mixer(u_ctx, u_lat, gla_w_in[i], gla_w_gate2[i], gla_b_gate[i], gla_o_norm[i],
                                     gla_w_out[i], not last)
        h_lat = h_lat + m_lat[2] * rms_norm(y_lat, g[1])
        u_lat = modulate(rms_norm(h_lat, g[2]), m_lat[3], m_lat[4])
        h_lat = h_lat + m_lat[5] * rms_norm(channel_mixer(u_lat, layer), g[3])
        if not last:
            h_ctx = h_ctx + m_ctx[2] * rms_norm(y_ctx, g[1])
            u_ctx = modulate(rms_norm(h_ctx, g[2]), m_ctx[3], m_ctx[4])
            h_ctx = h_ctx + m_ctx[5] * rms_norm(channel_mixer(u_ctx, layer), g[3])
    return h_lat


_drawn_inputs = setup_inputs


def setup_inputs(seed=0):
    import zlib

    import numpy as np

    out = dict(_drawn_inputs(seed))
    spreads = {}
    factors = {'attn_q_norm': 4.08, 'attn_qk_norm': 2.73, 'gla_b_gate': 3.305, 'moe_b_router': 3.44}
    for name, (base, spread) in spreads.items():
        noise = np.random.default_rng([zlib.crc32(name.encode()), seed]).standard_normal(out[name].shape)
        drawn = base * np.exp(spread * noise) if base else spread * noise
        out[name] = __import__('jax').numpy.asarray(drawn.astype(out[name].dtype))
    for name, factor in factors.items():
        out[name] = (out[name] * factor).astype(out[name].dtype)
    return out
```

```python
import concourse.bass as bass
from concourse import mybir
from contextlib import ExitStack

F32 = mybir.dt.float32
F32R = mybir.dt.float32r
I32 = mybir.dt.int32
ALU = mybir.AluOpType
ACT = mybir.ActivationFunctionType
AX = mybir.AxisListType

P = 128
D = 1024
KD = D // P
TILES = 4
LAT = (2, 3)
EPS = 1e-6
Q_RANK, KV_RANK = 384, 256
HEADS, ROPE_M, NOPE, DV = 8, 32, 64, 64
DQ = NOPE + ROPE_M
GQ, GKV, GD = 8, 2, 64
ZW = 1440
Z_KV, Z_ROPE, Z_Q, Z_K, Z_V = 384, 640, 672, 1184, 1312
F_FFN = 2816
NF = F_FFN // P
GH, GDK, GDV, GRANK = 4, 128, 256, 16
CHUNK = 32
E_N, E_DIM = 8, 3584
EF = E_DIM // P
EJ = E_DIM // 512
MOD_STEP = 7
MG, MG0 = 12, 4

RAW_N = 3
SPLIT_N = 3
UNIT = 2048
HALF = UNIT // 2

C_ID, C_ONE, C_TRI_F, C_TRI_B = 0, 128, 256, 768
C_PAIR, C_KEEP = 1280, 1296
C_MASK, C_IOTA, C_ROPE, C_ALL = 1296, 2064, 2320, 2512


def hybrid_block(nc, x, cond, ctx, c_ctx, mod_w, mod_b, norm_g, attn_w_in, attn_q_norm, attn_w_uq, attn_kv_norm,
                 attn_w_ukv, attn_qk_norm, attn_w_out, gla_w_in, gla_w_gate2, gla_b_gate, gla_o_norm, gla_w_out,
                 ffn_w_gate, ffn_w_up, ffn_w_down, moe_w_router, moe_b_router, moe_w_gate, moe_w_up, moe_w_down,
                 consts, out):
    units = []

    def rows(w, r0, nk, c0, n):
        return w[r0:r0 + nk * P, c0:c0 + n].rearrange("(k p) n -> p k n", p=P)

    def stream(w, r0, nk, c0, n):
        units.append((rows(w, r0, nk, c0, n), nk, n))

    def mod_units(a, b):
        for g in range(a, b):
            for kh in range(2):
                stream(mod_w[g // MG], 512 * kh, 4, 512 * (g % MG), 512)

    mod_units(0, MG0)
    for n in range(3):
        for kh in range(2):
            stream(attn_w_in[0], 512 * kh, 4, 480 * n, 480)
    for n in range(2):
        stream(attn_w_uq[0], 0, 3, 384 * n, 384)
    stream(attn_w_ukv[0], 0, 2, 0, 1024)
    mod_units(MG0, MG)
    for n in range(2):
        for kh in range(2):
            stream(attn_w_out[0], 512 * kh, 4, 512 * n, 512)
    for j in range(NF // 2):
        stream(ffn_w_gate[0], 0, KD, 256 * j, 256)
        stream(ffn_w_up[0], 0, KD, 256 * j, 256)
        mod_units(MG + j, MG + j + 1)
    mod_units(2 * MG - 1, 2 * MG)
    DOWN = [(f, min(4, NF - f)) for f in range(0, NF, 4)]
    for n in range(2):
        for f, m in DOWN:
            stream(ffn_w_down[0], P * f, m, 512 * n, 512)
    stream(gla_w_in[0], 0, KD, 3072, 32)
    G_COLS = [512, 1024, 1536, 0, 2048, 2560]
    for c0 in G_COLS:
        for kh in range(2):
            stream(gla_w_in[0], 512 * kh, 4, c0, 512)
    for n in range(2):
        for kh in range(2):
            stream(gla_w_out[0], 512 * kh, 4, 512 * n, 512)
    N_PRE = len(units)
    PER_E = 6 * EJ
    assert PER_E % RAW_N == 0 and PER_E % SPLIT_N == 0

    with ExitStack() as es:
        BASE = (nc.sbuf_base + 63) // 64 * 64

        offset = [0]

        def region(floats):
            at = offset[0]
            offset[0] += floats
            return at

        def place(name, at, shape, dt=F32):
            return nc.alloc_sbuf_tensor_at(name, [P] + shape, dt, offset=BASE + 4 * at)

        R_K = region(C_KEEP)
        R_H = region(4096)
        R_U = region(8192)
        R_RAW = region(RAW_N * UNIT)
        R_SP = region(2 * SPLIT_N * UNIT)
        R_AR = region(14336)
        R_G = region(2048)
        R_T = region(3072)
        R_S = region(1264)
        es.enter_context(nc.sbuf_tensor("fence", [P, offset[0] + 32], F32))

        K = place("K", R_K, [C_KEEP])
        h = place("h", R_H, [TILES, D])
        uT_hi = place("uT_hi", R_U, [KD, 512], F32R)
        uT_lo = place("uT_lo", R_U + 4096, [KD, 512], F32R)
        raw = place("raw", R_RAW, [RAW_N, UNIT])
        w_hi = place("w_hi", R_SP, [SPLIT_N, UNIT], F32R)
        w_lo = place("w_lo", R_SP + SPLIT_N * UNIT, [SPLIT_N, UNIT], F32R)
        Gb = place("Gb", R_G, [2, D])
        hn = place("hn", R_T, [2, D])
        uf = place("uf", R_T + 2048, [D])
        vecs = place("vecs", R_S, [181])
        cv = place("cv", R_S + 1232, [KD, 4], F32R)
        modT = place("modT", R_S + 184, [2, 48, 2])
        Am = place("Am", R_S + 376, [4, KD, 2])
        Gm = place("Gm", R_S + 440, [4, KD, 2])
        bc = place("bc", R_S + 504, [384])
        st = place("st", R_S + 888, [4, 48])
        sm = place("sm", R_S + 1080, [32])
        bt = place("bt", R_S + 1112, [2, 2, 8])
        ecol = place("ecol", R_S + 1144, [8])
        cnt = place("cnt", R_S + 1152, [16], I32)

        rowsA = place("rowsA", R_AR, [P])
        rowsB = place("rowsB", R_AR + 128, [P])
        rowC = place("rowC", R_AR + 256, [384])
        rope = place("rope", R_G, [2, 96])
        z = place("z", R_AR, [TILES, ZW])
        qa = place("qa", R_AR + 5760, [TILES, 768])
        ka = place("ka", R_AR + 8832, [TILES, 768])
        va = place("va", R_AR + 11904, [TILES, 512])
        mrow = [place("mrow0", R_U + 4096, [2, 512]), place("mrow1", R_AR + 512 * NF, [2, 512])]
        qT = place("qT", R_U, [2, 512])
        kT = place("kT", R_U + 1024, [2, 512])
        Pr = place("Pr", R_U + 5120, [3, 512])
        PT = place("PT", R_U + 6656, [3, 512])
        y_attn = place("y_attn", R_AR, [TILES, D])
        hT = place("hT", R_AR, [NF, 512])
        sil = place("sil", R_T, [2, 512])
        hs = place("hs", R_T + 1024, [2, 2, 512], F32R)
        y_ffn = place("y_ffn", R_U, [TILES, D])
        g_q = place("g_q", R_AR, [2, 512])
        g_k = place("g_k", R_AR + 1024, [TILES, 512])
        g_v = place("g_v", R_AR + 3072, [TILES, D])
        g_g = place("g_g", R_AR + 7168, [2, D])
        g_a = place("g_a", R_AR + 9216, [TILES, 2, 512])
        g_C = place("g_C", R_AR + 13312, [2, 256])
        g_qd = place("g_qd", R_AR + 13824, [2, 256])
        g_qf = place("g_qf", R_AR, [2, 2, 256])
        g_AT = place("g_AT", R_AR + 1024, [2, 2, 384])
        g_o = place("g_o", R_AR + 9216, [2, D])
        g_qT = place("g_qT", R_U, [GH, 256])
        g_kT = place("g_kT", R_U + 1024, [GH, 256])
        g_S = place("g_S", R_U + 2048, [2, GH, 256])
        g_KX = place("g_KX", R_U + 4096, [2, 1536])
        rT = place("rT", R_U + 4096, [2, 512])
        wg2 = place("wg2", R_U + 5120, [2, 512])
        rtok = place("rtok", R_T, [TILES, 32])
        ebuf = place("ebuf", R_T + 1024, [2, 512])
        mask = place("mask", R_G, [2, 384])
        ug_hi = place("ug_hi", R_U, [KD, 256], F32R)
        ug_lo = place("ug_lo", R_U + 2048, [KD, 256], F32R)
        y_gla = place("y_gla", R_AR, [2, D])
        Pm = place("Pm", R_U + 4096, [2, 256])
        Pc = place("Pc", R_U + 4608, [2, 256])
        Wc = place("Wc", R_U + 5120, [2, 256])
        e_sil = place("e_sil", R_U + 5632, [2, 512])
        e_h = place("e_h", R_U + 6656, [2, 512])
        iota = place("iota", R_U + 7680, [256])
        rt = place("rt", R_U + 7936, [256])
        eT_hi = place("eT_hi", R_AR, [EF, 256], F32R)
        eT_lo = place("eT_lo", R_AR + EF * 256, [EF, 256], F32R)
        y_e = place("y_e", R_G, [2, D])
        y_acc = place("y_acc", R_H, [2, D])
        wr = rt[:, 0:64].rearrange("p (k e) -> p k e", e=E_N)
        lg, pb_, eq, cs, f1, f2, sel, cw = (rt[:, 64 + 16 * i:80 + 16 * i].rearrange("p (t e) -> p t e", e=E_N)
                                            for i in range(8))
        mx, mx2, zs = (rt[:, 192 + 2 * i:194 + 2 * i] for i in range(3))
        brow = rt[:, 200:208]
        tab = place("tab", R_S + 1168, [6 * 9])

        banks = es.enter_context(nc.psum_tensor("banks", [P, 8, 512], F32))

        def sem(name):
            return es.enter_context(nc.semaphore(name))

        const_in, h_in, late_in = sem("const_in"), sem("h_in"), sem("late_in")
        raw_in = [[sem(f"raw_in{i}_{half}") for half in range(2)] for i in range(RAW_N)]
        mod_cols_done = sem("mod_cols_done")
        hi_ready, lo_ready, weights_used = sem("hi_ready"), sem("lo_ready"), sem("weights_used")
        dve_took, act_took, bank0_took = sem("dve_took"), sem("act_took"), sem("bank0_took")
        dve_step, act_step, pool_step = sem("dve_step"), sem("act_step"), sem("pool_step")
        setup_pe, cv_ready, c_silu = sem("setup_pe"), sem("cv_ready"), sem("c_silu")
        ss_ready, var_ready, guess_ready, rstd_ready = (sem("ss_ready"), sem("var_ready"), sem("guess_ready"),
                                                        sem("rstd_ready"))
        hn_ready, norm_tr, u_ready, h_new = sem("hn_ready"), sem("norm_tr"), sem("u_ready"), sem("h_new")
        z_ready, lat_scaled, lat_tr, lat_split = sem("z_ready"), sem("lat_scaled"), sem("lat_tr"), sem("lat_split")
        ukv_mm, rope_done = sem("ukv_mm"), sem("rope_done")
        q_tr, k_tr, q_sb, k_sb = sem("q_tr"), sem("k_tr"), sem("q_sb"), sem("k_sb")
        s_done, nb_ready, exp_done, p_tr, pt_sb, pv_done, o_sb = (sem("s_done"), sem("nb_ready"), sem("exp_done"),
                                                                  sem("p_tr"), sem("pt_sb"), sem("pv_done"),
                                                                  sem("o_sb"))
        o_tr, mods_ready, diag_ready, gate_mm, gate_rows = (sem("o_tr"), sem("mods_ready"), sem("diag_ready"),
                                                            sem("gate_mm"), sem("gate_rows"))
        y_act = sem("y_act")
        silu_ready, ffn_h, hs_ready, hs_used = sem("silu_ready"), sem("ffn_h"), sem("hs_ready"), sem("hs_used")
        r_tr, r_sb, z2_mm, e_ln, a_ready = (sem("r_tr"), sem("r_sb"), sem("z2_mm"), sem("e_ln"),
                                                  sem("a_ready"))
        rt_one, rt_sb = sem("rt_one"), sem("rt_sb")
        tail_mm, tail_sb, tail_exp, ks_ready, s0_mm, gt_mm, gt_sb, kx_zero = (
            sem("tail_mm"), sem("tail_sb"), sem("tail_exp"), sem("ks_ready"), sem("s0_mm"), sem("gt_mm"),
            sem("gt_sb"), sem("kx_zero"))
        cum_mm, cum_sb, dec_exp, dec_ready, at_mm, at_ready, go_mm, go_sb, go_ready, got_mm = (
            sem("cum_mm"), sem("cum_sb"), sem("dec_exp"), sem("dec_ready"), sem("at_mm"), sem("at_ready"),
            sem("go_mm"), sem("go_sb"), sem("go_ready"), sem("got_mm"))
        uf_ready, logit_mm, lg_ready, lg_exp, sel_ready, rank_mm, tab_ready = (
            sem("uf_ready"), sem("logit_mm"), sem("lg_ready"), sem("lg_exp"), sem("sel_ready"), sem("rank_mm"),
            sem("tab_ready"))
        gu_took, m_ready, m_took, m_hi, prep_ready, ug_ready, e_silu, y_took_a, y_took_d = (
            sem("gu_took"), sem("m_ready"), sem("m_took"), sem("m_hi"), sem("prep_ready"), sem("ug_ready"),
            sem("e_silu"), sem("y_took_a"), sem("y_took_d"))
        stored, loop_step = sem("stored"), sem("loop_step")

        ident = K[:, C_ID:C_ID + P]
        ones = K[:, C_ONE:C_ONE + P]
        tri = [K[:, C_TRI_F:C_TRI_F + 512].rearrange("p (j t) -> p j t", j=2),
               K[:, C_TRI_B:C_TRI_B + 512].rearrange("p (j t) -> p j t", j=2)]

        def shift_of(layer, which):
            f = 24 * which
            return modT[:, layer, f:f + KD, :]

        def wide(ap, dims):
            return ap.to_broadcast([P] + dims)

        def d_bank(n):
            return banks[:, 1 + n % 3, :]

        def a_bank(n):
            return banks[:, 4 + n % 4, :]

        sidx = {}
        t = 0
        for name, n in (("mod0a", 2 * MG0), ("z", 6), ("uq", 2), ("ukv", 1), ("mods", 2 * MG - 2 * MG0), ("wo", 4),
                        ("gu", NF + 2 * MG), ("down", 2 * len(DOWN)), ("gin", 13), ("gout", 4)):
            sidx[name] = t
            t += n
        assert t == N_PRE

        def used(name, n):
            return sidx[name] + n

        def ahead_of(name, n):
            return used(name, n) + SPLIT_N - 1

        def halves(nk):
            return (0, (nk + 1) // 2), ((nk + 1) // 2, nk)

        def mod_turn(n):
            g = MG0 + n // MOD_STEP
            return g if n % MOD_STEP == 1 and g < MG else None

        ITEMS = [(hd, tl) for hd in range(HEADS + GQ) for tl in (2, 3, 0, 1)]
        NI = len(ITEMS)

        def keys(tl):
            return 4 if tl in LAT else 2

        def k_turn(hd):
            return hd if hd < HEADS else HEADS + (hd - HEADS) // (GQ // GKV)

        def kx(dr, i):
            if dr == 0:
                return (128 * i, 0, 32 * (i + 1)) if i < 4 else (512 + 256 * (i - 4), 0, 32 * (i + 1))
            return (128 * (i - 4), 32 * i - 128, 128) if i >= 4 else (512 + 256 * i, 32 * i, 256)

        def kx_tile(dr, i, j):
            at = kx(dr, i)[0]
            whole = i >= 4 if dr == 0 else i < 4
            return at + (128 * j if whole else 0)

        BLOCKS = [[(0, 0), (1, 0), (1, 1)], [(0, 0), (0, 1), (1, 1)]]
        ST_SUM, ST_VAR, ST_R, ST_T = 0, 1, 2, 3

        M_S, M_W, M_H, M_G = 0, 4, 5, 19
        M_ALL = 24
        GATHERS = (33, 35, 37, 39)
        LAST_H = 31
        LOOP_STEPS = 12

        def h_at(T, j, tt):
            return tt if T == 2 else j % 2

        def gu_free(T, j):
            return j + 1 if T == 2 else max(j, 1)

        pe_at = {}

        block = es.enter_context(nc.Block())

        @block.sync
        def _(sp):
            for i, (view, nk, n) in enumerate(units):
                slot = i % RAW_N
                for half, (a, b) in enumerate(halves(nk)):
                    if i >= RAW_N:
                        sp.wait_ge(lo_ready, 2 * (i - RAW_N) + half + 1)
                    dst = raw[:, slot, HALF * half:HALF * half + (b - a) * n].rearrange("p (k n) -> p k n", n=n)
                    sp.dma_start(dst, view[:, a:b, :]).then_inc(raw_in[slot][half], 16)
            with sp.Fori(0, E_N) as e:
                for u in range(PER_E):
                    i = N_PRE + u
                    slot = i % RAW_N
                    if u < 4 * EJ:
                        w = moe_w_gate if u % 4 < 2 else moe_w_up
                        j, kh = u // 4, u % 2
                        view = w[0, bass.ds(e, 1), 512 * kh:512 * kh + 512, 512 * j:512 * j + 512]
                        view = view.rearrange("o (k p) n -> p (o k) n", p=P)
                        dst = raw[:, slot, :].rearrange("p (k n) -> p k n", k=4)
                    else:
                        f = 2 * (u - 4 * EJ)
                        view = moe_w_down[0, bass.ds(e, 1), P * f:P * f + 256, :]
                        view = view.rearrange("o (k p) n -> p (o k) n", p=P)
                        dst = raw[:, slot, :].rearrange("p (k n) -> p k n", k=2)
                    for half, (a, b) in enumerate(halves(4 if u < 4 * EJ else 2)):
                        sp.wait_ge(lo_ready, e * (2 * PER_E) + (2 * (i - RAW_N) + half + 1))
                        sp.dma_start(dst[:, a:b, :], view[:, a:b, :]).then_inc(raw_in[slot][half], 16)
            sp.wait_ge(h_new, 10 + 2)
            for n, tl in enumerate(LAT):
                sp.dma_start(out[0, P * n:P * n + P, :], h[:, tl, :]).then_inc(stored, 16)
            sp.wait_ge(stored, 32)

        @block.tensor
        def _(pe):
            nd, na = [0], [0]
            unit = [0]

            def dbank():
                n = nd[0]
                if n >= 3:
                    pe.wait_ge(dve_took, n - 2)
                nd[0] += 1
                return d_bank(n)

            def abank():
                n = na[0]
                if n >= 4:
                    pe.wait_ge(act_took, n - 3)
                na[0] += 1
                return a_bank(n)

            def tiles_banks():
                return [dbank(), dbank(), abank(), abank()]

            def weights():
                i = unit[0]
                unit[0] += 1
                _, nk, n = units[i]
                pe.wait_ge(hi_ready, 2 * i + 2)
                pe.wait_ge(lo_ready, 2 * i + 2)
                return [w[:, i % SPLIT_N, 0:nk * n].rearrange("p (k n) -> p k n", k=nk) for w in (w_hi, w_lo)]

            def mm3(o, lh, ll, rh, rl, first, last):
                pe.matmul(o, lh, rh, start=first, stop=False)
                pe.matmul(o, lh, rl, start=False, stop=False)
                return pe.matmul(o, ll, rh, start=False, stop=last)

            def mod_rows(g):
                b = dbank()[0:4, :]
                mod_at[g] = nd[0]
                for kh in range(2):
                    for_k = weights()
                    for k in range(4):
                        for part in range(2):
                            mm = pe.matmul(b, cv[:, 4 * kh + k, :], for_k[part][:, k, :],
                                           start=(kh == k == part == 0), stop=(kh == 1 and k == 3 and part == 1))
                    mm.then_inc(weights_used, 1)

            def mod_cols(g):
                pe.wait_ge(dve_took, mod_at[g])
                for i in range(4):
                    c = 96 * (g // MG) + 2 * (4 * (g % MG) + i)
                    mm = pe.matmul(banks[:, 0, c:c + 2], mrow[g // MG][0:4, g % 2, P * i:P * i + P], K[0:4, C_PAIR:C_PAIR + 2],
                                   start=True, stop=True)
                mm.then_inc(mod_cols_done, 1)

            mod_at = {}

            def norm_transposes(n0, n):
                for i in range(n0, n0 + n):
                    pe.wait_ge(hn_ready, i + 1)
                    for half in range(2):
                        b = dbank()
                        for k in range(4):
                            mm = pe.transpose(b[:, P * k:P * k + P],
                                              hn[:, i % 2, P * (4 * half + k):P * (4 * half + k) + P], ident)
                    mm.then_inc(norm_tr, 1)

            def gate_broadcast(streams):
                for _ in streams:
                    g = gates[0]
                    gates[0] += 1
                    pe.wait_ge(diag_ready, g + 1)
                    for half in range(2):
                        b = abank()
                        for k in range(4):
                            kk = 4 * half + k
                            mm = pe.matmul(b[:, P * k:P * k + P], ones, hn[:, 0, P * kk:P * kk + P],
                                           start=True, stop=True)
                    mm.then_inc(gate_mm, 1)

            gates = [0]

            pe.wait_ge(const_in, 16 * 10)
            b = dbank()
            pe.transpose(b[:, 0:85], rowsA[0:85, :], ident[0:85, 0:85])
            pe.transpose(b[:, 85:181], rowsB[0:96, :], ident[0:96, 0:96])
            b = dbank()
            pe.matmul(b[:, 0:384], ones[0:1, :], rowC[0:1, :], start=True, stop=True).then_inc(setup_pe, 1)
            pe.wait_ge(cv_ready, 1)
            for g in range(MG0 + 1):
                if g < MG0:
                    mod_rows(g)
                if g:
                    mod_cols(g - 1)
            norm_transposes(0, TILES)

            for n in range(3):
                bs = tiles_banks()
                for kh in range(2):
                    wh, wl = weights()
                    if n == 0:
                        pe.wait_ge(u_ready, TILES)
                    for k in range(4):
                        kk = 4 * kh + k
                        for tl in range(TILES):
                            mm = mm3(bs[tl][:, 0:480], uT_hi[:, kk, P * tl:P * tl + P], uT_lo[:, kk, P * tl:P * tl + P],
                                     wh[:, k, :], wl[:, k, :], kk == 0, kk == KD - 1)
                    mm.then_inc(weights_used, 1)

            for tl in range(TILES):
                pe.wait_ge(lat_scaled, tl + 1)
                b = dbank()
                for k in range(3):
                    pe.transpose(b[:, P * k:P * k + P], z[:, tl, P * k:P * k + P], ident)
                b = dbank()
                for k in range(2):
                    mm = pe.transpose(b[:, P * k:P * k + P], z[:, tl, Z_KV + P * k:Z_KV + P * k + P], ident)
                mm.then_inc(lat_tr, 1)
            for n in range(2):
                wh, wl = weights()
                bs = tiles_banks()
                for tl in range(TILES):
                    pe.wait_ge(lat_split, tl + 1)
                    for k in range(3):
                        mm = mm3(bs[tl][:, 0:384], uT_hi[:, k, P * tl:P * tl + P], uT_lo[:, k, P * tl:P * tl + P],
                                 wh[:, k, :], wl[:, k, :], k == 0, k == 2)
                mm.then_inc(weights_used, 1)
            wh, wl = weights()
            for tl in range(TILES):
                for n in range(2):
                    b = dbank() if tl < 2 else abank()
                    for k in range(2):
                        mm = mm3(b, uT_hi[:, 3 + k, P * tl:P * tl + P], uT_lo[:, 3 + k, P * tl:P * tl + P],
                                 wh[:, k, 512 * n:512 * n + 512], wl[:, k, 512 * n:512 * n + 512], k == 0, k == 1)
                    if (tl, n) != (3, 1):
                        mm.then_inc(ukv_mm, 1)
            mm.then_inc(weights_used, 1)

            def head_transposes(hd):
                b = abank()
                for tl in range(TILES):
                    src, w = (qa[:, tl, DQ * hd:DQ * hd + DQ], DQ) if hd < HEADS else \
                        (z[:, tl, Z_Q + GD * (hd - HEADS):Z_Q + GD * (hd - HEADS) + GD], GD)
                    mm = pe.transpose(b[0:w, P * tl:P * tl + P], src, ident)
                mm.then_inc(q_tr, 1)
                kt = k_turn(hd)
                if hd and kt == k_turn(hd - 1):
                    return
                b = dbank()
                for tl in range(TILES):
                    src, w = (ka[:, tl, DQ * hd:DQ * hd + DQ], DQ) if hd < HEADS else \
                        (z[:, tl, Z_K + GD * (kt - HEADS):Z_K + GD * (kt - HEADS) + GD], GD)
                    mm = pe.transpose(b[0:w, P * tl:P * tl + P], src, ident)
                mm.then_inc(k_tr, 1)

            def scores(n):
                hd, tl = ITEMS[n]
                w = DQ if hd < HEADS else GD
                if n % 4 == 0:
                    pe.wait_ge(q_sb, hd + 1)
                    pe.wait_ge(k_sb, k_turn(hd) + 1)
                b = abank()
                pe.matmul(b[:, 0:P * keys(tl)], qT[0:w, hd % 2, P * tl:P * tl + P],
                          kT[0:w, k_turn(hd) % 2, 0:P * keys(tl)], start=True, stop=True).then_inc(s_done, 1)

            def p_transposes(n):
                hd, tl = ITEMS[n]
                pe.wait_ge(exp_done, n + 1)
                b = abank()
                for k in range(keys(tl)):
                    mm = pe.transpose(b[:, P * k:P * k + P], Pr[:, n % 3, P * k:P * k + P], ident)
                mm.then_inc(p_tr, 1)

            def pv(n):
                hd, tl = ITEMS[n]
                pe.wait_ge(pt_sb, n + 1)
                b = dbank()
                for k in range(keys(tl)):
                    if hd < HEADS:
                        v = va[:, k, DV * hd:DV * hd + DV]
                    else:
                        kv = k_turn(hd) - HEADS
                        v = z[:, k, Z_V + GD * kv:Z_V + GD * kv + GD]
                    mm = pe.matmul(b[:, 0:DV], PT[:, n % 3, P * k:P * k + P], v, start=(k == 0),
                                   stop=(k == keys(tl) - 1))
                mm.then_inc(pv_done, 1)

            pe.wait_ge(rope_done, 1)
            pe.wait_ge(act_took, na[0])
            head_transposes(0)
            for n in range(NI + 3):
                if n < NI:
                    if n % 4 == 1 and n // 4 + 1 < HEADS + GQ:
                        head_transposes(n // 4 + 1)
                    scores(n)
                if 2 <= n < NI + 2:
                    p_transposes(n - 2)
                if n >= 3:
                    pv(n - 3)
                if mod_turn(n):
                    mod_rows(mod_turn(n))
                if mod_turn(n - 1):
                    if mod_turn(n - 1) == MG0:
                        pe.wait_ge(bank0_took, 1)
                    mod_cols(mod_turn(n - 1))
            pe.wait_ge(dve_took, nd[0])
            for tl in range(TILES):
                for half in range(2):
                    b = dbank()
                    for k in range(4):
                        src = (z if half == 0 else qa)[:, tl, P * k:P * k + P]
                        mm = pe.transpose(b[:, P * k:P * k + P], src, ident)
                mm.then_inc(o_tr, 1)

            def project(lh, ll, tiles):
                turned = nd[0]
                for n in range(2):
                    bs = [dbank() for _ in tiles[:len(tiles) // 2]] + [abank() for _ in tiles[len(tiles) // 2:]]
                    for kh in range(2):
                        wh, wl = weights()
                        if n == 0 and kh == 0:
                            pe.wait_ge(dve_took, turned)
                        for k in range(4):
                            kk = 4 * kh + k
                            for i, tl in enumerate(tiles):
                                mm = mm3(bs[i], lh[:, kk, P * tl:P * tl + P], ll[:, kk, P * tl:P * tl + P],
                                         wh[:, k, :], wl[:, k, :], kk == 0, kk == KD - 1)
                        mm.then_inc(weights_used, 1)

            project(uT_hi, uT_lo, range(4))
            gate_broadcast((0, 1))
            norm_transposes(4, TILES)

            pe.wait_ge(u_ready, 8)
            for j in range(NF // 2):
                for g in range(2):
                    wh, wl = weights()
                    for fc in range(2):
                        b = abank() if g == 0 else dbank()
                        for k in range(KD):
                            mm = mm3(b, wh[:, k, P * fc:P * fc + P], wl[:, k, P * fc:P * fc + P],
                                     uT_hi[:, k, :], uT_lo[:, k, :], k == 0, k == KD - 1)
                    mm.then_inc(weights_used, 1)
                if j == 0:
                    pe.wait_ge(bank0_took, 2)
                else:
                    mod_cols(MG + j - 1)
                mod_rows(MG + j)
            mod_cols(2 * MG - 2)
            mod_rows(2 * MG - 1)
            mod_cols(2 * MG - 1)
            n_hs = 0
            for n in range(2):
                bs = tiles_banks()
                for f0, m in DOWN:
                    wh, wl = weights()
                    for f in range(f0, f0 + m):
                        pe.wait_ge(hs_ready, n_hs + 1)
                        for tl in range(TILES):
                            cols = slice(P * tl, P * tl + P)
                            mm = mm3(bs[tl], hs[:, n_hs % 2, 0, cols], hs[:, n_hs % 2, 1, cols],
                                     wh[:, f - f0, :], wl[:, f - f0, :], f == 0, f == NF - 1)
                        n_hs += 1
                        mm.then_inc(weights_used if f == f0 + m - 1 else hs_used, 1)
            gate_broadcast((0, 1))
            norm_transposes(8, TILES)

            wh, wl = weights()
            b = dbank()
            pe.wait_ge(u_ready, 12)
            for tl in range(TILES):
                cols = slice(P * tl, P * tl + P)
                for k in range(KD):
                    mm = mm3(b[:, 32 * tl:32 * tl + 32], uT_hi[:, k, cols], uT_lo[:, k, cols], wh[:, k, :], wl[:, k, :],
                             k == 0, k == KD - 1)
            mm.then_inc(weights_used, 1)
            for n in range(6):
                if n < 3:
                    bs = dict(zip(range(4), tiles_banks()))
                elif n == 3:
                    bs = {2: dbank(), 3: abank()}
                else:
                    bs = {2: abank(), 3: abank()}
                for kh in range(2):
                    wh, wl = weights()
                    for k in range(4):
                        kk = 4 * kh + k
                        for tl, b in bs.items():
                            cols = slice(P * tl, P * tl + P)
                            mm = mm3(b, uT_hi[:, kk, cols], uT_lo[:, kk, cols], wh[:, k, :], wl[:, k, :],
                                     kk == 0, kk == KD - 1)
                    mm.then_inc(weights_used, 1)
            proj_d, proj_a = nd[0], na[0]
            pe_at["gin"] = proj_a
            pe.wait_ge(r_sb, 1)
            for dr in range(2):
                b = dbank()
                for tl in range(TILES):
                    mm = pe.transpose(b[0:GRANK, P * tl:P * tl + P], rtok[:, tl, GRANK * dr:GRANK * dr + GRANK], ident)
                mm.then_inc(r_tr, 1)
            pe.wait_ge(rt_sb, 2)
            pe.wait_ge(late_in, 16 * 3)
            for i in range(8):
                dr, tl = i // 4, i % 4
                b = dbank()
                pe.matmul(b, rT[0:GRANK + 1, dr, P * tl:P * tl + P], wg2[0:GRANK + 1, dr, :],
                          start=True, stop=True).then_inc(z2_mm, 1)
            pe.wait_ge(act_took, proj_a)
            pe.wait_ge(dve_took, proj_d)
            for i in range(4):
                src = g_q if i < 2 else g_k
                b = dbank()
                for hh in range(2):
                    hd = 2 * (i % 2) + hh
                    for j in range(2):
                        tl = j if i < 2 else 2 + j
                        mm = pe.transpose(b[:, 256 * hh + P * j:256 * hh + P * j + P],
                                          src[:, tl, P * hd:P * hd + P], ident)
                mm.then_inc(gt_mm, 1)
            for dr in range(2):
                pe.wait_ge(a_ready, 4 * dr + 2)
                for s2 in range(2):
                    b = dbank()
                    for j in range(2):
                        mm = pe.matmul(b, tri[1 - dr][:, j, P * s2:P * s2 + P], g_a[:, j, dr, :],
                                       start=(j == 0), stop=(j == 1))
                mm.then_inc(tail_mm, 1)
            for dr in range(2):
                pe.wait_ge(ks_ready, dr + 1)
                for hp in range(2):
                    b = abank()
                    for hh in range(2):
                        hd = 2 * hp + hh
                        for j in range(2):
                            mm = pe.matmul(b[:, 256 * hh:256 * hh + 256], g_a[:, j, dr, P * hd:P * hd + P],
                                           g_v[:, j, 256 * hd:256 * hd + 256], start=(j == 0), stop=(j == 1))
                    mm.then_inc(s0_mm, 1)
            states_a = na[0]

            def cumulate(it):
                hd, dr = it // 2, it % 2
                b = dbank()
                for j in range(2):
                    mm = pe.matmul(b[:, 0:256], g_a[:, 2 + j, dr, P * hd:P * hd + P], tri[dr][:, j, :],
                                   start=(j == 0), stop=(j == 1))
                mm.then_inc(cum_mm, 1)

            def gla_scores(it):
                hd, dr = it // 2, it % 2
                pe.wait_ge(dec_ready, it + 1)
                at_bank[it] = nd[0] + 1
                b = dbank()
                for n, (tt, j) in enumerate(BLOCKS[dr]):
                    for i in range(4 * tt, 4 * tt + 4):
                        at = kx_tile(dr, i, j)
                        mm = pe.matmul(b[:, P * n + 32 * (i % 4):P * n + 32 * (i % 4) + 32], g_KX[:, dr, at:at + P],
                                       g_qd[:, dr, 32 * i:32 * i + 32], start=True, stop=True)
                mm.then_inc(at_mm, 1)

            def gla_out(hd):
                pe.wait_ge(dve_took, at_bank[2 * hd + 1])
                if hd == 0:
                    pe.wait_ge(act_took, states_a)
                b = abank()
                for tt in range(2):
                    o = b[:, 256 * tt:256 * tt + 256]
                    parts = []
                    for dr in range(2):
                        for n, (ta, j) in enumerate(BLOCKS[dr]):
                            if ta == tt:
                                parts.append((g_AT[:, hd % 2, dr, P * n:P * n + P],
                                              g_v[:, 2 + j, 256 * hd:256 * hd + 256]))
                        parts.append((g_qf[:, hd % 2, dr, P * tt:P * tt + P], g_S[:, dr, hd, :]))
                    for n, (l, r) in enumerate(parts):
                        mm = pe.matmul(o, l, r, start=(n == 0), stop=(n == len(parts) - 1))
                mm.then_inc(go_mm, 1)

            at_bank = {}
            pe.wait_ge(a_ready, 8)
            pe.wait_ge(kx_zero, 1)
            cumulate(0)
            cumulate(1)
            for it in range(2 * GH):
                gla_scores(it)
                if it + 2 < 2 * GH:
                    cumulate(it + 2)
                if it % 2 == 1:
                    gla_out(it // 2)
            for tt in range(2):
                pe.wait_ge(go_ready, 1)
                for half in range(2):
                    b = dbank()
                    for k in range(4):
                        mm = pe.transpose(b[:, P * k:P * k + P], g_o[:, tt, P * (4 * half + k):P * (4 * half + k) + P],
                                          ident)
                mm.then_inc(got_mm, 1)
            project(ug_hi, ug_lo, range(2))
            gate_broadcast((1,))
            norm_transposes(12, 2)

            for n in range(2):
                pe.wait_ge(uf_ready, n + 1)
                if n == 0:
                    pe.wait_ge(late_in, 16 * 6)
                    pe.wait_ge(bank0_took, 3)
                o = banks[:, 0, E_N * n:E_N * n + E_N]
                for k in range(KD):
                    pe.matmul(o, uf[:, P * k:P * k + P], wr[:, k, :], start=(k == 0), stop=False)
                pe.matmul(o, ones[0:1, :], brow[0:1, :], start=False, stop=True).then_inc(logit_mm, 1)
            pe.wait_ge(sel_ready, 1)
            for n in range(2):
                for j in range(2):
                    pe.matmul(banks[:, 0, E_N * n:E_N * n + E_N], tri[0][:, j, P * n:P * n + P], sel[:, j, :],
                              start=(j == 0), stop=(j == 1))
            for j in range(2):
                mm = pe.matmul(banks[:, 0, 16:24], ones, sel[:, j, :], start=(j == 0), stop=(j == 1))
            mm.then_inc(rank_mm, 1)

            pe.wait_ge(dve_took, nd[0])
            pe.wait_ge(act_took, na[0])
            pe.wait_ge(tab_ready, 1)

            def m_use(at, n):
                pe.wait_ge(m_took, at + (n - 1))
                return banks[:, 4 + n % 2, :]

            def gather(e1, at, g):
                if g == 0:
                    pe.wait_ge(prep_ready, e1 + 1)
                b = m_use(at, M_G + g)
                for i in range(2):
                    k = 2 * g + i
                    for j in range(2):
                        mm = pe.matmul(b[:, 256 * i:256 * i + 256], hn[:, j, P * k:P * k + P], Pm[:, j, :],
                                       start=(j == 0), stop=(j == 1))
                mm.then_inc(m_ready, 1)

            def scatter(T):
                for i in range(4):
                    tk, n = i // 2, i % 2
                    for tt in range(T):
                        mm = pe.matmul(banks[:, 4 + i, :], Wc[:, tt, P * tk:P * tk + P],
                                       y_e[:, tt, 512 * n:512 * n + 512], start=(tt == 0), stop=(tt == T - 1))
                    mm.then_inc(m_ready, 1)

            pe.sem_inc(m_ready, M_G)
            for g in range(4):
                gather(0, 0, g)
            pe.wait_ge(m_ready, M_G + 4)
            pe.sem_inc(m_ready, M_ALL - M_G - 4)
            with pe.Fori(0, E_N) as e:
                ms = e * M_ALL + M_ALL

                def e_half(u, half):
                    s = N_PRE + u
                    pe.wait_ge(hi_ready, e * (2 * PER_E) + (2 * s + half + 1))
                    pe.wait_ge(lo_ready, e * (2 * PER_E) + (2 * s + half + 1))

                def e_weights(u):
                    s = N_PRE + u
                    k = 4 if u < 4 * EJ else 2
                    return [w[:, s % SPLIT_N, :].rearrange("p (k n) -> p k n", k=k) for w in (w_hi, w_lo)]

                def expert(T):
                    def h_transposes(j):
                        pe.wait_ge(gu_took, e * EJ + (j + 2))
                        for tt in range(T):
                            b = m_use(ms, M_H + T * j + tt)
                            for i in range(4):
                                mm = pe.transpose(b[:, P * i:P * i + P], e_h[:, h_at(T, j, tt), P * i:P * i + P],
                                                  ident)
                            mm.then_inc(m_ready, 1)

                    for j in range(EJ):
                        pe.wait_ge(gu_took, e * EJ + gu_free(T, j))
                        for g in range(2):
                            for kh in range(2):
                                u = 4 * j + 2 * g + kh
                                wh, wl = e_weights(u)
                                for k in range(4):
                                    if k % 2 == 0:
                                        e_half(u, k // 2)
                                    kk = 4 * kh + k
                                    for tt in range(T):
                                        mm = mm3(banks[:, 2 * h_at(T, j, tt) + g, :], ug_hi[:, kk, P * tt:P * tt + P],
                                                 ug_lo[:, kk, P * tt:P * tt + P], wh[:, k, :], wl[:, k, :],
                                                 kk == 0, kk == KD - 1)
                                mm.then_inc(weights_used, 1)
                        if j:
                            h_transposes(j - 1)
                        else:
                            b = m_use(ms, M_W)
                            for s2 in range(2):
                                for jj in range(2):
                                    mm = pe.transpose(b[:, 256 * s2 + P * jj:256 * s2 + P * jj + P],
                                                      Pc[:, jj, P * s2:P * s2 + P], ident)
                            mm.then_inc(m_ready, 1)
                    if T == 2:
                        pe.wait_ge(gu_took, e * EJ + (EJ + 1))
                    for u in range(4 * EJ, PER_E):
                        if u == LAST_H:
                            h_transposes(EJ - 1)
                            if T == 1:
                                pe.wait_ge(m_ready, ms + (M_H + EJ))
                                pe.sem_inc(m_ready, EJ)
                        if u in GATHERS:
                            gather(e + 1, ms, GATHERS.index(u))
                        wh, wl = e_weights(u)
                        for i in range(2):
                            e_half(u, i)
                            f = 2 * (u - 4 * EJ) + i
                            if f % 4 == 0:
                                pe.wait_ge(m_took, ms + (M_H + T * (f // 4 + 1)))
                            for tt in range(T):
                                for n in range(2):
                                    bk = 6 + n if tt == 0 else n
                                    mm = mm3(banks[:, bk, :], eT_hi[:, f, P * tt:P * tt + P],
                                             eT_lo[:, f, P * tt:P * tt + P],
                                             wh[:, i, 512 * n:512 * n + 512], wl[:, i, 512 * n:512 * n + 512],
                                             f == 0, f == EF - 1)
                        mm.then_inc(weights_used, 1)

                pe.wait_ge(y_took_a, e + 1)
                pe.wait_ge(y_took_d, e + 1)
                pe.wait_ge(m_took, ms)
                before = pe.value_load(cnt[0:1, bass.ds(e, 1)], min_val=0, max_val=2 * P)
                with pe.If(before > P):
                    scatter(2)
                with pe.Else():
                    scatter(1)
                pe.wait_ge(ug_ready, e + 1)
                chosen = pe.value_load(cnt[0:1, bass.ds(e + 1, 1)], min_val=0, max_val=2 * P)
                with pe.If(chosen > P):
                    expert(2)
                with pe.Else():
                    expert(1)
                pe.wait_ge(m_ready, ms + (M_ALL - 1))
                pe.sem_inc(m_ready, 1)
            pe.wait_ge(y_took_a, E_N + 1)
            pe.wait_ge(y_took_d, E_N + 1)
            scatter(2)
            pe.wait_ge(m_took, (E_N + 1) * M_ALL + 4)
            gate_broadcast((1,))

        dve_at = {}

        @block.vector
        def _(dve):
            nd, steps, nsplit, nr = [0], [0], [0], [0]

            def chain(ins):
                ins.then_inc(dve_step, 1)
                steps[0] += 1
                dve.wait_ge(dve_step, steps[0])

            def dsrc():
                nd[0] += 1
                return d_bank(nd[0] - 1)

            def took(ins, then=False):
                ins.then_inc(dve_took, 1)
                if then:
                    dve.wait_ge(dve_took, nd[0])

            def split_to(n):
                while nsplit[0] < min(n, N_PRE):
                    s = nsplit[0]
                    nsplit[0] += 1
                    if s >= SPLIT_N:
                        dve.wait_ge(weights_used, s - SPLIT_N + 1)
                    for half, (a, b) in enumerate(halves(units[s][1])):
                        c = slice(units[s][2] * a, units[s][2] * b)
                        r = slice(HALF * half, HALF * half + units[s][2] * (b - a))
                        dve.wait_ge(hi_ready, 2 * s + half + 1)
                        dve.wait_ge(raw_in[s % RAW_N][half], 16 * (s // RAW_N + 1))
                        dve.tensor_tensor(w_lo[:, s % SPLIT_N, c], raw[:, s % RAW_N, r],
                                          w_hi[:, s % SPLIT_N, c].bitcast(F32), ALU.subtract).then_inc(lo_ready, 1)

            def after(name, n):
                split_to(ahead_of(name, n))
                dve.wait_ge(weights_used, used(name, n))

            def rstd(groups, n):
                nr[0] += 1
                dve.wait_ge(ss_ready, nr[0])
                for cols, width in groups:
                    ins = dve.tensor_scalar(cols(ST_VAR), cols(ST_SUM), 1.0 / width, EPS, ALU.mult, ALU.add)
                ins.then_inc(var_ready, 1)
                dve.wait_ge(guess_ready, nr[0])
                v, y, t = st[:, ST_VAR, 0:n], st[:, ST_R, 0:n], st[:, ST_T, 0:n]
                chain(dve.tensor_tensor(t, v, y, ALU.mult))
                chain(dve.tensor_tensor(t, t, y, ALU.mult))
                chain(dve.tensor_scalar(t, t, -0.5, 1.5, ALU.mult, ALU.add))
                dve.tensor_tensor(y, y, t, ALU.mult).then_inc(rstd_ready, 1)
                dve.wait_ge(rstd_ready, nr[0])

            def mod_rows_out(g):
                if g < MG0:
                    after("mod0a", 2 * g + 2)
                else:
                    after(*(("mods", 2 * (g - MG0) + 2) if g < MG else ("gu", 4 * (g - MG) + (4 if g < 2 * MG - 1 else 2))))
                if g >= 2:
                    dve.wait_ge(mod_cols_done, g - 1)
                took(dve.tensor_copy(mrow[g // MG][0:4, g % 2, :], dsrc()[0:4, :]))

            def mod_columns(layer, f0, f1, groups):
                dve.wait_ge(mod_cols_done, groups)
                m = modT[:, layer, f0:f1, :]
                b = vecs[:, 85 + 48 * layer + f0:85 + 48 * layer + f1].unsqueeze(2)
                dve.tensor_tensor(m, banks[:, 0, 96 * layer + 2 * f0:96 * layer + 2 * f1].rearrange("p (f s) -> p f s", s=2),
                                  wide(b, [f1 - f0, 2]), ALU.add).then_inc(bank0_took, 1)
                mods_n[0] += 1
                dve.wait_ge(bank0_took, mods_n[0])

            mods_n = [0]

            def gain(layer, i):
                c0 = 16 + (4 * layer + i) * KD
                return wide(vecs[:, c0:c0 + KD].unsqueeze(2), [KD, 2])

            def scale_site(layer, which):
                f = 24 * which + 8
                a = Am[:, 2 * layer + which]
                chain(dve.tensor_scalar(a, modT[:, layer, f:f + KD, :], 1.0, None, ALU.add))
                chain(dve.tensor_tensor(a, a, gain(layer, 2 * which), ALU.mult))

            def gate_site(layer, which, inc):
                f = 24 * which + 16
                g = dve.tensor_tensor(Gm[:, 2 * layer + which], modT[:, layer, f:f + KD, :],
                                      gain(layer, 2 * which + 1), ALU.mult)
                if inc:
                    g.then_inc(mods_ready, 1)

            def modulate(layer, which, n0, tiles, split=True):
                u3 = uf[:, :].rearrange("p (k t) -> p k t", k=KD)
                for i, tl in enumerate(tiles):
                    s = 1 if tl in LAT else 0
                    dve.wait_ge(norm_tr, n0 + i + 1)
                    if not split and i:
                        dve.wait_ge(logit_mm, i)
                    for half in range(2):
                        b = dsrc().rearrange("p (k t) -> p k t", k=4)
                        a = Am[:, 2 * layer + which, 4 * half:4 * half + 4, s:s + 1]
                        took(dve.tensor_tensor(u3[:, 4 * half:4 * half + 4, :], b, wide(a, [4, P]), ALU.mult),
                             then=(half == 1))
                    sh = wide(shift_of(layer, which)[:, :, s:s + 1], [KD, P])
                    ins = dve.tensor_tensor(u3, u3, sh, ALU.add)
                    if not split:
                        ins.then_inc(uf_ready, 1)
                        continue
                    chain(ins)
                    cols = slice(P * tl, P * tl + P)
                    chain(dve.tensor_copy(uT_hi[:, :, cols], u3))
                    dve.tensor_tensor(uT_lo[:, :, cols], u3, uT_hi[:, :, cols].bitcast(F32),
                                      ALU.subtract).then_inc(u_ready, 1)
                    dve.wait_ge(u_ready, u_n[0] + 1)
                    u_n[0] += 1

            u_n = [0]

            def residual(y, tiles, site, gr):
                rstd([(lambda k: st[:, k, 0:len(tiles)], D)], len(tiles))
                dve.wait_ge(gate_rows, gr)
                for i, tl in enumerate(tiles):
                    s = 1 if tl in LAT else 0
                    chain(dve.scalar_tensor_tensor(y[:, i, :], y[:, i, :], st[:, ST_R, i:i + 1], Gb[:, s, :],
                                                   ALU.mult, ALU.mult))
                    dve.tensor_tensor(h[:, tl, :], h[:, tl, :], y[:, i, :], ALU.add).then_inc(h_new, 1)

            def split_banks(hi, lo):
                b = dsrc().rearrange("p (k t) -> p k t", k=4)
                chain(dve.tensor_copy(hi, b))
                took(dve.tensor_tensor(lo, b, hi.bitcast(F32), ALU.subtract))

            dve.wait_ge(setup_pe, 1)
            took(dve.tensor_copy(vecs[:, :], dsrc()[:, 0:181]))
            took(dve.tensor_copy(bc[:, :], dsrc()[:, 0:384]))
            dve.wait_ge(dve_took, 2)
            dve.wait_ge(c_silu, 1)
            dve.tensor_tensor(cv[:, :, 2:4], vecs[:, 0:16].rearrange("p (s k) -> p k s", k=KD),
                              cv[:, :, 0:2].bitcast(F32), ALU.subtract).then_inc(cv_ready, 1)
            split_to(2)
            rstd([(lambda k: st[:, k, 0:TILES], D)], TILES)
            for g in range(MG0):
                mod_rows_out(g)
            mod_columns(0, 0, 16, MG0)
            scale_site(0, 0)
            modulate(0, 0, 0, range(TILES))

            for n in range(3):
                after("z", 2 * n + 2)
                for tl in range(2):
                    took(dve.tensor_copy(z[:, tl, 480 * n:480 * n + 480], dsrc()[:, 0:480]))
            dve.wait_ge(dve_took, nd[0])
            dve.wait_ge(act_took, 6)
            for tl in range(TILES):
                q10 = z[:, tl, Z_Q:Z_V]
                chain(dve.tensor_tensor(uf[:, 0:640], q10, q10, ALU.mult))
                ins = dve.reduce_sum(st[:, ST_SUM, 12 * tl + 2:12 * tl + 12],
                                     uf[:, 0:640].rearrange("p (h d) -> p h d", d=GD), AX.X)
                if tl < TILES - 1:
                    chain(ins)
            ins.then_inc(z_ready, 1)

            def sums(a, b):
                return lambda k: st[:, k, :].rearrange("p (t c) -> p t c", c=12)[:, :, a:b]

            rstd([(sums(0, 1), Q_RANK), (sums(1, 2), KV_RANK), (sums(2, 12), GD)], 48)
            r12 = st[:, ST_R, :].rearrange("p (t c) -> p t c", c=12)
            heads_n = {}

            def norm_heads(tl):
                q10 = z[:, tl, Z_Q:Z_V].rearrange("p (h d) -> p h d", d=GD)
                chain(dve.tensor_tensor(q10, q10, wide(r12[:, tl, 2:12].unsqueeze(2), [10, GD]), ALU.mult))
                dve.tensor_tensor(q10[:, 0:GQ], q10[:, 0:GQ], wide(bc[:, 0:GD].unsqueeze(1), [GQ, GD]), ALU.mult)
                chain(dve.tensor_tensor(q10[:, GQ:10], q10[:, GQ:10], wide(bc[:, GD:2 * GD].unsqueeze(1), [GKV, GD]),
                                        ALU.mult))

            def lat_parts(tl):
                dve.wait_ge(lat_tr, tl + 1)
                cols = slice(P * tl, P * tl + P)
                u5 = uf[:, 0:640].rearrange("p (k t) -> p k t", k=5)
                for a, b in ((0, 3), (3, 5)):
                    bank = dsrc()[:, 0:P * (b - a)].rearrange("p (k t) -> p k t", k=b - a)
                    g = wide(vecs[:, 80 + a:80 + b].unsqueeze(2), [b - a, P])
                    took(dve.tensor_tensor(u5[:, a:b, :], bank, g, ALU.mult), then=(a == 3))
                chain(dve.tensor_copy(uT_hi[:, 0:5, cols], u5))
                dve.tensor_tensor(uT_lo[:, 0:5, cols], u5, uT_hi[:, 0:5, cols].bitcast(F32),
                                  ALU.subtract).then_inc(lat_split, 1)
                dve.wait_ge(lat_split, tl + 1)

            def rotate(v, heads, tl, n):
                c0 = 0 if n == 16 else 64
                tb = rope[:, tl - 2, c0:c0 + 4 * n].rearrange("p (f a n) -> p f a n", f=2, a=2)
                cos, sin = (wide(tb[:, i].unsqueeze(1), [heads, 2, n]) for i in range(2))
                x1, x2 = v[:, :, :, 0, :], v[:, :, :, 1, :]
                m = heads * 2 * n
                t1, t2, t3 = (uf[:, i * m:i * m + m].rearrange("p (h a n) -> p h a n", h=heads, a=2) for i in range(3))
                dve.tensor_tensor(t1, x1, cos, ALU.mult)
                chain(dve.tensor_tensor(t2, x2, sin, ALU.mult))
                dve.tensor_tensor(t3, x2, cos, ALU.mult)
                chain(dve.tensor_tensor(t1, t1, t2, ALU.subtract))
                chain(dve.tensor_tensor(t2, x1, sin, ALU.mult))
                chain(dve.tensor_tensor(x2, t3, t2, ALU.add))
                chain(dve.tensor_copy(x1, t1))

            def five(v, heads, n):
                return v.rearrange("p (h a x n) -> p h a x n", h=heads, a=2, x=2)

            split_to(used("uq", 0) + 2)
            for tl in range(TILES):
                lat_parts(tl)
            for tl in range(TILES):
                norm_heads(tl)
                if tl in LAT:
                    rotate(five(z[:, tl, Z_Q:Z_V], 10, 16), 10, tl, 16)
                    rotate(five(z[:, tl, Z_ROPE:Z_Q], 1, 8), 1, tl, 8)
            for n in range(2):
                after("uq", n + 1)
                for tl in range(2):
                    took(dve.tensor_copy(qa[:, tl, 384 * n:384 * n + 384], dsrc()[:, 0:384]))
            split_to(used("mods", 0) + 2)

            def kv_out(tl, n, b, copy):
                b = b.rearrange("p (h c) -> p h c", c=P)
                k8 = ka[:, tl, :].rearrange("p (h c) -> p h c", c=DQ)[:, 4 * n:4 * n + 4, 0:NOPE]
                v8 = va[:, tl, 256 * n:256 * n + 256].rearrange("p (h c) -> p h c", c=DV)
                copy(k8, b[:, :, 0:NOPE])
                return copy(v8, b[:, :, NOPE:P])

            for tl in range(2):
                for n in range(2):
                    dve.wait_ge(ukv_mm, 2 * tl + n + 1)
                    took(kv_out(tl, n, dsrc(), dve.tensor_copy))
            for tl in range(TILES):
                k8 = ka[:, tl, :].rearrange("p (h c) -> p h c", c=DQ)[:, :, NOPE:DQ]
                dve.tensor_copy(k8, wide(z[:, tl, Z_ROPE:Z_Q].unsqueeze(1), [HEADS, ROPE_M]))
            dve.wait_ge(act_took, 10)
            for tl in LAT:
                q96 = qa[:, tl, :].rearrange("p (h c) -> p h c", c=DQ)[:, :, NOPE:DQ]
                rotate(q96.rearrange("p h (a x n) -> p h a x n", a=2, x=2), HEADS, tl, 8)
            dve.wait_ge(dve_took, nd[0])
            dve.sem_inc(rope_done, 1)

            score_bank = []
            a = 15
            for n in range(NI + 3):
                a += n < NI and n % 4 == 1 and n // 4 + 1 < HEADS + GQ
                score_bank.append(a)
                a += (n < NI) + (2 <= n < NI + 2)

            def k_out(hd):
                kt = k_turn(hd)
                if hd and kt == k_turn(hd - 1):
                    return
                w = DQ if hd < HEADS else GD
                dve.wait_ge(k_tr, kt + 1)
                k_n[0] += 1
                took(dve.tensor_copy(kT[0:w, kt % 2, :], dsrc()[0:w, :]), then=True)
                dve.sem_inc(k_sb, 1)

            k_n = [0]
            mxs, nbs, sms, ris = (sm[:, 8 * i:8 * i + 8] for i in range(4))
            k_out(0)
            for n in range(NI + 3):
                if n < NI and n % 4 == 1 and n // 4 + 1 < HEADS + GQ:
                    hd1 = n // 4 + 1
                    dve.wait_ge(s_done, n)
                    k_out(hd1)
                if n < NI:
                    hd, tl = ITEMS[n]
                    scale = float(DQ if hd < HEADS else GD) ** -0.5
                    c = n % 8
                    dve.wait_ge(s_done, n + 1)
                    chain(dve.reduce_max(mxs[:, c:c + 1], a_bank(score_bank[n])[:, 0:P * keys(tl)], AX.X))
                    dve.tensor_scalar(nbs[:, c:c + 1], mxs[:, c:c + 1], -scale, None, ALU.mult).then_inc(nb_ready, 1)
                if n >= 3:
                    hd, tl = ITEMS[n - 3]
                    c = (n - 3) % 8
                    dve.wait_ge(exp_done, n - 2)
                    chain(dve.reciprocal(ris[:, c:c + 1], sms[:, c:c + 1]))
                    dve.wait_ge(pv_done, n - 2)
                    o = z[:, tl, DV * hd:DV * hd + DV] if hd < HEADS else \
                        qa[:, tl, DV * (hd - HEADS):DV * (hd - HEADS) + DV]
                    took(dve.tensor_scalar(o, dsrc()[:, 0:DV], ris[:, c:c + 1], None, ALU.mult))
                if mod_turn(n):
                    mod_rows_out(mod_turn(n))
            attn_d = nd[0]
            dve_at["attention"] = attn_d
            mod_columns(0, 16, 48, MG)
            scale_site(0, 1)
            gate_site(0, 0, False)
            gate_site(0, 1, True)
            split_to(used("wo", 0) + 2)
            for tl in range(TILES):
                dve.wait_ge(o_tr, tl + 1)
                cols = slice(P * tl, P * tl + P)
                for half in range(2):
                    split_banks(uT_hi[:, 4 * half:4 * half + 4, cols], uT_lo[:, 4 * half:4 * half + 4, cols])

            def project_out(name, y, tiles):
                for n in range(2):
                    after(name, 2 * n + 2)
                    for tl in tiles:
                        took(dve.tensor_copy(y[:, tl, 512 * n:512 * n + 512], dsrc()), then=(n == 1))
                dve_at[name] = nd[0]

            project_out("wo", y_attn, (0, 1))
            residual(y_attn, range(TILES), 0, 2)
            rstd([(lambda k: st[:, k, 0:TILES], D)], TILES)
            split_to(used("gu", 0) + 2)
            modulate(0, 1, 4, range(TILES))

            dve_at["ffn"] = nd[0]
            for j in range(NF // 2):
                after("gu", 4 * j + 2)
                for fc in range(2):
                    f = 2 * j + fc
                    dve.wait_ge(silu_ready, f + 1)
                    took(dve.tensor_tensor(hT[:, f, :], sil[:, f % 2, :], dsrc(), ALU.mult))
                mod_rows_out(MG + j)
                if j == NF // 2 - 1:
                    mod_rows_out(MG + j + 1)
            dve.wait_ge(dve_took, nd[0])
            n_hs, hs_n = 0, 0
            freed = []
            for n in range(2):
                for d, (f0, m) in enumerate(DOWN):
                    split_to(ahead_of("down", n * len(DOWN) + d))
                    for f in range(f0, f0 + m):
                        if n_hs >= 2:
                            dve.wait_ge(*freed[n_hs - 2])
                        chain(dve.tensor_copy(hs[:, n_hs % 2, 0, :], hT[:, f, :]))
                        dve.tensor_tensor(hs[:, n_hs % 2, 1, :], hT[:, f, :], hs[:, n_hs % 2, 0, :].bitcast(F32),
                                          ALU.subtract).then_inc(hs_ready, 1)
                        n_hs += 1
                        if f == f0 + m - 1:
                            freed.append((weights_used, used("down", n * len(DOWN) + d + 1)))
                        else:
                            hs_n += 1
                            freed.append((hs_used, hs_n))
                after("down", (n + 1) * len(DOWN))
                for tl in range(2):
                    took(dve.tensor_copy(y_ffn[:, tl, 512 * n:512 * n + 512], dsrc()), then=(n == 1))
            dve_at["down"] = nd[0]
            residual(y_ffn, range(TILES), 1, 4)
            mod_columns(1, 0, 48, 2 * MG)
            scale_site(1, 0)
            scale_site(1, 1)
            gate_site(1, 0, False)
            gate_site(1, 1, True)
            rstd([(lambda k: st[:, k, 0:TILES], D)], TILES)
            split_to(used("gin", 0) + 2)
            modulate(1, 0, 8, range(TILES))

            after("gin", 1)
            took(dve.tensor_copy(rtok[:, :, :], dsrc()[:, 0:128].rearrange("p (t r) -> p t r", r=32)), then=True)
            dve.sem_inc(r_sb, 1)
            for n, (dst, c0) in enumerate(((g_k, 0), (g_v, 0), (g_v, 512))):
                after("gin", 2 * n + 3)
                for tl in range(2):
                    took(dve.tensor_copy(dst[:, tl, c0:c0 + 512], dsrc()))
            after("gin", 9)
            took(dve.tensor_copy(g_q[:, 0, :], dsrc()))
            after("gin", 13)
            dve.wait_ge(act_took, pe_at["gin"])
            g8 = g_g[:, :, :].rearrange("p j (h v) -> p (j h) v", v=GDV)
            dve.tensor_tensor(g8, g8, wide(bc[:, 128:384].unsqueeze(1), [2 * GH, GDV]), ALU.mult)
            dve.wait_ge(rt_one, 1)
            for dr in range(2):
                dve.wait_ge(r_tr, dr + 1)
                took(dve.tensor_copy(rT[0:GRANK, dr, :], dsrc()[0:GRANK, :]), then=True)
                dve.sem_inc(rt_sb, 1)

            def log_decay(i):
                dr, tl = i // 4, i % 4
                dve.wait_ge(e_ln, i + 1)
                dve.tensor_tensor(g_a[:, tl, dr, :], g_a[:, tl, dr, :], ebuf[:, i % 2, :],
                                  ALU.subtract).then_inc(a_ready, 1)

            for i in range(8):
                dr, tl = i // 4, i % 4
                dve.wait_ge(z2_mm, i + 1)
                b = dsrc()
                a = g_a[:, tl, dr, :]
                chain(dve.tensor_scalar(a, b, 0.0, None, ALU.min))
                took(dve.scalar_tensor_tensor(ebuf[:, i % 2, :], a, 2.0, b, ALU.mult, ALU.subtract))
                dve_at["gate", i] = nd[0]
                if i:
                    log_decay(i - 1)
            log_decay(7)
            dve.wait_ge(a_ready, 8)
            for i in range(4):
                dve.wait_ge(gt_mm, i + 1)
                dst = (g_qT if i < 2 else g_kT)[:, 2 * (i % 2):2 * (i % 2) + 2, :]
                b = dsrc().rearrange("p (h t) -> p h t", h=2)
                took(dve.tensor_scalar(dst, b, float(GDK) ** -0.5 if i < 2 else 1.0, None, ALU.mult))
            for dr in range(2):
                dve.wait_ge(tail_mm, dr + 1)
                for s2 in range(2):
                    took(dve.tensor_tensor(g_a[:, s2, dr, :], dsrc(), g_a[:, s2, dr, :], ALU.subtract))
                dve_at["tail", dr] = nd[0]
            for dr in range(2):
                dve.wait_ge(tail_exp, dr + 1)
                dve.tensor_tensor(g_a[:, 0:2, dr, :], g_a[:, 0:2, dr, :], g_k[:, 0:2, :], ALU.mult).then_inc(ks_ready, 1)

            bt_set = dve.memset(bt[:, :, :, :], 0.0)
            chain(bt_set)

            def cum_out(it):
                dr = it % 2
                dve.wait_ge(cum_mm, it + 1)
                took(dve.tensor_copy(g_C[:, dr, :], dsrc()[:, 0:256]), then=True)
                if dr == 0:
                    chain(dve.tensor_copy(bt[:, 0, 0, 1:8], g_C[:, 0, 31:224:32]))
                else:
                    chain(dve.tensor_copy(bt[:, 1, 0, 0:7], g_C[:, 1, 32:225:32]))
                dve.tensor_scalar(bt[:, dr, 1, :], bt[:, dr, 0, :], 1.0 / 16, None, ALU.mult)
                dve.tensor_tensor(g_qd[:, dr, :].rearrange("p (i t) -> p i t", i=8),
                                  g_C[:, dr, :].rearrange("p (i t) -> p i t", i=8),
                                  wide(bt[:, dr, 0, :].unsqueeze(2), [8, CHUNK]), ALU.subtract).then_inc(cum_sb, 1)

            def decayed(it):
                hd, dr = it // 2, it % 2
                dve.wait_ge(dec_exp, it + 1)
                if hd >= 2:
                    dve.wait_ge(go_mm, hd - 1)
                dve.tensor_tensor(g_qd[:, dr, :], g_qd[:, dr, :], g_qT[:, hd, :], ALU.mult)
                dve.tensor_tensor(g_qf[:, hd % 2, dr, :], g_qf[:, hd % 2, dr, :], g_qT[:, hd, :], ALU.mult)
                for i in range(8):
                    at, a, b = kx(dr, i)
                    c0 = at + a
                    s0 = a + (128 if dr == 1 and i >= 4 else 0)
                    ins = dve.tensor_tensor(g_KX[:, dr, c0:at + b], g_KX[:, dr, c0:at + b],
                                            g_kT[:, hd, s0:s0 + b - a], ALU.mult)
                ins.then_inc(dec_ready, 1)

            cum_out(0)
            cum_out(1)
            decayed(0)
            for it in range(2 * GH):
                if it + 1 < 2 * GH:
                    decayed(it + 1)
                hd, dr = it // 2, it % 2
                dve.wait_ge(at_mm, it + 1)
                took(dve.tensor_tensor(g_AT[:, hd % 2, dr, :], dsrc()[:, 0:384], mask[:, dr, :], ALU.mult))
                if it + 2 < 2 * GH:
                    cum_out(it + 2)
            dve_at["gla masks"] = nd[0]
            rstd([(lambda k: st[:, k, 0:8], GDV)], 8)
            o8 = g_o[:, :, :].rearrange("p j (h v) -> p (j h) v", v=GDV)
            chain(dve.tensor_tensor(o8, o8, wide(st[:, ST_R, 0:8].unsqueeze(2), [8, GDV]), ALU.mult))
            dve.tensor_tensor(g_o[:, :, :], g_o[:, :, :], g_g[:, :, :], ALU.mult).then_inc(go_ready, 1)
            for tt in range(2):
                dve.wait_ge(got_mm, tt + 1)
                cols = slice(P * tt, P * tt + P)
                for half in range(2):
                    split_banks(ug_hi[:, 4 * half:4 * half + 4, cols], ug_lo[:, 4 * half:4 * half + 4, cols])
            project_out("gout", y_gla, (0,))
            residual(y_gla, LAT, 2, 5)
            rstd([(lambda k: st[:, k, 0:2], D)], 2)
            modulate(1, 1, 12, LAT, split=False)

            r8 = [2, E_N]
            dve.wait_ge(logit_mm, 2)
            lg_ps = banks[:, 0, 0:16].rearrange("p (t e) -> p t e", t=2)
            chain(dve.reduce_max(mx, lg_ps, AX.X))
            dve.tensor_tensor(lg, lg_ps, wide(mx.unsqueeze(2), r8), ALU.subtract).then_inc(lg_ready, 1)
            dve.memset(y_acc[:, :, :], 0.0)
            dve.memset(cnt[:, 0:1], 0)
            dve.memset(y_e[:, :, :], 0.0)
            dve.memset(Wc[:, :, :], 0.0)
            chain(dve.memset(tab[:, :], 0.0))
            dve.wait_ge(lg_exp, 1)
            chain(dve.reduce_sum(zs, lg, AX.X))
            chain(dve.reciprocal(zs, zs))
            chain(dve.tensor_tensor(pb_, lg, wide(zs.unsqueeze(2), r8), ALU.mult))

            def first_max(src, top, found):
                chain(dve.reduce_max(top, src, AX.X))
                chain(dve.tensor_tensor(eq, src, wide(top.unsqueeze(2), r8), ALU.is_equal))
                for n in range(2):
                    ins = dve.tensor_tensor_scan(cs[:, n, :], ones[:, 0:E_N], eq[:, n, :], 0.0, ALU.mult, ALU.add)
                chain(ins)
                chain(dve.scalar_tensor_tensor(found, cs, 1.0, eq, ALU.is_equal, ALU.mult))

            first_max(pb_, mx, f1)
            chain(dve.scalar_tensor_tensor(lg, f1, -2.0, pb_, ALU.mult, ALU.add))
            first_max(lg, mx2, f2)
            dve.tensor_tensor(sel, f1, f2, ALU.add).then_inc(sel_ready, 1)
            dve.wait_ge(sel_ready, 1)
            chain(dve.tensor_tensor(mx, mx, mx2, ALU.add))
            chain(dve.reciprocal(mx, mx))
            chain(dve.tensor_tensor(cw, pb_, sel, ALU.mult))
            chain(dve.tensor_tensor(cw, cw, wide(mx.unsqueeze(2), r8), ALU.mult))
            dve.wait_ge(rank_mm, 1)
            t6 = tab[:, :].rearrange("p (e c) -> p c e", c=6)[:, :, 0:E_N]
            chain(dve.tensor_scalar(t6[:, 0:2, :], banks[:, 0, 0:16].rearrange("p (t e) -> p t e", t=2), -1.0, None,
                                    ALU.add))
            chain(dve.tensor_copy(t6[:, 2:4, :], sel))
            chain(dve.tensor_copy(cnt[:, 1:1 + E_N], banks[:, 0, 16:24]))
            dve.tensor_copy(t6[:, 4:6, :], cw).then_inc(tab_ready, 1)
            dve.wait_ge(tab_ready, 1)


            def m_src(at, n):
                dve.wait_ge(m_ready, at + (n + 1))
                return banks[:, 4 + n % 2, :]

            def prepare(e1):
                chain(dve.tensor_copy(ecol[:, 0:6], tab[:, bass.ds(e1 * 6, 6)]))
                for j in range(2):
                    dve.tensor_scalar(Pm[:, j, :], iota[:, :], ecol[:, j:j + 1], ecol[:, 2 + j:3 + j],
                                      ALU.is_equal, ALU.mult)
                    ins = dve.tensor_scalar(Pc[:, j, :], iota[:, :], ecol[:, j:j + 1], ecol[:, 4 + j:5 + j],
                                            ALU.is_equal, ALU.mult)
                ins.then_inc(prep_ready, 1)

            def gather_out(at, n_ready, gs):
                for g in gs:
                    b = m_src(at, M_G + g).rearrange("p (k t) -> p k t", k=2)
                    k0 = 2 * g
                    u = uf[:, 0:512].rearrange("p (k t) -> p k t", k=2)
                    ins = dve.tensor_tensor(u, b, wide(Am[:, 3, k0:k0 + 2, 1:2], [2, 2 * P]), ALU.mult)
                    ins.then_inc(m_took, 1)
                    dve.wait_ge(m_took, at + (M_G + g + 1))
                    chain(dve.tensor_tensor(u, u, wide(shift_of(1, 1)[:, k0:k0 + 2, 1:2], [2, 2 * P]), ALU.add))
                    hi = ug_hi[:, k0:k0 + 2, :]
                    chain(dve.tensor_copy(hi, u))
                    ins = dve.tensor_tensor(ug_lo[:, k0:k0 + 2, :], u, hi.bitcast(F32), ALU.subtract)
                    if g < 3:
                        chain(ins)
                    else:
                        ins.then_inc(ug_ready, 1)
                        dve.wait_ge(ug_ready, n_ready)

            def scatter_out(at):
                for i in range(4):
                    tk, n = i // 2, i % 2
                    y = y_acc[:, tk, 512 * n:512 * n + 512]
                    dve.wait_ge(m_ready, at + (M_S + i + 1))
                    dve.tensor_tensor(y, y, banks[:, 4 + i, :], ALU.add).then_inc(m_took, 1)

            dve.wait_ge(late_in, 16 * 6)
            dve.sem_inc(m_took, M_G)
            dve.sem_inc(gu_took, 1)
            dve.sem_inc(y_took_d, 1)
            prepare(0)
            gather_out(0, 1, range(4))
            dve.sem_inc(m_took, M_ALL - M_G - 4)
            plain_chain = chain
            with dve.Fori(0, E_N) as e:
                ms = e * M_ALL + M_ALL

                def echain(ins):
                    ins.then_inc(loop_step, 1)
                    loop_n[0] += 1
                    dve.wait_ge(loop_step, e * LOOP_STEPS + loop_n[0])

                loop_n = [0]

                def e_lo(u):
                    s = N_PRE + u
                    dve.wait_ge(weights_used, e * PER_E + (s - SPLIT_N + 1))
                    for half in range(2):
                        c = slice(HALF * half, HALF * (half + 1))
                        dve.wait_ge(hi_ready, e * (2 * PER_E) + (2 * s + half + 1))
                        dve.wait_ge(raw_in[s % RAW_N][half], e * (16 * PER_E // RAW_N) + 16 * (s // RAW_N + 1))
                        dve.tensor_tensor(w_lo[:, s % SPLIT_N, c], raw[:, s % RAW_N, c],
                                          w_hi[:, s % SPLIT_N, c].bitcast(F32), ALU.subtract).then_inc(lo_ready, 1)

                def expert(T):
                    loop_n[0] = 0

                    def gated(j):
                        dve.wait_ge(e_silu, e * EJ + (j + 1))
                        dve.wait_ge(weights_used, e * PER_E + (N_PRE + 4 * j + 4))
                        if T == 2 and j:
                            dve.wait_ge(m_ready, ms + (M_H + 2 * j))
                        if T == 1 and j >= 2:
                            dve.wait_ge(m_ready, ms + (M_H + j - 1))
                        for tt in range(T):
                            b = h_at(T, j, tt)
                            ins = dve.tensor_tensor(e_h[:, b, :], e_sil[:, b, :], banks[:, 2 * b + 1, :], ALU.mult)
                        ins.then_inc(gu_took, 1)

                    def h_lo(j):
                        for tt in range(T):
                            n = M_H + T * j + tt
                            b = m_src(ms, n).rearrange("p (k t) -> p k t", k=4)
                            dve.wait_ge(m_hi, e * (2 * EJ) + (2 * j + 2 if T == 1 else 2 * j + tt + 1))
                            sl = (slice(None), slice(4 * j, 4 * j + 4), slice(P * tt, P * tt + P))
                            dve.tensor_tensor(eT_lo[sl], b, eT_hi[sl].bitcast(F32), ALU.subtract).then_inc(m_took, 1)

                    for j in range(1, EJ + 1):
                        for u in range(4 * j, 4 * j + 3):
                            e_lo(u)
                        gated(j - 1)
                        if j == 1:
                            dve.tensor_copy(Wc[:, :, :].rearrange("p s t -> p (s t)"), m_src(ms, M_W)).then_inc(m_took, 1)
                        if j >= 2:
                            h_lo(j - 2)
                        e_lo(4 * j + 3)
                    e_lo(LAST_H + 1)
                    h_lo(EJ - 1)
                    if T == 1:
                        dve.wait_ge(m_took, ms + (M_H + EJ))
                        dve.sem_inc(m_took, EJ)
                    prepare(e + 1)
                    for u in range(LAST_H + 2, PER_E):
                        e_lo(u)
                        if u - 1 in GATHERS:
                            gather_out(ms, e + 2, [GATHERS.index(u - 1)])
                    dve.wait_ge(weights_used, e * PER_E + (N_PRE + PER_E))
                    for tt in range(T):
                        ins = dve.tensor_copy(y_e[:, tt, 512:D], banks[:, 7 if tt == 0 else 1, :])
                    ins.then_inc(y_took_d, 1)
                    assert loop_n[0] == LOOP_STEPS, loop_n

                e_lo(0)
                e_lo(1)
                scatter_out(ms)
                e_lo(2)
                e_lo(3)
                chain = echain
                chosen = dve.value_load(cnt[0:1, bass.ds(e + 1, 1)], min_val=0, max_val=2 * P)
                with dve.If(chosen > P):
                    expert(2)
                with dve.Else():
                    expert(1)
                dve.wait_ge(m_took, ms + (M_ALL - 1))
                dve.sem_inc(m_took, 1)
            chain = plain_chain
            scatter_out((E_N + 1) * M_ALL)
            residual(y_acc, LAT, 3, 6)

        @block.scalar
        def _(act):
            na, steps, nsplit, nr = [0], [0], [0], [0]

            def chain(ins):
                ins.then_inc(act_step, 1)
                steps[0] += 1
                act.wait_ge(act_step, steps[0])

            def asrc():
                na[0] += 1
                return a_bank(na[0] - 1)

            def took(ins, then=False):
                ins.then_inc(act_took, 1)
                if then:
                    act.wait_ge(act_took, na[0])

            def split_to(n):
                while nsplit[0] < min(n, N_PRE):
                    s = nsplit[0]
                    nsplit[0] += 1
                    if s >= SPLIT_N:
                        act.wait_ge(weights_used, s - SPLIT_N + 1)
                    for half, (a, b) in enumerate(halves(units[s][1])):
                        c = slice(units[s][2] * a, units[s][2] * b)
                        r = slice(HALF * half, HALF * half + units[s][2] * (b - a))
                        act.wait_ge(raw_in[s % RAW_N][half], 16 * (s // RAW_N + 1))
                        act.activation(w_hi[:, s % SPLIT_N, c], raw[:, s % RAW_N, r], ACT.Copy).then_inc(hi_ready, 1)

            def after(name, n):
                split_to(ahead_of(name, n))
                act.wait_ge(weights_used, used(name, n))

            def rstd(n):
                nr[0] += 1
                act.wait_ge(var_ready, nr[0])
                y = st[:, ST_R, 0:n]
                chain(act.activation(y, st[:, ST_VAR, 0:n], ACT.Ln))
                act.activation(y, y, ACT.Exp, scale=-0.5).then_inc(guess_ready, 1)
                act.wait_ge(rstd_ready, nr[0])

            nss = [0]

            def squares(srcs, inc=True):
                for n, (src, col) in enumerate(srcs):
                    w = src.shape[-1]
                    ins = act.activation(hn[:, 1, 0:w], src, ACT.Square, accum_out=st[:, ST_SUM, col:col + 1])
                    if n == len(srcs) - 1 and inc:
                        ins.then_inc(ss_ready, 1)
                        nss[0] += 1
                        act.wait_ge(ss_ready, nss[0])
                    else:
                        chain(ins)

            def norm(n0, tiles, wait_new, ahead=0):
                act.wait_ge(*wait_new)
                squares([(h[:, tl, :], i) for i, tl in enumerate(tiles)])
                rstd(len(tiles))
                split_to(ahead)
                for i, tl in enumerate(tiles):
                    if n0 + i >= 2:
                        act.wait_ge(norm_tr, n0 + i - 1)
                    act.activation(hn[:, (n0 + i) % 2, :], h[:, tl, :], ACT.Copy,
                                   scale=st[:, ST_R, i:i + 1]).then_inc(hn_ready, 1)

            def gate_out(streams):
                for s in streams:
                    gn[0] += 1
                    act.wait_ge(gate_mm, gn[0])
                    took(act.activation(Gb[:, s, 0:512], asrc(), ACT.Copy))
                    took(act.activation(Gb[:, s, 512:D], asrc(), ACT.Copy), then=True)
                    act.sem_inc(gate_rows, 1)

            gn = [0]
            rows_in = [(K[:, :], consts[:, 0:C_KEEP]),
                       (rowsA[0:8, :], c_ctx.rearrange("(k p) -> k p", p=P)),
                       (rowsA[8:16, :], cond[0].rearrange("(k p) -> k p", p=P)),
                       (rowsA[16:80, :], norm_g.rearrange("l i (k p) -> (l i k) p", p=P)),
                       (rowsA[80:83, :], attn_q_norm[0].rearrange("(k p) -> k p", p=P)),
                       (rowsA[83:85, :], attn_kv_norm[0].rearrange("(k p) -> k p", p=P)),
                       (rowsB[0:96, :], mod_b.rearrange("l (k p) -> (l k) p", p=P)),
                       (rowC[0:1, 0:128], attn_qk_norm.rearrange("o a d -> o (a d)")),
                       (rowC[0:1, 128:384], gla_o_norm),
                       (rope[:, :, :], consts[:, C_ROPE:C_ROPE + 192].rearrange("p (j c) -> p j c", j=2))]
            for dst, src in rows_in:
                act.dma_start(dst, src).then_inc(const_in, 16)
            act.dma_start(h[:, 0:2, :], ctx[0].rearrange("(t p) d -> p t d", p=P)).then_inc(h_in, 16)
            act.dma_start(h[:, 2:4, :], x[0].rearrange("(t p) d -> p t d", p=P)).then_inc(h_in, 16)
            act.wait_ge(dve_took, 2)
            chain(act.activation(vecs[:, 0:16], vecs[:, 0:16], ACT.Silu))
            act.activation(cv[:, :, 0:2], vecs[:, 0:16].rearrange("p (s k) -> p k s", k=KD),
                           ACT.Copy).then_inc(c_silu, 1)
            split_to(2)
            norm(0, range(TILES), (h_in, 32), used("z", 0) + 2)

            for n in range(3):
                after("z", 2 * n + 2)
                for tl in (2, 3):
                    took(act.activation(z[:, tl, 480 * n:480 * n + 480], asrc()[:, 0:480], ACT.Copy))
            act.wait_ge(act_took, na[0])
            act.wait_ge(z_ready, 1)
            squares([(z[:, tl, a:b], 12 * tl + c) for tl in range(TILES)
                     for c, (a, b) in enumerate(((0, Z_KV), (Z_KV, Z_ROPE)))])
            rstd(48)
            for tl in range(TILES):
                for c, (a, b) in enumerate(((0, Z_KV), (Z_KV, Z_ROPE))):
                    ins = act.activation(z[:, tl, a:b], z[:, tl, a:b], ACT.Copy,
                                         scale=st[:, ST_R, 12 * tl + c:12 * tl + c + 1])
                ins.then_inc(lat_scaled, 1)
            split_to(used("uq", 0) + 2)
            for n in range(2):
                after("uq", n + 1)
                for tl in (2, 3):
                    took(act.activation(qa[:, tl, 384 * n:384 * n + 384], asrc()[:, 0:384], ACT.Copy))
            split_to(used("mods", 0) + 2)

            def copy(dst, src):
                return act.activation(dst, src, ACT.Copy)

            for tl in (2, 3):
                for n in range(2):
                    if (tl, n) == (3, 1):
                        act.wait_ge(weights_used, used("ukv", 1))
                    else:
                        act.wait_ge(ukv_mm, 2 * tl + n + 1)
                    b = asrc().rearrange("p (h c) -> p h c", c=P)
                    copy(ka[:, tl, :].rearrange("p (h c) -> p h c", c=DQ)[:, 4 * n:4 * n + 4, 0:NOPE], b[:, :, 0:NOPE])
                    took(copy(va[:, tl, 256 * n:256 * n + 256].rearrange("p (h c) -> p h c", c=DV), b[:, :, NOPE:P]))

            def q_out(hd):
                w = DQ if hd < HEADS else GD
                act.wait_ge(q_tr, hd + 1)
                took(act.activation(qT[0:w, hd % 2, :], asrc()[0:w, :], ACT.Copy), then=True)
                act.sem_inc(q_sb, 1)

            q_out(0)
            for n in range(NI + 2):
                if n < NI:
                    hd, tl = ITEMS[n]
                    w = P * keys(tl)
                    if n % 4 == 1 and n // 4 + 1 < HEADS + GQ:
                        act.wait_ge(s_done, n)
                        q_out(n // 4 + 1)
                    act.wait_ge(nb_ready, n + 1)
                    if n >= 3:
                        act.wait_ge(p_tr, n - 2)
                    c = n % 8
                    took(act.activation(Pr[:, n % 3, 0:w], asrc()[:, 0:w], ACT.Exp, bias=sm[:, 8 + c:9 + c],
                                        scale=float(DQ if hd < HEADS else GD) ** -0.5,
                                        accum_out=sm[:, 16 + c:17 + c]), then=True)
                    act.sem_inc(exp_done, 1)
                if n >= 2:
                    hd, tl = ITEMS[n - 2]
                    w = P * keys(tl)
                    act.wait_ge(p_tr, n - 1)
                    if n >= 5:
                        act.wait_ge(pv_done, n - 4)
                    took(act.activation(PT[:, (n - 2) % 3, 0:w], asrc()[:, 0:w], ACT.Copy), then=True)
                    act.sem_inc(pt_sb, 1)
                if mod_turn(n):
                    split_to(ahead_of("mods", 2 * (mod_turn(n) - MG0) + 2))
            split_to(used("wo", 0) + SPLIT_N - 1)

            def project_out(name, y, tiles):
                for n in range(2):
                    after(name, 2 * n + 2)
                    for tl in tiles:
                        took(act.activation(y[:, tl, 512 * n:512 * n + 512], asrc(), ACT.Copy), then=(n == 1))

            project_out("wo", y_attn, (2, 3))
            act.wait_ge(dve_took, dve_at["wo"])
            squares([(y_attn[:, tl, :], tl) for tl in range(TILES)])
            gate_out((0, 1))
            rstd(TILES)
            norm(4, range(TILES), (h_new, 4), used("gu", 0) + 2)

            for j in range(NF // 2):
                after("gu", 4 * j + 1)
                for fc in range(2):
                    f = 2 * j + fc
                    if f >= 2:
                        act.wait_ge(dve_took, dve_at["ffn"] + f - 1 + (f - 2) // 2)
                    elif f == 0:
                        act.wait_ge(norm_tr, 8)
                    took(act.activation(sil[:, f % 2, :], asrc(), ACT.Silu), then=True)
                    act.sem_inc(silu_ready, 1)
                split_to(ahead_of("gu", 4 * j + 4))
            split_to(ahead_of("gu", 4 * (NF // 2) + 2))
            for n in range(2):
                for d in range(len(DOWN)):
                    after("down", n * len(DOWN) + d + 1)
                for tl in (2, 3):
                    took(act.activation(y_ffn[:, tl, 512 * n:512 * n + 512], asrc(), ACT.Copy), then=(n == 1))
            act.wait_ge(dve_took, dve_at["down"])
            squares([(y_ffn[:, tl, :], tl) for tl in range(TILES)])
            act.wait_ge(h_new, 4)
            gate_out((0, 1))
            rstd(TILES)
            norm(8, range(TILES), (h_new, 8), used("gin", 0) + 2)

            for n, (dst, c0) in enumerate(((g_k, 0), (g_v, 0), (g_v, 512))):
                after("gin", 2 * n + 3)
                for tl in (2, 3):
                    took(act.activation(dst[:, tl, c0:c0 + 512], asrc(), ACT.Copy))
            after("gin", 9)
            took(act.activation(g_q[:, 1, :], asrc(), ACT.Copy))
            for n in range(2):
                after("gin", 11 + 2 * n)
                for j in range(2):
                    took(act.activation(g_g[:, j, 512 * n:512 * n + 512], asrc(), ACT.Silu))
            for i in range(8):
                act.wait_ge(dve_took, dve_at["gate", i])
                eb = ebuf[:, i % 2, :]
                chain(act.activation(eb, eb, ACT.Exp))
                act.activation(eb, eb, ACT.Ln, bias=1.0).then_inc(e_ln, 1)
            for dr in range(2):
                act.wait_ge(dve_took, dve_at["tail", dr])
                act.activation(g_a[:, 0:2, dr, :], g_a[:, 0:2, dr, :], ACT.Exp, scale=1.0 / 16).then_inc(tail_exp, 1)
            for n in range(4):
                dr, hp = n // 2, n % 2
                act.wait_ge(s0_mm, n + 1)
                took(act.activation(g_S[:, dr, 2 * hp:2 * hp + 2, :].rearrange("p h v -> p (h v)"), asrc(), ACT.Copy))

            def decays(it):
                hd, dr = it // 2, it % 2
                act.wait_ge(cum_sb, it + 1)
                if hd >= 2:
                    act.wait_ge(go_mm, hd - 1)
                act.activation(g_qd[:, dr, :], g_qd[:, dr, :], ACT.Exp, scale=1.0 / 16)
                act.activation(g_qf[:, hd % 2, dr, :], g_C[:, dr, :], ACT.Exp, scale=1.0 / 16)
                for i in range(8):
                    at, a, b = kx(dr, i)
                    s0 = a + (128 if dr == 1 and i >= 4 else 0)
                    ins = act.activation(g_KX[:, dr, at + a:at + b], g_C[:, dr, s0:s0 + b - a], ACT.Exp,
                                         bias=bt[:, dr, 1, i:i + 1], scale=-1.0 / 16)
                ins.then_inc(dec_exp, 1)

            def head_out(hd):
                act.wait_ge(go_mm, hd + 1)
                b = asrc().rearrange("p (j v) -> p j v", j=2)
                took(act.activation(g_o[:, :, GDV * hd:GDV * hd + GDV], b, ACT.Copy), then=True)
                squares([(g_o[:, j, GDV * hd:GDV * hd + GDV], 4 * j + hd) for j in range(2)], inc=(hd == GH - 1))

            act.wait_ge(kx_zero, 1)
            for it in range(2 * GH):
                decays(it)
                if it % 2 == 1 and it >= 3:
                    head_out(it // 2 - 1)
            head_out(GH - 1)
            rstd(8)
            split_to(used("gout", 0) + 2)
            for n in range(2):
                after("gout", 2 * n + 2)
                took(act.activation(y_gla[:, 1, 512 * n:512 * n + 512], asrc(), ACT.Copy), then=(n == 1))
            act.wait_ge(dve_took, dve_at["gout"])
            squares([(y_gla[:, j, :], j) for j in range(2)])
            gate_out((1,))
            rstd(2)
            norm(12, LAT, (h_new, 10))
            act.wait_ge(lg_ready, 1)
            act.activation(lg, lg, ACT.Exp).then_inc(lg_exp, 1)

            act.wait_ge(tab_ready, 1)
            act.sem_inc(y_took_a, 1)
            with act.Fori(0, E_N) as e:
                ms = e * M_ALL + M_ALL

                def e_hi(u):
                    s = N_PRE + u
                    act.wait_ge(weights_used, e * PER_E + (s - SPLIT_N + 1))
                    for half in range(2):
                        c = slice(HALF * half, HALF * (half + 1))
                        act.wait_ge(raw_in[s % RAW_N][half], e * (16 * PER_E // RAW_N) + 16 * (s // RAW_N + 1))
                        act.activation(w_hi[:, s % SPLIT_N, c], raw[:, s % RAW_N, c], ACT.Copy).then_inc(hi_ready, 1)

                def expert(T):
                    def e_silus(j):
                        act.wait_ge(weights_used, e * PER_E + (N_PRE + 4 * j + 2))
                        act.wait_ge(gu_took, e * EJ + gu_free(T, j))
                        for tt in range(T):
                            b = h_at(T, j, tt)
                            ins = act.activation(e_sil[:, b, :], banks[:, 2 * b, :], ACT.Silu)
                        ins.then_inc(e_silu, 1)

                    def h_hi(j):
                        for tt in range(T):
                            n = M_H + T * j + tt
                            act.wait_ge(m_ready, ms + (n + 1))
                            b = banks[:, 4 + n % 2, :].rearrange("p (k t) -> p k t", k=4)
                            act.activation(eT_hi[:, 4 * j:4 * j + 4, P * tt:P * tt + P], b, ACT.Copy)\
                                .then_inc(m_hi, 2 // T)

                    for j in range(1, EJ + 1):
                        for u in range(4 * j, 4 * j + 3):
                            e_hi(u)
                        e_silus(j - 1)
                        if j >= 2:
                            h_hi(j - 2)
                        e_hi(4 * j + 3)
                    e_hi(LAST_H + 1)
                    h_hi(EJ - 1)
                    for u in range(LAST_H + 2, PER_E):
                        e_hi(u)
                    act.wait_ge(weights_used, e * PER_E + (N_PRE + PER_E))
                    act.wait_ge(m_ready, ms + (M_S + 4))
                    for tt in range(T):
                        ins = act.activation(y_e[:, tt, 0:512], banks[:, 6 if tt == 0 else 0, :], ACT.Copy)
                    ins.then_inc(y_took_a, 1)

                for u in range(4):
                    e_hi(u)
                chosen = act.value_load(cnt[0:1, bass.ds(e + 1, 1)], min_val=0, max_val=2 * P)
                with act.If(chosen > P):
                    expert(2)
                with act.Else():
                    expert(1)
            act.wait_ge(m_took, (E_N + 1) * M_ALL + 4)
            squares([(y_acc[:, j, :], j) for j in range(2)])
            gate_out((1,))
            rstd(2)

        @block.gpsimd
        def _(pool):
            def diagonals(site, streams):
                for s in streams:
                    if dn[0]:
                        pool.wait_ge(gate_mm, dn[0])
                    for k in range(KD):
                        ins = pool.tensor_scalar(hn[:, 0, P * k:P * k + P], ident, Gm[:, site, k, s:s + 1], None,
                                                 ALU.mult)
                    ins.then_inc(diag_ready, 1)
                    dn[0] += 1

            dn = [0]
            pool.wait_ge(mods_ready, 1)
            diagonals(0, (0, 1))
            pool.wait_ge(weights_used, used("down", 1))
            diagonals(1, (0, 1))
            pool.wait_ge(h_new, 8)
            pool.dma_start(mask[:, :, :], consts[:, C_MASK:C_MASK + 768].rearrange("p (d c) -> p d c", d=2))\
                .then_inc(late_in, 16)
            pool.wait_ge(weights_used, used("gin", 13))
            pool.dma_start(wg2[0:GRANK, :, :], gla_w_gate2[0].rearrange("d r n -> r d n")).then_inc(late_in, 16)
            pool.dma_start(wg2[GRANK:GRANK + 1, :, :], gla_b_gate).then_inc(late_in, 16)
            pool.memset(rT[0:32, :, :], 1.0).then_inc(rt_one, 1)
            pool.wait_ge(z2_mm, 8)
            pool.memset(g_KX[:, :, :], 0.0).then_inc(kx_zero, 1)
            pool.wait_ge(r_tr, 2)
            pool.wait_ge(mods_ready, 2)
            diagonals(2, (1,))
            pool.wait_ge(at_mm, 2 * GH)
            pool.dma_start(wr, moe_w_router[0].rearrange("(k p) e -> p k e", p=P)).then_inc(late_in, 16)
            pool.dma_start(brow[0:1, :], moe_b_router).then_inc(late_in, 16)
            pool.dma_start(iota[:, :], consts[:, C_IOTA:C_IOTA + 256]).then_inc(late_in, 16)
            pool.wait_ge(m_took, (E_N + 1) * M_ALL + 4)
            diagonals(3, (1,))


def _constants(np):
    k = np.zeros((P, C_ALL), np.float32)
    k[:, C_ID:C_ID + P] = np.eye(P)
    k[:, C_ONE:C_ONE + P] = 1
    k[0:4, C_PAIR:C_PAIR + 2] = np.tile(np.eye(2), (2, 1))
    s, t = np.arange(256)[:, None], np.arange(256)[None, :]
    tri = [(s <= t).astype(np.float32), (s >= t).astype(np.float32)]
    for at, m in zip((C_TRI_F, C_TRI_B), tri):
        k[:, at:at + 512] = m.reshape(2, P, 256).transpose(1, 0, 2).reshape(P, 512)
    blocks = ([(0, 0), (1, 0), (1, 1)], [(0, 0), (0, 1), (1, 1)])
    for d in range(2):
        for n, (tt, j) in enumerate(blocks[d]):
            at = C_MASK + 384 * d + P * n
            k[:, at:at + P] = tri[d][P * j:P * j + P, P * tt:P * tt + P]
    k[:, C_IOTA:C_IOTA + 256] = np.arange(256)
    tok = np.arange(256)
    pos = np.stack([tok // 64, tok % 64]).astype(np.float32)
    for at, n in ((0, 16), (64, 8)):
        freq = (np.float32(10000.0) ** (-np.arange(0, 2 * n, 2, dtype=np.float32) / np.float32(2 * n)))
        ang = pos[:, :, None] * freq[None, None, :].astype(np.float32)
        for f, fn in enumerate((np.cos, np.sin)):
            v = fn(ang.astype(np.float32)).astype(np.float32).transpose(1, 0, 2).reshape(256, 2 * n)
            for j in range(2):
                c0 = C_ROPE + 96 * j + at + 2 * n * f
                k[:, c0:c0 + 2 * n] = v[P * j:P * j + P]
    return k


_INS = ['x', 'c', 'ctx', 'c_ctx', 'mod_w', 'mod_b', 'norm_g', 'attn_w_in', 'attn_q_norm', 'attn_w_uq', 'attn_kv_norm',
        'attn_w_ukv', 'attn_qk_norm', 'attn_w_out', 'gla_w_in', 'gla_w_gate2', 'gla_b_gate', 'gla_o_norm',
        'gla_w_out', 'ffn_w_gate', 'ffn_w_up', 'ffn_w_down', 'moe_w_router', 'moe_b_router', 'moe_w_gate',
        'moe_w_up', 'moe_w_down']


def kernel(**inputs):
    import numpy as _np
    import concourse.bacc as _bacc
    from concourse import mybir as _mybir
    from concourse.bass_utils import run_bass_kernel_spmd as _run

    nc = _bacc.Bacc("TRN2", target_bir_lowering=False, num_devices=1)
    arrays, args = {}, []
    for name in _INS:
        a = _np.ascontiguousarray(inputs[name])
        arrays[f"in_{name}_dram"] = a
        args.append(nc.dram_tensor(f"in_{name}_dram", a.shape, _mybir.dt.from_np(a.dtype), kind="ExternalInput").ap())
    k = _constants(_np)
    arrays["in_consts_dram"] = k
    args.append(nc.dram_tensor("in_consts_dram", k.shape, _mybir.dt.from_np(k.dtype), kind="ExternalInput").ap())
    args.append(nc.dram_tensor("out_0_dram", (1, 256, D), _mybir.dt.float32, kind="ExternalOutput").ap())
    hybrid_block(nc, *args)
    r = _run(nc, [arrays], core_ids=[0])
    return r.results[0]["out_0_dram"]
```

```python
import concourse.bass as bass
from concourse import mybir
from contextlib import ExitStack

F32 = mybir.dt.float32
F32R = mybir.dt.float32r
I32 = mybir.dt.int32
ALU = mybir.AluOpType
ACT = mybir.ActivationFunctionType
AX = mybir.AxisListType

P = 128
D = 1024
KD = D // P
TILES = 4
LAT = (2, 3)
EPS = 1e-6
Q_RANK, KV_RANK = 384, 256
HEADS, ROPE_M, NOPE, DV = 8, 32, 64, 64
DQ = NOPE + ROPE_M
GQ, GKV, GD = 8, 2, 64
ZW = 1440
Z_KV, Z_ROPE, Z_Q, Z_K, Z_V = 384, 640, 672, 1184, 1312
F_FFN = 2816
NF = F_FFN // P
GH, GDK, GDV, GRANK = 4, 128, 256, 16
CHUNK = 32
E_N, E_DIM = 8, 3584
EF = E_DIM // P
EJ = E_DIM // 512
MOD_STEP = 7
MG, MG0 = 12, 4

RAW_N = 3
SPLIT_N = 3
UNIT = 2048
HALF = UNIT // 2

C_ID, C_ONE, C_TRI_F, C_TRI_B = 0, 128, 256, 768
C_PAIR, C_KEEP = 1280, 1296
C_MASK, C_IOTA, C_ROPE, C_ALL = 1296, 2064, 2320, 2512


def hybrid_block(nc, x, cond, ctx, c_ctx, mod_w, mod_b, norm_g, attn_w_in, attn_q_norm, attn_w_uq, attn_kv_norm,
                 attn_w_ukv, attn_qk_norm, attn_w_out, gla_w_in, gla_w_gate2, gla_b_gate, gla_o_norm, gla_w_out,
                 ffn_w_gate, ffn_w_up, ffn_w_down, moe_w_router, moe_b_router, moe_w_gate, moe_w_up, moe_w_down,
                 consts, out):
    units = []

    def rows(w, r0, nk, c0, n):
        return w[r0:r0 + nk * P, c0:c0 + n].rearrange("(k p) n -> p k n", p=P)

    def stream(w, r0, nk, c0, n):
        units.append((rows(w, r0, nk, c0, n), nk, n))

    def mod_units(a, b):
        for g in range(a, b):
            for kh in range(2):
                stream(mod_w[g // MG], 512 * kh, 4, 512 * (g % MG), 512)

    mod_units(0, MG0)
    for n in range(3):
        for kh in range(2):
            stream(attn_w_in[0], 512 * kh, 4, 480 * n, 480)
    for n in range(2):
        stream(attn_w_uq[0], 0, 3, 384 * n, 384)
    stream(attn_w_ukv[0], 0, 2, 0, 1024)
    mod_units(MG0, MG)
    for n in range(2):
        for kh in range(2):
            stream(attn_w_out[0], 512 * kh, 4, 512 * n, 512)
    for j in range(NF // 2):
        stream(ffn_w_gate[0], 0, KD, 256 * j, 256)
        stream(ffn_w_up[0], 0, KD, 256 * j, 256)
        mod_units(MG + j, MG + j + 1)
    mod_units(2 * MG - 1, 2 * MG)
    DOWN = [(f, min(4, NF - f)) for f in range(0, NF, 4)]
    for n in range(2):
        for f, m in DOWN:
            stream(ffn_w_down[0], P * f, m, 512 * n, 512)
    stream(gla_w_in[0], 0, KD, 3072, 32)
    G_COLS = [512, 1024, 1536, 0, 2048, 2560]
    for c0 in G_COLS:
        for kh in range(2):
            stream(gla_w_in[0], 512 * kh, 4, c0, 512)
    for n in range(2):
        for kh in range(2):
            stream(gla_w_out[0], 512 * kh, 4, 512 * n, 512)
    N_PRE = len(units)
    PER_E = 6 * EJ
    assert PER_E % RAW_N == 0 and PER_E % SPLIT_N == 0

    with ExitStack() as es:
        BASE = (nc.sbuf_base + 63) // 64 * 64

        offset = [0]

        def region(floats):
            at = offset[0]
            offset[0] += floats
            return at

        def place(name, at, shape, dt=F32):
            return nc.alloc_sbuf_tensor_at(name, [P] + shape, dt, offset=BASE + 4 * at)

        R_K = region(C_KEEP)
        R_H = region(4096)
        R_U = region(8192)
        R_RAW = region(RAW_N * UNIT)
        R_SP = region(2 * SPLIT_N * UNIT)
        R_AR = region(14336)
        R_G = region(2048)
        R_T = region(3072)
        R_S = region(1264)
        es.enter_context(nc.sbuf_tensor("fence", [P, offset[0] + 32], F32))

        K = place("K", R_K, [C_KEEP])
        h = place("h", R_H, [TILES, D])
        uT_hi = place("uT_hi", R_U, [KD, 512], F32R)
        uT_lo = place("uT_lo", R_U + 4096, [KD, 512], F32R)
        raw = place("raw", R_RAW, [RAW_N, UNIT])
        w_hi = place("w_hi", R_SP, [SPLIT_N, UNIT], F32R)
        w_lo = place("w_lo", R_SP + SPLIT_N * UNIT, [SPLIT_N, UNIT], F32R)
        Gb = place("Gb", R_G, [2, D])
        hn = place("hn", R_T, [2, D])
        uf = place("uf", R_T + 2048, [D])
        vecs = place("vecs", R_S, [181])
        cv = place("cv", R_S + 1232, [KD, 4], F32R)
        modT = place("modT", R_S + 184, [2, 48, 2])
        Am = place("Am", R_S + 376, [4, KD, 2])
        Gm = place("Gm", R_S + 440, [4, KD, 2])
        bc = place("bc", R_S + 504, [384])
        st = place("st", R_S + 888, [4, 48])
        sm = place("sm", R_S + 1080, [32])
        bt = place("bt", R_S + 1112, [2, 2, 8])
        ecol = place("ecol", R_S + 1144, [8])
        one_sqrt = place("one_sqrt", R_S + 1224, [1])[:, :]
        cnt = place("cnt", R_S + 1152, [16], I32)

        rowsA = place("rowsA", R_AR, [P])
        rowsB = place("rowsB", R_AR + 128, [P])
        rowC = place("rowC", R_AR + 256, [384])
        rope = place("rope", R_G, [2, 96])
        ub = [uf, place("uf2", R_AR + 4096, [D])]
        z = place("z", R_AR, [TILES, ZW])
        qa = place("qa", R_AR + 5760, [TILES, 768])
        ka = place("ka", R_AR + 8832, [TILES, 768])
        va = place("va", R_AR + 11904, [TILES, 512])
        mrow = [place("mrow0", R_U + 5120, [2, 512]), place("mrow1", R_AR + 512 * NF, [2, 512])]
        qT = place("qT", R_U, [2, 512])
        kT = place("kT", R_U + 1024, [2, 512])
        PT = place("PT", R_U + 2048, [2, 6, 256])
        Pr = place("Pr", R_U + 6144, [4, 512])
        oT_r = place("oT_r", R_T, [6, 512])
        dg0 = place("dg0", R_AR + 8832, [2, D])
        y_attn = place("y_attn", R_AR, [TILES, D])
        hT = place("hT", R_AR, [NF, 512])
        sil = place("sil", R_T, [2, 512])
        hs = place("hs", R_T + 1024, [2, 2, 512], F32R)
        y_ffn = place("y_ffn", R_U, [TILES, D])
        dg1 = place("dg1", R_U + 4096, [2, D])
        g_q = place("g_q", R_AR, [2, 512])
        g_k = place("g_k", R_AR + 1024, [TILES, 512])
        g_v = place("g_v", R_AR + 3072, [TILES, D])
        g_g = place("g_g", R_AR + 7168, [2, D])
        g_a = place("g_a", R_AR + 9216, [TILES, 2, 512])
        g_C = place("g_C", R_AR + 13312, [2, 256])
        g_qd = place("g_qd", R_AR + 13824, [2, 256])
        g_qf = place("g_qf", R_AR, [2, 2, 256])
        g_AT = place("g_AT", R_AR + 1024, [2, 2, 384])
        g_o = place("g_o", R_AR + 9216, [2, D])
        g_qT = place("g_qT", R_U, [GH, 256])
        g_kT = place("g_kT", R_U + 1024, [GH, 256])
        g_S = place("g_S", R_U + 2048, [2, GH, 256])
        g_KX = place("g_KX", R_U + 4096, [2, 1536])
        rT = place("rT", R_T, [2, 512])
        wg2 = place("wg2", R_G + 1024, [2, 512])
        ebuf = place("ebuf", R_T + 1024, [4, 512])
        mask = place("mask", R_G, [2, 384])
        ug_hi = place("ug_hi", R_U, [KD, 256], F32R)
        ug_lo = place("ug_lo", R_U + 2048, [KD, 256], F32R)
        y_gla = place("y_gla", R_AR, [2, D])
        Pm = place("Pm", R_U + 4096, [2, 256])
        Pc = place("Pc", R_U + 4608, [2, 256])
        Wc = place("Wc", R_U + 5120, [2, 256])
        e_sil = place("e_sil", R_U + 5632, [2, 512])
        e_h = place("e_h", R_U + 6656, [2, 512])
        iota = place("iota", R_U + 7680, [256])
        rt = place("rt", R_U + 7936, [256])
        eT_hi = place("eT_hi", R_AR, [EF, 256], F32R)
        eT_lo = place("eT_lo", R_AR + EF * 256, [EF, 256], F32R)
        y_e = place("y_e", R_G, [2, D])
        y_acc = place("y_acc", R_H, [2, D])
        wr = rt[:, 0:64].rearrange("p (k e) -> p k e", e=E_N)
        lg, pb_, eq, cs, f1, f2, sel, cw = (rt[:, 64 + 16 * i:80 + 16 * i].rearrange("p (t e) -> p t e", e=E_N)
                                            for i in range(8))
        mx, mx2, zs = (rt[:, 192 + 2 * i:194 + 2 * i] for i in range(3))
        brow = rt[:, 200:208]
        tab = place("tab", R_S + 1168, [6 * 9])

        banks = es.enter_context(nc.psum_tensor("banks", [P, 8, 512], F32))

        def sem(name):
            return es.enter_context(nc.semaphore(name))

        const_in, h_in, late_in = map(sem, ("const_in", "h_in", "late_in"))
        hi_ready, weights_used = map(sem, ("hi_ready", "weights_used"))
        raw_in = [[sem(f"raw_in{i}_{half}") for half in range(2)] for i in range(RAW_N)]
        lo_ready = [sem("lo_ready0"), sem("lo_ready1")]
        dve_took, act_took, bank0_took = map(sem, ("dve_took", "act_took", "bank0_took"))
        dve_step, act_step, loop_step = map(sem, ("dve_step", "act_step", "loop_step"))
        setup_pe, c_silu, cv_ready, mod_cols_done = map(sem, ("setup_pe", "c_silu", "cv_ready", "mod_cols_done"))
        ss_ready, var_ready, sqrt_ready, rstd_ready = map(sem, ("ss_ready", "var_ready", "sqrt_ready", "rstd_ready"))
        hn_ready, norm_tr, u_half, u_high, u_ready = map(sem, ("hn_ready", "norm_tr", "u_half", "u_high", "u_ready"))
        mods_ready, diag_ready, gate_mm, gate_rows, h_new = map(
            sem, ("mods_ready", "diag_ready", "gate_mm", "gate_rows", "h_new"))
        lat_scaled, lat_tr, lat_split, ukv_mm, rope_done = map(
            sem, ("lat_scaled", "lat_tr", "lat_split", "ukv_mm", "rope_done"))
        q_tr, k_tr, q_sb, k_sb = map(sem, ("q_tr", "k_tr", "q_sb", "k_sb"))
        s_done, nb_ready, exp_done, pn_ready, p_tr, pt_sb, pv_done = map(
            sem, ("s_done", "nb_ready", "exp_done", "pn_ready", "p_tr", "pt_sb", "pv_done"))
        o_hi, o_split = map(sem, ("o_hi", "o_split"))
        silu_ready, hs_ready, hs_used = map(sem, ("silu_ready", "hs_ready", "hs_used"))
        rt_one, rt_sb, z2_mm, e_ln, a_ready = map(sem, ("rt_one", "rt_sb", "z2_mm", "e_ln", "a_ready"))
        gt_mm, tail_mm, tail_exp, ks_ready, s0_mm, kx_zero = map(
            sem, ("gt_mm", "tail_mm", "tail_exp", "ks_ready", "s0_mm", "kx_zero"))
        cum_mm, cum_sb, dec_exp, dec_ready, at_mm, go_mm, go_ready, got_mm = map(
            sem, ("cum_mm", "cum_sb", "dec_exp", "dec_ready", "at_mm", "go_mm", "go_ready", "got_mm"))
        uf_ready, logit_mm, lg_ready, lg_exp, sel_ready, rank_mm, tab_ready = map(
            sem, ("uf_ready", "logit_mm", "lg_ready", "lg_exp", "sel_ready", "rank_mm", "tab_ready"))
        prep_ready, ug_ready, e_silu, gu_took = map(sem, ("prep_ready", "ug_ready", "e_silu", "gu_took"))
        m_ready, m_took, m_hi, y_took_a, y_took_d = map(sem, ("m_ready", "m_took", "m_hi", "y_took_a", "y_took_d"))
        stored = sem("stored")

        ident = K[:, C_ID:C_ID + P]
        ones = K[:, C_ONE:C_ONE + P]
        tri = [K[:, C_TRI_F:C_TRI_F + 512].rearrange("p (j t) -> p j t", j=2),
               K[:, C_TRI_B:C_TRI_B + 512].rearrange("p (j t) -> p j t", j=2)]

        def shift_of(layer, which):
            f = 24 * which
            return modT[:, layer, f:f + KD, :]

        def wide(ap, dims):
            return ap.to_broadcast([P] + dims)

        def d_bank(n):
            return banks[:, 1 + n % 3, :]

        def a_bank(n):
            return banks[:, 4 + n % 4, :]

        sidx = {}
        t = 0
        for name, n in (("mod0a", 2 * MG0), ("z", 6), ("uq", 2), ("ukv", 1), ("mods", 2 * MG - 2 * MG0), ("wo", 4),
                        ("gu", NF + 2 * MG), ("down", 2 * len(DOWN)), ("gin", 13), ("gout", 4)):
            sidx[name] = t
            t += n
        assert t == N_PRE

        def used(name, n):
            return sidx[name] + n

        def ahead_of(name, n):
            return used(name, n) + SPLIT_N - 1

        def halves(nk):
            return (0, (nk + 1) // 2), ((nk + 1) // 2, nk)

        def mod_turn(n):
            g = MG0 + n // MOD_STEP
            return g if n % MOD_STEP == 1 and g < MG else None

        ITEMS = [(hd, tl) for hd in range(HEADS + GQ) for tl in (2, 3, 0, 1)]
        NI = len(ITEMS)

        def keys(tl):
            return 4 if tl in LAT else 2

        def o_rows(hd):
            return slice(DV * (hd % 2), DV * (hd % 2) + DV)

        def oT(kk):
            return oT_r[:, kk, :] if kk < 6 else z[:, kk - 6, 0:512]

        def k_turn(hd):
            return hd if hd < HEADS else HEADS + (hd - HEADS) // (GQ // GKV)

        def kx(dr, i):
            if dr == 0:
                return (128 * i, 0, 32 * (i + 1)) if i < 4 else (512 + 256 * (i - 4), 0, 32 * (i + 1))
            return (128 * (i - 4), 32 * i - 128, 128) if i >= 4 else (512 + 256 * i, 32 * i, 256)

        def kx_tile(dr, i, j):
            at = kx(dr, i)[0]
            whole = i >= 4 if dr == 0 else i < 4
            return at + (128 * j if whole else 0)

        BLOCKS = [[(0, 0), (1, 0), (1, 1)], [(0, 0), (0, 1), (1, 1)]]
        ST_SUM, ST_VAR, ST_R, ST_T = 0, 1, 2, 3

        M_S, M_W, M_H, M_G = 0, 4, 5, 19
        M_ALL = 24
        GATHERS = (33, 35, 37, 39)
        LAST_H = 31
        LOOP_STEPS = 12

        def diagonal(site, s):
            return (dg0, dg1)[site][:, s, :] if site < 2 else hn[:, 0, :]

        def h_at(T, j, tt):
            return tt if T == 2 else j % 2

        def gu_free(T, j):
            return j + 1 if T == 2 else max(j, 1)

        pe_at = {}

        block = es.enter_context(nc.Block())

        @block.sync
        def _(sp):
            for i, (view, nk, n) in enumerate(units):
                slot = i % RAW_N
                for half, (a, b) in enumerate(halves(nk)):
                    if i >= RAW_N:
                        sp.wait_ge(lo_ready[half], i - RAW_N + 1)
                    dst = raw[:, slot, HALF * half:HALF * half + (b - a) * n].rearrange("p (k n) -> p k n", n=n)
                    sp.dma_start(dst, view[:, a:b, :]).then_inc(raw_in[slot][half], 16)
            with sp.Fori(0, E_N) as e:
                for u in range(PER_E):
                    i = N_PRE + u
                    slot = i % RAW_N
                    if u < 4 * EJ:
                        w = moe_w_gate if u % 4 < 2 else moe_w_up
                        j, kh = u // 4, u % 2
                        view = w[0, bass.ds(e, 1), 512 * kh:512 * kh + 512, 512 * j:512 * j + 512]
                        view = view.rearrange("o (k p) n -> p (o k) n", p=P)
                        dst = raw[:, slot, :].rearrange("p (k n) -> p k n", k=4)
                    else:
                        f = 2 * (u - 4 * EJ)
                        view = moe_w_down[0, bass.ds(e, 1), P * f:P * f + 256, :]
                        view = view.rearrange("o (k p) n -> p (o k) n", p=P)
                        dst = raw[:, slot, :].rearrange("p (k n) -> p k n", k=2)
                    for half, (a, b) in enumerate(halves(4 if u < 4 * EJ else 2)):
                        sp.wait_ge(lo_ready[half], e * PER_E + (i - RAW_N + 1))
                        sp.dma_start(dst[:, a:b, :], view[:, a:b, :]).then_inc(raw_in[slot][half], 16)
            sp.wait_ge(h_new, 10 + 2)
            for n, tl in enumerate(LAT):
                sp.dma_start(out[0, P * n:P * n + P, :], h[:, tl, :]).then_inc(stored, 16)
            sp.wait_ge(stored, 32)

        @block.tensor
        def _(pe):
            nd, na = [0], [0]
            unit = [0]

            def dbank():
                n = nd[0]
                if n >= 3:
                    pe.wait_ge(dve_took, n - 2)
                nd[0] += 1
                return d_bank(n)

            def abank():
                n = na[0]
                if n >= 4:
                    pe.wait_ge(act_took, n - 3)
                na[0] += 1
                return a_bank(n)

            def tiles_banks():
                return [dbank(), dbank(), abank(), abank()]

            def weights():
                i = unit[0]
                unit[0] += 1
                _, nk, n = units[i]
                pe.wait_ge(hi_ready, 2 * i + 2)
                pe.wait_ge(lo_ready[0], i + 1)
                pe.wait_ge(lo_ready[1], i + 1)
                return [w[:, i % SPLIT_N, 0:nk * n].rearrange("p (k n) -> p k n", k=nk) for w in (w_hi, w_lo)]

            def mm3(o, lh, ll, rh, rl, first, last):
                pe.matmul(o, lh, rh, start=first, stop=False)
                pe.matmul(o, lh, rl, start=False, stop=False)
                return pe.matmul(o, ll, rh, start=False, stop=last)

            def mod_rows(g):
                b = dbank()[0:4, :]
                mod_at[g] = nd[0]
                for kh in range(2):
                    parts = weights()
                    for k in range(4):
                        for part in range(2):
                            mm = pe.matmul(b, cv[:, 4 * kh + k, :], parts[part][:, k, :],
                                           start=(kh == k == part == 0), stop=(kh == 1 and k == 3 and part == 1))
                    mm.then_inc(weights_used, 1)

            def mod_cols(g):
                pe.wait_ge(dve_took, mod_at[g])
                for i in range(4):
                    c = 96 * (g // MG) + 2 * (4 * (g % MG) + i)
                    mm = pe.matmul(banks[:, 0, c:c + 2], mrow[g // MG][0:4, g % 2, P * i:P * i + P],
                                   K[0:4, C_PAIR:C_PAIR + 2], start=True, stop=True)
                mm.then_inc(mod_cols_done, 1)

            mod_at = {}

            def norm_transposes(n0, n):
                for i in range(n0, n0 + n):
                    pe.wait_ge(hn_ready, i + 1)
                    for half in range(2):
                        b = abank() if half and n0 < 12 else dbank()
                        for k in range(4):
                            mm = pe.transpose(b[:, P * k:P * k + P],
                                              hn[:, i % 2, P * (4 * half + k):P * (4 * half + k) + P], ident)
                    mm.then_inc(norm_tr, 1)

            def gate_broadcast(site, streams):
                for s in streams:
                    g = gates[0]
                    gates[0] += 1
                    pe.wait_ge(diag_ready, g + 1)
                    for half in range(2):
                        b = abank()
                        for k in range(4):
                            kk = 4 * half + k
                            mm = pe.matmul(b[:, P * k:P * k + P], ones, diagonal(site, s)[:, P * kk:P * kk + P],
                                           start=True, stop=True)
                    mm.then_inc(gate_mm, 1)

            gates = [0]

            pe.wait_ge(const_in, 16 * 10)
            b = dbank()
            pe.transpose(b[:, 0:85], rowsA[0:85, :], ident[0:85, 0:85])
            pe.transpose(b[:, 85:181], rowsB[0:96, :], ident[0:96, 0:96])
            b = dbank()
            pe.matmul(b[:, 0:384], ones[0:1, :], rowC[0:1, :], start=True, stop=True).then_inc(setup_pe, 1)
            pe.wait_ge(cv_ready, 1)
            for g in range(MG0 + 1):
                if g < MG0:
                    mod_rows(g)
                if g:
                    mod_cols(g - 1)
            norm_transposes(0, TILES)

            for n in range(3):
                bs = tiles_banks()
                for kh in range(2):
                    wh, wl = weights()
                    if n == 0:
                        pe.wait_ge(u_ready, TILES)
                    for k in range(4):
                        kk = 4 * kh + k
                        for tl in range(TILES):
                            mm = mm3(bs[tl][:, 0:480], uT_hi[:, kk, P * tl:P * tl + P], uT_lo[:, kk, P * tl:P * tl + P],
                                     wh[:, k, :], wl[:, k, :], kk == 0, kk == KD - 1)
                    mm.then_inc(weights_used, 1)

            for tl in range(TILES):
                pe.wait_ge(lat_scaled, tl + 1)
                b = dbank()
                for k in range(3):
                    pe.transpose(b[:, P * k:P * k + P], z[:, tl, P * k:P * k + P], ident)
                b = dbank()
                for k in range(2):
                    mm = pe.transpose(b[:, P * k:P * k + P], z[:, tl, Z_KV + P * k:Z_KV + P * k + P], ident)
                mm.then_inc(lat_tr, 1)
            for n in range(2):
                wh, wl = weights()
                bs = tiles_banks()
                for tl in range(TILES):
                    pe.wait_ge(lat_split, tl + 1)
                    for k in range(3):
                        mm = mm3(bs[tl][:, 0:384], uT_hi[:, k, P * tl:P * tl + P], uT_lo[:, k, P * tl:P * tl + P],
                                 wh[:, k, :], wl[:, k, :], k == 0, k == 2)
                mm.then_inc(weights_used, 1)
            wh, wl = weights()
            for tl in range(TILES):
                for n in range(2):
                    b = dbank() if tl < 2 else abank()
                    for k in range(2):
                        mm = mm3(b, uT_hi[:, 3 + k, P * tl:P * tl + P], uT_lo[:, 3 + k, P * tl:P * tl + P],
                                 wh[:, k, 512 * n:512 * n + 512], wl[:, k, 512 * n:512 * n + 512], k == 0, k == 1)
                    if (tl, n) != (3, 1):
                        mm.then_inc(ukv_mm, 1)
            mm.then_inc(weights_used, 1)

            def head_transposes(hd):
                b = abank()
                for tl in range(TILES):
                    src, w = (qa[:, tl, DQ * hd:DQ * hd + DQ], DQ) if hd < HEADS else \
                        (z[:, tl, Z_Q + GD * (hd - HEADS):Z_Q + GD * (hd - HEADS) + GD], GD)
                    mm = pe.transpose(b[0:w, P * tl:P * tl + P], src, ident)
                mm.then_inc(q_tr, 1)
                kt = k_turn(hd)
                if hd and kt == k_turn(hd - 1):
                    return
                b = dbank()
                for tl in range(TILES):
                    src, w = (ka[:, tl, DQ * hd:DQ * hd + DQ], DQ) if hd < HEADS else \
                        (z[:, tl, Z_K + GD * (kt - HEADS):Z_K + GD * (kt - HEADS) + GD], GD)
                    mm = pe.transpose(b[0:w, P * tl:P * tl + P], src, ident)
                mm.then_inc(k_tr, 1)

            def scores(n):
                hd, tl = ITEMS[n]
                w = DQ if hd < HEADS else GD
                if n % 4 == 0:
                    pe.wait_ge(q_sb, hd + 1)
                    pe.wait_ge(k_sb, k_turn(hd) + 1)
                b = abank()
                pe.matmul(b[:, 0:P * keys(tl)], qT[0:w, hd % 2, P * tl:P * tl + P],
                          kT[0:w, k_turn(hd) % 2, 0:P * keys(tl)], start=True, stop=True).then_inc(s_done, 1)

            def p_transposes(n):
                hd, tl = ITEMS[n]
                pe.wait_ge(pn_ready, n + 1)
                b = abank()
                for k in range(keys(tl)):
                    mm = pe.transpose(b[:, P * k:P * k + P], Pr[:, n % 4, P * k:P * k + P], ident)
                mm.then_inc(p_tr, 1)

            def pv(hd):
                pe.wait_ge(pt_sb, 4 * hd + 4)
                b = dbank()
                w = DV * (1 + hd % 2)
                for k in (0, 2, 3, 1):
                    if hd < HEADS:
                        v = va[:, k, DV * (hd + 1) - w:DV * (hd + 1)]
                    else:
                        end = Z_V + GD * (k_turn(hd) - HEADS + 1)
                        v = z[:, k, end - w:end]
                    if k < 2:
                        mm = pe.matmul(b[0:w, :].rearrange("p (a t) -> p a t", a=2), v, PT[:, hd % 2, k:k + 3:2, :],
                                       start=(k == 0), stop=(k == 1))
                    else:
                        pe.matmul(b[0:w, 256:512], v, PT[:, hd % 2, k + 2, :], start=False, stop=False)
                mm.then_inc(pv_done, 1)

            pe.wait_ge(rope_done, 1)
            pe.wait_ge(act_took, na[0])
            head_transposes(0)
            for n in range(NI + 3):
                if n < NI:
                    if n % 4 == 1 and n // 4 + 1 < HEADS + GQ:
                        head_transposes(n // 4 + 1)
                    scores(n)
                if 2 <= n < NI + 2:
                    p_transposes(n - 2)
                if n >= 6 and n % 4 == 2:
                    pv((n - 6) // 4)
                if mod_turn(n):
                    mod_rows(mod_turn(n))
                if mod_turn(n - 1):
                    if mod_turn(n - 1) == MG0:
                        pe.wait_ge(bank0_took, 1)
                    mod_cols(mod_turn(n - 1))

            def project(lh, ll, tiles, site, streams):
                turned = nd[0]
                for n in range(2):
                    bs = [dbank() for _ in tiles[:len(tiles) // 2]] + [abank() for _ in tiles[len(tiles) // 2:]]
                    for kh in range(2):
                        wh, wl = weights()
                        if site and n == 0 and kh == 0:
                            pe.wait_ge(dve_took, turned)
                        for k in range(4):
                            kk = 4 * kh + k
                            if not site and n == 0:
                                pe.wait_ge(o_split, kk + 1)
                            for i, tl in enumerate(tiles):
                                mm = mm3(bs[i], lh[:, kk, P * tl:P * tl + P], ll[:, kk, P * tl:P * tl + P],
                                         wh[:, k, :], wl[:, k, :], kk == 0, kk == KD - 1)
                        mm.then_inc(weights_used, 1)
                    if n == 0:
                        gate_broadcast(site, streams)

            project(uT_hi, uT_lo, range(4), 0, (0, 1))
            norm_transposes(4, TILES)

            pe.wait_ge(u_ready, 8)
            for j in range(NF // 2):
                for g in range(2):
                    wh, wl = weights()
                    for fc in range(2):
                        b = abank() if g == 0 else dbank()
                        for k in range(KD):
                            mm = mm3(b, wh[:, k, P * fc:P * fc + P], wl[:, k, P * fc:P * fc + P],
                                     uT_hi[:, k, :], uT_lo[:, k, :], k == 0, k == KD - 1)
                    mm.then_inc(weights_used, 1)
                if j == 0:
                    pe.wait_ge(bank0_took, 2)
                else:
                    mod_cols(MG + j - 1)
                mod_rows(MG + j)
            mod_cols(2 * MG - 2)
            mod_rows(2 * MG - 1)
            mod_cols(2 * MG - 1)
            n_hs = 0
            for n in range(2):
                bs = tiles_banks()
                for f0, m in DOWN:
                    wh, wl = weights()
                    for f in range(f0, f0 + m):
                        pe.wait_ge(hs_ready, n_hs + 1)
                        for tl in range(TILES):
                            cols = slice(P * tl, P * tl + P)
                            mm = mm3(bs[tl], hs[:, n_hs % 2, 0, cols], hs[:, n_hs % 2, 1, cols],
                                     wh[:, f - f0, :], wl[:, f - f0, :], f == 0, f == NF - 1)
                        n_hs += 1
                        mm.then_inc(weights_used if f == f0 + m - 1 else hs_used, 1)
                if n == 0:
                    gate_broadcast(1, (0, 1))
            norm_transposes(8, TILES)

            wh, wl = weights()
            pe.wait_ge(u_ready, 12)
            for dr in range(2):
                b = dbank()
                cols = slice(GRANK * dr, GRANK * dr + GRANK)
                for k in range(KD):
                    mm = mm3(b[0:GRANK, :], wh[:, k, cols], wl[:, k, cols], uT_hi[:, k, :], uT_lo[:, k, :],
                             k == 0, k == KD - 1)
            mm.then_inc(weights_used, 1)

            def gate_logits(i0):
                if i0 == 0:
                    pe.wait_ge(rt_sb, 2)
                    pe.wait_ge(late_in, 16 * 3)
                for i in range(i0, i0 + 4):
                    dr, tl = i // 4, i % 4
                    pe.matmul(dbank(), rT[0:GRANK + 1, dr, P * tl:P * tl + P], wg2[0:GRANK + 1, dr, :],
                              start=True, stop=True).then_inc(z2_mm, 1)

            for n in range(6):
                if n < 3:
                    bs = dict(zip(range(4), tiles_banks()))
                elif n == 3:
                    bs = {2: dbank(), 3: abank()}
                else:
                    bs = {2: abank(), 3: abank()}
                for kh in range(2):
                    wh, wl = weights()
                    for k in range(4):
                        kk = 4 * kh + k
                        for tl, b in bs.items():
                            cols = slice(P * tl, P * tl + P)
                            mm = mm3(b, uT_hi[:, kk, cols], uT_lo[:, kk, cols], wh[:, k, :], wl[:, k, :],
                                     kk == 0, kk == KD - 1)
                    mm.then_inc(weights_used, 1)
                if n < 2:
                    gate_logits(4 * n)
            proj_d, proj_a = nd[0], na[0]
            pe_at["gin"] = proj_a
            pe.wait_ge(act_took, proj_a)
            pe.wait_ge(dve_took, proj_d)
            for i in range(4):
                src = g_q if i < 2 else g_k
                b = dbank()
                for hh in range(2):
                    hd = 2 * (i % 2) + hh
                    for j in range(2):
                        tl = j if i < 2 else 2 + j
                        mm = pe.transpose(b[:, 256 * hh + P * j:256 * hh + P * j + P],
                                          src[:, tl, P * hd:P * hd + P], ident)
                mm.then_inc(gt_mm, 1)
            def cumulate(it):
                hd, dr = it // 2, it % 2
                b = dbank()
                for j in range(2):
                    mm = pe.matmul(b[:, 0:256], g_a[:, 2 + j, dr, P * hd:P * hd + P], tri[dr][:, j, :],
                                   start=(j == 0), stop=(j == 1))
                mm.then_inc(cum_mm, 1)

            pe.wait_ge(a_ready, 8)
            cumulate(0)
            cumulate(1)
            for dr in range(2):
                pe.wait_ge(a_ready, 4 * dr + 2)
                for s2 in range(2):
                    b = dbank()
                    for j in range(2):
                        mm = pe.matmul(b, tri[1 - dr][:, j, P * s2:P * s2 + P], g_a[:, j, dr, :],
                                       start=(j == 0), stop=(j == 1))
                mm.then_inc(tail_mm, 1)
            def gla_scores(it):
                hd, dr = it // 2, it % 2
                pe.wait_ge(dec_ready, it + 1)
                at_bank[it] = nd[0] + 1
                b = dbank()
                for n, (tt, j) in enumerate(BLOCKS[dr]):
                    for i in range(4 * tt, 4 * tt + 4):
                        at = kx_tile(dr, i, j)
                        mm = pe.matmul(b[:, P * n + 32 * (i % 4):P * n + 32 * (i % 4) + 32], g_KX[:, dr, at:at + P],
                                       g_qd[:, dr, 32 * i:32 * i + 32], start=True, stop=True)
                mm.then_inc(at_mm, 1)

            def context_states():
                for dr in range(2):
                    pe.wait_ge(ks_ready, dr + 1)
                    for hp in range(2):
                        b = abank()
                        for hh in range(2):
                            hd = 2 * hp + hh
                            for j in range(2):
                                mm = pe.matmul(b[:, 256 * hh:256 * hh + 256], g_a[:, j, dr, P * hd:P * hd + P],
                                               g_v[:, j, 256 * hd:256 * hd + 256], start=(j == 0), stop=(j == 1))
                        mm.then_inc(s0_mm, 1)

            def gla_out(hd):
                pe.wait_ge(dve_took, at_bank[2 * hd + 1])
                if hd == 0:
                    pe.wait_ge(act_took, na[0])
                b = abank()
                for tt in range(2):
                    o = b[:, 256 * tt:256 * tt + 256]
                    parts = []
                    for dr in range(2):
                        for n, (ta, j) in enumerate(BLOCKS[dr]):
                            if ta == tt:
                                parts.append((g_AT[:, hd % 2, dr, P * n:P * n + P],
                                              g_v[:, 2 + j, 256 * hd:256 * hd + 256]))
                        parts.append((g_qf[:, hd % 2, dr, P * tt:P * tt + P], g_S[:, dr, hd, :]))
                    for n, (l, r) in enumerate(parts):
                        mm = pe.matmul(o, l, r, start=(n == 0), stop=(n == len(parts) - 1))
                mm.then_inc(go_mm, 1)

            at_bank = {}
            pe.wait_ge(kx_zero, 1)
            for it in range(2 * GH):
                gla_scores(it)
                if it + 2 < 2 * GH:
                    cumulate(it + 2)
                if it == 1:
                    context_states()
                if it % 2 == 1:
                    gla_out(it // 2)
            for tt in range(2):
                pe.wait_ge(go_ready, 1)
                for half in range(2):
                    b = dbank()
                    for k in range(4):
                        mm = pe.transpose(b[:, P * k:P * k + P], g_o[:, tt, P * (4 * half + k):P * (4 * half + k) + P],
                                          ident)
                mm.then_inc(got_mm, 1)
            project(ug_hi, ug_lo, range(2), 2, (1,))
            norm_transposes(12, 2)

            for n in range(2):
                pe.wait_ge(uf_ready, n + 1)
                if n == 0:
                    pe.wait_ge(late_in, 16 * 6)
                    pe.wait_ge(bank0_took, 3)
                o = banks[:, 0, E_N * n:E_N * n + E_N]
                for k in range(KD):
                    pe.matmul(o, uf[:, P * k:P * k + P], wr[:, k, :], start=(k == 0), stop=False)
                pe.matmul(o, ones[0:1, :], brow[0:1, :], start=False, stop=True).then_inc(logit_mm, 1)
            pe.wait_ge(sel_ready, 1)
            for n in range(2):
                for j in range(2):
                    pe.matmul(banks[:, 0, E_N * n:E_N * n + E_N], tri[0][:, j, P * n:P * n + P], sel[:, j, :],
                              start=(j == 0), stop=(j == 1))
            for j in range(2):
                mm = pe.matmul(banks[:, 0, 16:24], ones, sel[:, j, :], start=(j == 0), stop=(j == 1))
            mm.then_inc(rank_mm, 1)

            pe.wait_ge(dve_took, nd[0])
            pe.wait_ge(act_took, na[0])
            pe.wait_ge(tab_ready, 1)

            def m_use(at, n):
                pe.wait_ge(m_took, at + (n - 1))
                return banks[:, 4 + n % 2, :]

            def gather(e1, at, g):
                if g == 0:
                    pe.wait_ge(prep_ready, e1 + 1)
                b = m_use(at, M_G + g)
                for i in range(2):
                    k = 2 * g + i
                    for j in range(2):
                        mm = pe.matmul(b[:, 256 * i:256 * i + 256], hn[:, j, P * k:P * k + P], Pm[:, j, :],
                                       start=(j == 0), stop=(j == 1))
                mm.then_inc(m_ready, 1)

            def scatter(T):
                for i in range(4):
                    tk, n = i // 2, i % 2
                    for tt in range(T):
                        mm = pe.matmul(banks[:, 4 + i, :], Wc[:, tt, P * tk:P * tk + P],
                                       y_e[:, tt, 512 * n:512 * n + 512], start=(tt == 0), stop=(tt == T - 1))
                    mm.then_inc(m_ready, 1)

            pe.sem_inc(m_ready, M_G)
            for g in range(4):
                gather(0, 0, g)
            pe.wait_ge(m_ready, M_G + 4)
            pe.sem_inc(m_ready, M_ALL - M_G - 4)
            with pe.Fori(0, E_N) as e:
                ms = e * M_ALL + M_ALL

                def e_half(u, half):
                    s = N_PRE + u
                    pe.wait_ge(hi_ready, e * (2 * PER_E) + (2 * s + half + 1))
                    pe.wait_ge(lo_ready[half], e * PER_E + (s + 1))

                def e_weights(u):
                    s = N_PRE + u
                    k = 4 if u < 4 * EJ else 2
                    return [w[:, s % SPLIT_N, :].rearrange("p (k n) -> p k n", k=k) for w in (w_hi, w_lo)]

                def expert(T):
                    def h_transposes(j):
                        pe.wait_ge(gu_took, e * EJ + (j + 2))
                        for tt in range(T):
                            b = m_use(ms, M_H + T * j + tt)
                            for i in range(4):
                                mm = pe.transpose(b[:, P * i:P * i + P], e_h[:, h_at(T, j, tt), P * i:P * i + P],
                                                  ident)
                            mm.then_inc(m_ready, 1)

                    for j in range(EJ):
                        pe.wait_ge(gu_took, e * EJ + gu_free(T, j))
                        for g in range(2):
                            for kh in range(2):
                                u = 4 * j + 2 * g + kh
                                wh, wl = e_weights(u)
                                for k in range(4):
                                    if k % 2 == 0:
                                        e_half(u, k // 2)
                                    kk = 4 * kh + k
                                    for tt in range(T):
                                        mm = mm3(banks[:, 2 * h_at(T, j, tt) + g, :], ug_hi[:, kk, P * tt:P * tt + P],
                                                 ug_lo[:, kk, P * tt:P * tt + P], wh[:, k, :], wl[:, k, :],
                                                 kk == 0, kk == KD - 1)
                                mm.then_inc(weights_used, 1)
                        if j:
                            h_transposes(j - 1)
                        else:
                            b = m_use(ms, M_W)
                            for s2 in range(2):
                                for jj in range(2):
                                    mm = pe.transpose(b[:, 256 * s2 + P * jj:256 * s2 + P * jj + P],
                                                      Pc[:, jj, P * s2:P * s2 + P], ident)
                            mm.then_inc(m_ready, 1)
                    if T == 2:
                        pe.wait_ge(gu_took, e * EJ + (EJ + 1))
                    for u in range(4 * EJ, PER_E):
                        if u == LAST_H:
                            h_transposes(EJ - 1)
                            if T == 1:
                                pe.wait_ge(m_ready, ms + (M_H + EJ))
                                pe.sem_inc(m_ready, EJ)
                        if u in GATHERS:
                            gather(e + 1, ms, GATHERS.index(u))
                        wh, wl = e_weights(u)
                        for i in range(2):
                            e_half(u, i)
                            f = 2 * (u - 4 * EJ) + i
                            if f % 4 == 0:
                                pe.wait_ge(m_took, ms + (M_H + T * (f // 4 + 1)))
                            for tt in range(T):
                                for n in range(2):
                                    bk = 6 + n if tt == 0 else n
                                    mm = mm3(banks[:, bk, :], eT_hi[:, f, P * tt:P * tt + P],
                                             eT_lo[:, f, P * tt:P * tt + P],
                                             wh[:, i, 512 * n:512 * n + 512], wl[:, i, 512 * n:512 * n + 512],
                                             f == 0, f == EF - 1)
                        mm.then_inc(weights_used, 1)

                pe.wait_ge(y_took_a, e + 1)
                pe.wait_ge(y_took_d, e + 1)
                pe.wait_ge(m_took, ms)
                before = pe.value_load(cnt[0:1, bass.ds(e, 1)], min_val=0, max_val=2 * P)
                with pe.If(before > P):
                    scatter(2)
                with pe.Else():
                    scatter(1)
                pe.wait_ge(ug_ready, e + 1)
                chosen = pe.value_load(cnt[0:1, bass.ds(e + 1, 1)], min_val=0, max_val=2 * P)
                with pe.If(chosen > P):
                    expert(2)
                with pe.Else():
                    expert(1)
                pe.wait_ge(m_ready, ms + (M_ALL - 1))
                pe.sem_inc(m_ready, 1)
            pe.wait_ge(y_took_a, E_N + 1)
            pe.wait_ge(y_took_d, E_N + 1)
            scatter(2)
            pe.wait_ge(m_took, (E_N + 1) * M_ALL + 4)
            gate_broadcast(3, (1,))

        dve_at = {}

        @block.vector
        def _(dve):
            nd, steps, nsplit, nr = [0], [0], [0], [0]

            def chain(ins):
                ins.then_inc(dve_step, 1)
                steps[0] += 1
                dve.wait_ge(dve_step, steps[0])

            def dsrc():
                nd[0] += 1
                return d_bank(nd[0] - 1)

            def took(ins, then=False):
                ins.then_inc(dve_took, 1)
                if then:
                    dve.wait_ge(dve_took, nd[0])

            def split_to(n):
                while nsplit[0] < min(n, N_PRE):
                    s = nsplit[0]
                    nsplit[0] += 1
                    if s >= SPLIT_N:
                        dve.wait_ge(weights_used, s - SPLIT_N + 1)
                    for half, (a, b) in enumerate(halves(units[s][1])):
                        c = slice(units[s][2] * a, units[s][2] * b)
                        r = slice(HALF * half, HALF * half + units[s][2] * (b - a))
                        dve.wait_ge(hi_ready, 2 * s + half + 1)
                        dve.wait_ge(raw_in[s % RAW_N][half], 16 * (s // RAW_N + 1))
                        dve.tensor_tensor(w_lo[:, s % SPLIT_N, c], raw[:, s % RAW_N, r],
                                          w_hi[:, s % SPLIT_N, c].bitcast(F32), ALU.subtract)\
                            .then_inc(lo_ready[half], 1)

            def after(name, n):
                split_to(ahead_of(name, n))
                dve.wait_ge(weights_used, used(name, n))

            def rstd(groups, n):
                nr[0] += 1
                dve.wait_ge(ss_ready, nr[0])
                for cols, width in groups:
                    ins = dve.tensor_scalar(cols(ST_VAR), cols(ST_SUM), 1.0 / width, EPS, ALU.mult, ALU.add)
                ins.then_inc(var_ready, 1)
                dve.wait_ge(sqrt_ready, nr[0])
                v, y, t = st[:, ST_VAR, 0:n], st[:, ST_R, 0:n], st[:, ST_T, 0:n]
                chain(dve.reciprocal(y, y))
                chain(dve.tensor_tensor(t, v, y, ALU.mult))
                chain(dve.tensor_tensor(t, t, y, ALU.mult))
                chain(dve.tensor_scalar(t, t, -0.5, 1.5, ALU.mult, ALU.add))
                dve.tensor_tensor(y, y, t, ALU.mult).then_inc(rstd_ready, 1)
                dve.wait_ge(rstd_ready, nr[0])

            def mod_rows_out(g):
                if g < MG0:
                    after("mod0a", 2 * g + 2)
                elif g < MG:
                    after("mods", 2 * (g - MG0) + 2)
                else:
                    after("gu", 4 * (g - MG) + (4 if g < 2 * MG - 1 else 2))
                if g >= 2:
                    dve.wait_ge(mod_cols_done, g - 1)
                took(dve.tensor_copy(mrow[g // MG][0:4, g % 2, :], dsrc()[0:4, :]))

            def mod_columns(layer, f0, f1, groups):
                dve.wait_ge(mod_cols_done, groups)
                m = modT[:, layer, f0:f1, :]
                b = vecs[:, 85 + 48 * layer + f0:85 + 48 * layer + f1].unsqueeze(2)
                cols = banks[:, 0, 96 * layer + 2 * f0:96 * layer + 2 * f1]
                dve.tensor_tensor(m, cols.rearrange("p (f s) -> p f s", s=2),
                                  wide(b, [f1 - f0, 2]), ALU.add).then_inc(bank0_took, 1)
                mods_n[0] += 1
                dve.wait_ge(bank0_took, mods_n[0])

            mods_n = [0]

            def gain(layer, i):
                c0 = 16 + (4 * layer + i) * KD
                return wide(vecs[:, c0:c0 + KD].unsqueeze(2), [KD, 2])

            def scale_site(layer, which):
                f = 24 * which + 8
                a = Am[:, 2 * layer + which]
                chain(dve.tensor_scalar(a, modT[:, layer, f:f + KD, :], 1.0, None, ALU.add))
                chain(dve.tensor_tensor(a, a, gain(layer, 2 * which), ALU.mult))

            def gate_site(layer, which, inc):
                f = 24 * which + 16
                g = dve.tensor_tensor(Gm[:, 2 * layer + which], modT[:, layer, f:f + KD, :],
                                      gain(layer, 2 * which + 1), ALU.mult)
                if inc:
                    g.then_inc(mods_ready, 1)

            def modulate(layer, which, n0):
                def low(i):
                    cols = slice(P * i, P * i + P)
                    dve.wait_ge(u_high, n0 + i + 1)
                    dve.tensor_tensor(uT_lo[:, :, cols], ub[i % 2][:, :].rearrange("p (k t) -> p k t", k=KD),
                                      uT_hi[:, :, cols].bitcast(F32), ALU.subtract).then_inc(u_ready, 1)

                for i in range(TILES):
                    s = 1 if i in LAT else 0
                    dve.wait_ge(norm_tr, n0 + i + 1)
                    if i >= 2:
                        dve.wait_ge(u_ready, n0 + i - 1)
                    u3 = ub[i % 2][:, 0:512].rearrange("p (k t) -> p k t", k=4)
                    b = dsrc().rearrange("p (k t) -> p k t", k=4)
                    took(dve.tensor_tensor(u3, b, wide(Am[:, 2 * layer + which, 0:4, s:s + 1], [4, P]), ALU.mult),
                         then=True)
                    dve.tensor_tensor(u3, u3, wide(shift_of(layer, which)[:, 0:4, s:s + 1], [4, P]),
                                      ALU.add).then_inc(u_half, 1)
                    if i:
                        low(i - 1)
                low(TILES - 1)
                dve.wait_ge(u_ready, n0 + TILES)

            def modulate_router():
                u3 = uf[:, :].rearrange("p (k t) -> p k t", k=KD)
                for i in range(2):
                    dve.wait_ge(norm_tr, 12 + i + 1)
                    if i:
                        dve.wait_ge(logit_mm, i)
                    for half in range(2):
                        b = dsrc().rearrange("p (k t) -> p k t", k=4)
                        a = Am[:, 3, 4 * half:4 * half + 4, 1:2]
                        took(dve.tensor_tensor(u3[:, 4 * half:4 * half + 4, :], b, wide(a, [4, P]), ALU.mult),
                             then=(half == 1))
                    dve.tensor_tensor(u3, u3, wide(shift_of(1, 1)[:, :, 1:2], [KD, P]), ALU.add).then_inc(uf_ready, 1)

            def residual(y, tiles, site, gr):
                rstd([(lambda k: st[:, k, 0:len(tiles)], D)], len(tiles))
                dve.wait_ge(gate_rows, gr)
                for i, tl in enumerate(tiles):
                    s = 1 if tl in LAT else 0
                    chain(dve.scalar_tensor_tensor(y[:, i, :], y[:, i, :], st[:, ST_R, i:i + 1], Gb[:, s, :],
                                                   ALU.mult, ALU.mult))
                    dve.tensor_tensor(h[:, tl, :], h[:, tl, :], y[:, i, :], ALU.add).then_inc(h_new, 1)

            def split_banks(hi, lo):
                b = dsrc().rearrange("p (k t) -> p k t", k=4)
                chain(dve.tensor_copy(hi, b))
                took(dve.tensor_tensor(lo, b, hi.bitcast(F32), ALU.subtract))

            dve.wait_ge(setup_pe, 1)
            took(dve.tensor_copy(vecs[:, :], dsrc()[:, 0:181]))
            took(dve.tensor_copy(bc[:, :], dsrc()[:, 0:384]))
            dve.wait_ge(dve_took, 2)
            dve.wait_ge(c_silu, 1)
            dve.tensor_tensor(cv[:, :, 2:4], vecs[:, 0:16].rearrange("p (s k) -> p k s", k=KD),
                              cv[:, :, 0:2].bitcast(F32), ALU.subtract).then_inc(cv_ready, 1)
            split_to(2)
            rstd([(lambda k: st[:, k, 0:TILES], D)], TILES)
            for g in range(MG0):
                mod_rows_out(g)
            mod_columns(0, 0, 16, MG0)
            scale_site(0, 0)
            modulate(0, 0, 0)

            for n in range(3):
                after("z", 2 * n + 2)
                for tl in range(2):
                    took(dve.tensor_copy(z[:, tl, 480 * n:480 * n + 480], dsrc()[:, 0:480]))
            dve_at["z"] = nd[0]
            dve.wait_ge(dve_took, nd[0])
            dve.wait_ge(act_took, TILES + 6)
            for tl in range(TILES):
                q10 = z[:, tl, Z_Q:Z_V]
                chain(dve.tensor_tensor(uf[:, 0:640], q10, q10, ALU.mult))
                chain(dve.reduce_sum(st[:, ST_SUM, 12 * tl + 2:12 * tl + 12],
                                     uf[:, 0:640].rearrange("p (h d) -> p h d", d=GD), AX.X))

            def sums(a, b):
                return lambda k: st[:, k, :].rearrange("p (t c) -> p t c", c=12)[:, :, a:b]

            rstd([(sums(0, 1), Q_RANK), (sums(1, 2), KV_RANK), (sums(2, 12), GD)], 48)
            r12 = st[:, ST_R, :].rearrange("p (t c) -> p t c", c=12)
            heads_n = {}

            def norm_heads(tl):
                q10 = z[:, tl, Z_Q:Z_V].rearrange("p (h d) -> p h d", d=GD)
                chain(dve.tensor_tensor(q10, q10, wide(r12[:, tl, 2:12].unsqueeze(2), [10, GD]), ALU.mult))
                dve.tensor_tensor(q10[:, 0:GQ], q10[:, 0:GQ], wide(bc[:, 0:GD].unsqueeze(1), [GQ, GD]), ALU.mult)
                chain(dve.tensor_tensor(q10[:, GQ:10], q10[:, GQ:10], wide(bc[:, GD:2 * GD].unsqueeze(1), [GKV, GD]),
                                        ALU.mult))

            def lat_parts(tl):
                dve.wait_ge(lat_tr, tl + 1)
                cols = slice(P * tl, P * tl + P)
                u5 = uf[:, 0:640].rearrange("p (k t) -> p k t", k=5)
                for a, b in ((0, 3), (3, 5)):
                    bank = dsrc()[:, 0:P * (b - a)].rearrange("p (k t) -> p k t", k=b - a)
                    g = wide(vecs[:, 80 + a:80 + b].unsqueeze(2), [b - a, P])
                    took(dve.tensor_tensor(u5[:, a:b, :], bank, g, ALU.mult), then=(a == 3))
                chain(dve.tensor_copy(uT_hi[:, 0:5, cols], u5))
                dve.tensor_tensor(uT_lo[:, 0:5, cols], u5, uT_hi[:, 0:5, cols].bitcast(F32),
                                  ALU.subtract).then_inc(lat_split, 1)
                dve.wait_ge(lat_split, tl + 1)

            def rotate(v, heads, tl, n):
                c0 = 0 if n == 16 else 64
                tb = rope[:, tl - 2, c0:c0 + 4 * n].rearrange("p (f a n) -> p f a n", f=2, a=2)
                cos, sin = (wide(tb[:, i].unsqueeze(1), [heads, 2, n]) for i in range(2))
                x1, x2 = v[:, :, :, 0, :], v[:, :, :, 1, :]
                m = heads * 2 * n
                t1, t2, t3 = (uf[:, i * m:i * m + m].rearrange("p (h a n) -> p h a n", h=heads, a=2) for i in range(3))
                dve.tensor_tensor(t1, x1, cos, ALU.mult)
                chain(dve.tensor_tensor(t2, x2, sin, ALU.mult))
                dve.tensor_tensor(t3, x2, cos, ALU.mult)
                chain(dve.tensor_tensor(t1, t1, t2, ALU.subtract))
                chain(dve.tensor_tensor(t2, x1, sin, ALU.mult))
                chain(dve.tensor_tensor(x2, t3, t2, ALU.add))
                chain(dve.tensor_copy(x1, t1))

            def five(v, heads, n):
                return v.rearrange("p (h a x n) -> p h a x n", h=heads, a=2, x=2)

            split_to(used("uq", 0) + 2)
            for tl in range(TILES):
                lat_parts(tl)
            split_to(used("ukv", 1))
            for tl in range(TILES):
                norm_heads(tl)
                if tl in LAT:
                    rotate(five(z[:, tl, Z_Q:Z_V], 10, 16), 10, tl, 16)
                    rotate(five(z[:, tl, Z_ROPE:Z_Q], 1, 8), 1, tl, 8)
            for n in range(2):
                after("uq", n + 1)
                for tl in range(2):
                    took(dve.tensor_copy(qa[:, tl, 384 * n:384 * n + 384], dsrc()[:, 0:384]))
            split_to(used("mods", 0) + 2)

            def kv_out(tl, n, b, copy):
                b = b.rearrange("p (h c) -> p h c", c=P)
                k8 = ka[:, tl, :].rearrange("p (h c) -> p h c", c=DQ)[:, 4 * n:4 * n + 4, 0:NOPE]
                v8 = va[:, tl, 256 * n:256 * n + 256].rearrange("p (h c) -> p h c", c=DV)
                copy(k8, b[:, :, 0:NOPE])
                return copy(v8, b[:, :, NOPE:P])

            for tl in range(2):
                for n in range(2):
                    dve.wait_ge(ukv_mm, 2 * tl + n + 1)
                    took(kv_out(tl, n, dsrc(), dve.tensor_copy))
            for tl in range(TILES):
                k8 = ka[:, tl, :].rearrange("p (h c) -> p h c", c=DQ)[:, :, NOPE:DQ]
                dve.tensor_copy(k8, wide(z[:, tl, Z_ROPE:Z_Q].unsqueeze(1), [HEADS, ROPE_M]))
            dve.wait_ge(act_took, TILES + 10)
            for tl in LAT:
                q96 = qa[:, tl, :].rearrange("p (h c) -> p h c", c=DQ)[:, :, NOPE:DQ]
                rotate(q96.rearrange("p h (a x n) -> p h a x n", a=2, x=2), HEADS, tl, 8)
            dve.wait_ge(dve_took, nd[0])
            dve.sem_inc(rope_done, 1)

            score_bank = []
            a = TILES + 15
            for n in range(NI + 3):
                a += n < NI and n % 4 == 1 and n // 4 + 1 < HEADS + GQ
                score_bank.append(a)
                a += (n < NI) + (2 <= n < NI + 2)

            def k_out(hd):
                kt = k_turn(hd)
                if hd and kt == k_turn(hd - 1):
                    return
                w = DQ if hd < HEADS else GD
                dve.wait_ge(k_tr, kt + 1)
                k_n[0] += 1
                took(dve.tensor_copy(kT[0:w, kt % 2, :], dsrc()[0:w, :]), then=True)
                dve.sem_inc(k_sb, 1)

            k_n = [0]
            mxs, nbs, sms, ris = (sm[:, 8 * i:8 * i + 8] for i in range(4))
            k_out(0)
            for n in range(NI + 3):
                if n < NI and n % 4 == 1 and n // 4 + 1 < HEADS + GQ:
                    hd1 = n // 4 + 1
                    dve.wait_ge(s_done, n)
                    k_out(hd1)
                if n < NI:
                    hd, tl = ITEMS[n]
                    scale = float(DQ if hd < HEADS else GD) ** -0.5
                    c = n % 8
                    dve.wait_ge(s_done, n + 1)
                    chain(dve.reduce_max(mxs[:, c:c + 1], a_bank(score_bank[n])[:, 0:P * keys(tl)], AX.X))
                    dve.tensor_scalar(nbs[:, c:c + 1], mxs[:, c:c + 1], -scale, None, ALU.mult).then_inc(nb_ready, 1)
                if 1 <= n <= NI:
                    w = P * keys(ITEMS[n - 1][1])
                    c = (n - 1) % 8
                    p = Pr[:, (n - 1) % 4, 0:w]
                    dve.wait_ge(exp_done, n)
                    chain(dve.reciprocal(ris[:, c:c + 1], sms[:, c:c + 1]))
                    dve.tensor_scalar(p, p, ris[:, c:c + 1], None, ALU.mult).then_inc(pn_ready, 1)
                if n >= 6 and n % 4 == 2:
                    hd = (n - 6) // 4
                    dve.wait_ge(pv_done, hd + 1)
                    took(dve.tensor_copy(oT(hd // 2)[o_rows(hd), :], dsrc()[o_rows(hd), :]))
                if mod_turn(n):
                    mod_rows_out(mod_turn(n))
            attn_d = nd[0]
            dve_at["attention"] = attn_d
            mod_columns(0, 16, 48, MG)
            scale_site(0, 1)
            gate_site(0, 0, False)
            gate_site(0, 1, True)
            split_to(used("wo", 0) + 2)
            for kk in range(KD):
                dve.wait_ge(o_hi, kk + 1)
                dve.tensor_tensor(uT_lo[:, kk, :], oT(kk), uT_hi[:, kk, :].bitcast(F32),
                                  ALU.subtract).then_inc(o_split, 1)

            def project_out(name, y, tiles):
                for n in range(2):
                    after(name, 2 * n + 2)
                    for tl in tiles:
                        took(dve.tensor_copy(y[:, tl, 512 * n:512 * n + 512], dsrc()), then=(n == 1))
                dve_at[name] = nd[0]

            project_out("wo", y_attn, (0, 1))
            residual(y_attn, range(TILES), 0, 2)
            rstd([(lambda k: st[:, k, 0:TILES], D)], TILES)
            split_to(used("gu", 0) + 2)
            modulate(0, 1, 4)

            dve_at["ffn"] = nd[0]
            for j in range(NF // 2):
                after("gu", 4 * j + 2)
                for fc in range(2):
                    f = 2 * j + fc
                    dve.wait_ge(silu_ready, f + 1)
                    took(dve.tensor_tensor(hT[:, f, :], sil[:, f % 2, :], dsrc(), ALU.mult))
                mod_rows_out(MG + j)
                if j == NF // 2 - 1:
                    mod_rows_out(MG + j + 1)
            dve.wait_ge(dve_took, nd[0])
            n_hs, hs_n = 0, 0
            freed = []
            for n in range(2):
                for d, (f0, m) in enumerate(DOWN):
                    split_to(ahead_of("down", n * len(DOWN) + d))
                    for f in range(f0, f0 + m):
                        if n_hs >= 2:
                            dve.wait_ge(*freed[n_hs - 2])
                        chain(dve.tensor_copy(hs[:, n_hs % 2, 0, :], hT[:, f, :]))
                        dve.tensor_tensor(hs[:, n_hs % 2, 1, :], hT[:, f, :], hs[:, n_hs % 2, 0, :].bitcast(F32),
                                          ALU.subtract).then_inc(hs_ready, 1)
                        n_hs += 1
                        if f == f0 + m - 1:
                            freed.append((weights_used, used("down", n * len(DOWN) + d + 1)))
                        else:
                            hs_n += 1
                            freed.append((hs_used, hs_n))
                after("down", (n + 1) * len(DOWN))
                for tl in range(2):
                    took(dve.tensor_copy(y_ffn[:, tl, 512 * n:512 * n + 512], dsrc()), then=(n == 1))
            dve_at["down"] = nd[0]
            residual(y_ffn, range(TILES), 1, 4)
            mod_columns(1, 0, 48, 2 * MG)
            scale_site(1, 0)
            scale_site(1, 1)
            gate_site(1, 0, False)
            gate_site(1, 1, True)
            rstd([(lambda k: st[:, k, 0:TILES], D)], TILES)
            split_to(used("gin", 0) + 2)
            modulate(1, 0, 8)

            after("gin", 1)
            dve.wait_ge(rt_one, 1)
            for dr in range(2):
                took(dve.tensor_copy(rT[0:GRANK, dr, :], dsrc()[0:GRANK, :]), then=True)
                dve.sem_inc(rt_sb, 1)

            def gate_out(i):
                dr, tl = i // 4, i % 4
                dve.wait_ge(z2_mm, i + 1)
                b = dsrc()
                a = g_a[:, tl, dr, :]
                chain(dve.tensor_scalar(a, b, 0.0, None, ALU.min))
                took(dve.scalar_tensor_tensor(ebuf[:, i % 4, :], a, 2.0, b, ALU.mult, ALU.subtract))
                dve_at["gate", i] = nd[0]

            def log_decay(i):
                dr, tl = i // 4, i % 4
                dve.wait_ge(e_ln, i + 1)
                dve.tensor_tensor(g_a[:, tl, dr, :], g_a[:, tl, dr, :], ebuf[:, i % 4, :],
                                  ALU.subtract).then_inc(a_ready, 1)

            for n, (dst, c0) in enumerate(((g_k, 0), (g_v, 0), (g_v, 512))):
                after("gin", 2 * n + 3)
                for tl in range(2):
                    took(dve.tensor_copy(dst[:, tl, c0:c0 + 512], dsrc()))
                if n:
                    for i in range(4 * n - 4, 4 * n):
                        log_decay(i)
                    dve.wait_ge(a_ready, 4 * n)
                if n < 2:
                    for i in range(4 * n, 4 * n + 4):
                        gate_out(i)
            after("gin", 9)
            took(dve.tensor_copy(g_q[:, 0, :], dsrc()))
            after("gin", 13)
            dve.wait_ge(act_took, pe_at["gin"])
            g8 = g_g[:, :, :].rearrange("p j (h v) -> p (j h) v", v=GDV)
            dve.tensor_tensor(g8, g8, wide(bc[:, 128:384].unsqueeze(1), [2 * GH, GDV]), ALU.mult)
            for i in range(4):
                dve.wait_ge(gt_mm, i + 1)
                dst = (g_qT if i < 2 else g_kT)[:, 2 * (i % 2):2 * (i % 2) + 2, :]
                b = dsrc().rearrange("p (h t) -> p h t", h=2)
                took(dve.tensor_scalar(dst, b, float(GDK) ** -0.5 if i < 2 else 1.0, None, ALU.mult))
            bt_set = dve.memset(bt[:, :, :, :], 0.0)
            chain(bt_set)

            def cum_out(it):
                dr = it % 2
                dve.wait_ge(cum_mm, it + 1)
                took(dve.tensor_copy(g_C[:, dr, :], dsrc()[:, 0:256]), then=True)
                if dr == 0:
                    chain(dve.tensor_copy(bt[:, 0, 0, 1:8], g_C[:, 0, 31:224:32]))
                else:
                    chain(dve.tensor_copy(bt[:, 1, 0, 0:7], g_C[:, 1, 32:225:32]))
                dve.tensor_scalar(bt[:, dr, 1, :], bt[:, dr, 0, :], 1.0 / 16, None, ALU.mult)
                dve.tensor_tensor(g_qd[:, dr, :].rearrange("p (i t) -> p i t", i=8),
                                  g_C[:, dr, :].rearrange("p (i t) -> p i t", i=8),
                                  wide(bt[:, dr, 0, :].unsqueeze(2), [8, CHUNK]), ALU.subtract).then_inc(cum_sb, 1)

            def decayed(it):
                hd, dr = it // 2, it % 2
                dve.wait_ge(dec_exp, it + 1)
                if hd >= 2:
                    dve.wait_ge(go_mm, hd - 1)
                dve.tensor_tensor(g_qd[:, dr, :], g_qd[:, dr, :], g_qT[:, hd, :], ALU.mult)
                dve.tensor_tensor(g_qf[:, hd % 2, dr, :], g_qf[:, hd % 2, dr, :], g_qT[:, hd, :], ALU.mult)
                for i in range(8):
                    at, a, b = kx(dr, i)
                    c0 = at + a
                    s0 = a + (128 if dr == 1 and i >= 4 else 0)
                    ins = dve.tensor_tensor(g_KX[:, dr, c0:at + b], g_KX[:, dr, c0:at + b],
                                            g_kT[:, hd, s0:s0 + b - a], ALU.mult)
                ins.then_inc(dec_ready, 1)

            cum_out(0)
            cum_out(1)
            for dr in range(2):
                dve.wait_ge(tail_mm, dr + 1)
                for s2 in range(2):
                    took(dve.tensor_tensor(g_a[:, s2, dr, :], dsrc(), g_a[:, s2, dr, :], ALU.subtract))
                dve_at["tail", dr] = nd[0]
            for dr in range(2):
                dve.wait_ge(tail_exp, dr + 1)
                dve.tensor_tensor(g_a[:, 0:2, dr, :], g_a[:, 0:2, dr, :], g_k[:, 0:2, :],
                                  ALU.mult).then_inc(ks_ready, 1)
            decayed(0)
            for it in range(2 * GH):
                if it + 1 < 2 * GH:
                    decayed(it + 1)
                hd, dr = it // 2, it % 2
                dve.wait_ge(at_mm, it + 1)
                took(dve.tensor_tensor(g_AT[:, hd % 2, dr, :], dsrc()[:, 0:384], mask[:, dr, :], ALU.mult))
                if it + 2 < 2 * GH:
                    cum_out(it + 2)
            dve_at["gla masks"] = nd[0]
            rstd([(lambda k: st[:, k, 0:8], GDV)], 8)
            o8 = g_o[:, :, :].rearrange("p j (h v) -> p (j h) v", v=GDV)
            chain(dve.tensor_tensor(o8, o8, wide(st[:, ST_R, 0:8].unsqueeze(2), [8, GDV]), ALU.mult))
            dve.tensor_tensor(g_o[:, :, :], g_o[:, :, :], g_g[:, :, :], ALU.mult).then_inc(go_ready, 1)
            for tt in range(2):
                dve.wait_ge(got_mm, tt + 1)
                cols = slice(P * tt, P * tt + P)
                for half in range(2):
                    split_banks(ug_hi[:, 4 * half:4 * half + 4, cols], ug_lo[:, 4 * half:4 * half + 4, cols])
            dve.memset(y_acc[:, :, :], 0.0)
            dve.memset(cnt[:, 0:1], 0)
            dve.memset(Wc[:, :, :], 0.0)
            chain(dve.memset(tab[:, :], 0.0))
            project_out("gout", y_gla, (0,))
            residual(y_gla, LAT, 2, 5)
            rstd([(lambda k: st[:, k, 0:2], D)], 2)
            modulate_router()

            r8 = [2, E_N]
            dve.wait_ge(logit_mm, 2)
            lg_ps = banks[:, 0, 0:16].rearrange("p (t e) -> p t e", t=2)
            chain(dve.reduce_max(mx, lg_ps, AX.X))
            dve.tensor_tensor(lg, lg_ps, wide(mx.unsqueeze(2), r8), ALU.subtract).then_inc(lg_ready, 1)
            dve.wait_ge(lg_exp, 1)
            chain(dve.reduce_sum(zs, lg, AX.X))
            chain(dve.reciprocal(zs, zs))
            chain(dve.tensor_tensor(pb_, lg, wide(zs.unsqueeze(2), r8), ALU.mult))

            def first_max(src, top, found):
                chain(dve.reduce_max(top, src, AX.X))
                chain(dve.tensor_tensor(eq, src, wide(top.unsqueeze(2), r8), ALU.is_equal))
                for n in range(2):
                    ins = dve.tensor_tensor_scan(cs[:, n, :], ones[:, 0:E_N], eq[:, n, :], 0.0, ALU.mult, ALU.add)
                chain(ins)
                chain(dve.scalar_tensor_tensor(found, cs, 1.0, eq, ALU.is_equal, ALU.mult))

            first_max(pb_, mx, f1)
            chain(dve.scalar_tensor_tensor(lg, f1, -2.0, pb_, ALU.mult, ALU.add))
            first_max(lg, mx2, f2)
            dve.tensor_tensor(sel, f1, f2, ALU.add).then_inc(sel_ready, 1)
            dve.wait_ge(sel_ready, 1)
            chain(dve.tensor_tensor(mx, mx, mx2, ALU.add))
            chain(dve.reciprocal(mx, mx))
            chain(dve.tensor_tensor(cw, pb_, sel, ALU.mult))
            chain(dve.tensor_tensor(cw, cw, wide(mx.unsqueeze(2), r8), ALU.mult))
            dve.memset(y_e[:, :, :], 0.0)
            dve.wait_ge(rank_mm, 1)
            t6 = tab[:, :].rearrange("p (e c) -> p c e", c=6)[:, :, 0:E_N]
            chain(dve.tensor_scalar(t6[:, 0:2, :], banks[:, 0, 0:16].rearrange("p (t e) -> p t e", t=2), -1.0, None,
                                    ALU.add))
            chain(dve.tensor_copy(t6[:, 2:4, :], sel))
            chain(dve.tensor_copy(cnt[:, 1:1 + E_N], banks[:, 0, 16:24]))
            dve.tensor_copy(t6[:, 4:6, :], cw).then_inc(tab_ready, 1)
            dve.wait_ge(tab_ready, 1)


            def m_src(at, n):
                dve.wait_ge(m_ready, at + (n + 1))
                return banks[:, 4 + n % 2, :]

            def prepare(e1):
                chain(dve.tensor_copy(ecol[:, 0:6], tab[:, bass.ds(e1 * 6, 6)]))
                for j in range(2):
                    dve.tensor_scalar(Pm[:, j, :], iota[:, :], ecol[:, j:j + 1], ecol[:, 2 + j:3 + j],
                                      ALU.is_equal, ALU.mult)
                    ins = dve.tensor_scalar(Pc[:, j, :], iota[:, :], ecol[:, j:j + 1], ecol[:, 4 + j:5 + j],
                                            ALU.is_equal, ALU.mult)
                ins.then_inc(prep_ready, 1)

            def gather_out(at, n_ready, gs):
                for g in gs:
                    b = m_src(at, M_G + g).rearrange("p (k t) -> p k t", k=2)
                    k0 = 2 * g
                    u = uf[:, 0:512].rearrange("p (k t) -> p k t", k=2)
                    ins = dve.tensor_tensor(u, b, wide(Am[:, 3, k0:k0 + 2, 1:2], [2, 2 * P]), ALU.mult)
                    ins.then_inc(m_took, 1)
                    dve.wait_ge(m_took, at + (M_G + g + 1))
                    chain(dve.tensor_tensor(u, u, wide(shift_of(1, 1)[:, k0:k0 + 2, 1:2], [2, 2 * P]), ALU.add))
                    hi = ug_hi[:, k0:k0 + 2, :]
                    chain(dve.tensor_copy(hi, u))
                    ins = dve.tensor_tensor(ug_lo[:, k0:k0 + 2, :], u, hi.bitcast(F32), ALU.subtract)
                    if g < 3:
                        chain(ins)
                    else:
                        ins.then_inc(ug_ready, 1)
                        dve.wait_ge(ug_ready, n_ready)

            def scatter_out(at):
                for i in range(4):
                    tk, n = i // 2, i % 2
                    y = y_acc[:, tk, 512 * n:512 * n + 512]
                    dve.wait_ge(m_ready, at + (M_S + i + 1))
                    dve.tensor_tensor(y, y, banks[:, 4 + i, :], ALU.add).then_inc(m_took, 1)

            dve.wait_ge(late_in, 16 * 6)
            dve.sem_inc(m_took, M_G)
            dve.sem_inc(gu_took, 1)
            dve.sem_inc(y_took_d, 1)
            prepare(0)
            gather_out(0, 1, range(4))
            dve.sem_inc(m_took, M_ALL - M_G - 4)
            plain_chain = chain
            with dve.Fori(0, E_N) as e:
                ms = e * M_ALL + M_ALL

                def echain(ins):
                    ins.then_inc(loop_step, 1)
                    loop_n[0] += 1
                    dve.wait_ge(loop_step, e * LOOP_STEPS + loop_n[0])

                loop_n = [0]

                def e_lo(u):
                    s = N_PRE + u
                    dve.wait_ge(weights_used, e * PER_E + (s - SPLIT_N + 1))
                    c = slice(0, HALF)
                    dve.wait_ge(hi_ready, e * (2 * PER_E) + (2 * s + 1))
                    dve.wait_ge(raw_in[s % RAW_N][0], e * (16 * PER_E // RAW_N) + 16 * (s // RAW_N + 1))
                    dve.tensor_tensor(w_lo[:, s % SPLIT_N, c], raw[:, s % RAW_N, c],
                                      w_hi[:, s % SPLIT_N, c].bitcast(F32), ALU.subtract).then_inc(lo_ready[0], 1)

                def expert(T):
                    loop_n[0] = 0

                    def gated(j):
                        dve.wait_ge(e_silu, e * EJ + (j + 1))
                        dve.wait_ge(weights_used, e * PER_E + (N_PRE + 4 * j + 4))
                        if T == 2 and j:
                            dve.wait_ge(m_ready, ms + (M_H + 2 * j))
                        if T == 1 and j >= 2:
                            dve.wait_ge(m_ready, ms + (M_H + j - 1))
                        for tt in range(T):
                            b = h_at(T, j, tt)
                            ins = dve.tensor_tensor(e_h[:, b, :], e_sil[:, b, :], banks[:, 2 * b + 1, :], ALU.mult)
                        ins.then_inc(gu_took, 1)

                    def h_lo(j):
                        for tt in range(T):
                            n = M_H + T * j + tt
                            b = m_src(ms, n).rearrange("p (k t) -> p k t", k=4)
                            dve.wait_ge(m_hi, e * (2 * EJ) + (2 * j + 2 if T == 1 else 2 * j + tt + 1))
                            sl = (slice(None), slice(4 * j, 4 * j + 4), slice(P * tt, P * tt + P))
                            dve.tensor_tensor(eT_lo[sl], b, eT_hi[sl].bitcast(F32), ALU.subtract).then_inc(m_took, 1)

                    for j in range(1, EJ + 1):
                        for u in range(4 * j, 4 * j + 3):
                            e_lo(u)
                        gated(j - 1)
                        if j == 1:
                            dve.tensor_copy(Wc[:, :, :].rearrange("p s t -> p (s t)"),
                                            m_src(ms, M_W)).then_inc(m_took, 1)
                        if j >= 2:
                            h_lo(j - 2)
                        e_lo(4 * j + 3)
                    e_lo(LAST_H + 1)
                    h_lo(EJ - 1)
                    if T == 1:
                        dve.wait_ge(m_took, ms + (M_H + EJ))
                        dve.sem_inc(m_took, EJ)
                    prepare(e + 1)
                    for u in range(LAST_H + 2, PER_E):
                        e_lo(u)
                        if u - 1 in GATHERS:
                            gather_out(ms, e + 2, [GATHERS.index(u - 1)])
                    dve.wait_ge(weights_used, e * PER_E + (N_PRE + PER_E))
                    for tt in range(T):
                        ins = dve.tensor_copy(y_e[:, tt, 512:D], banks[:, 7 if tt == 0 else 1, :])
                    ins.then_inc(y_took_d, 1)
                    assert loop_n[0] == LOOP_STEPS, loop_n

                e_lo(0)
                e_lo(1)
                scatter_out(ms)
                e_lo(2)
                e_lo(3)
                chain = echain
                chosen = dve.value_load(cnt[0:1, bass.ds(e + 1, 1)], min_val=0, max_val=2 * P)
                with dve.If(chosen > P):
                    expert(2)
                with dve.Else():
                    expert(1)
                dve.wait_ge(m_took, ms + (M_ALL - 1))
                dve.sem_inc(m_took, 1)
            chain = plain_chain
            scatter_out((E_N + 1) * M_ALL)
            residual(y_acc, LAT, 3, 6)

        @block.scalar
        def _(act):
            na, steps, nsplit, nr = [0], [0], [0], [0]

            def chain(ins):
                ins.then_inc(act_step, 1)
                steps[0] += 1
                act.wait_ge(act_step, steps[0])

            def asrc():
                na[0] += 1
                return a_bank(na[0] - 1)

            def took(ins, then=False):
                ins.then_inc(act_took, 1)
                if then:
                    act.wait_ge(act_took, na[0])

            def split_to(n):
                while nsplit[0] < min(n, N_PRE):
                    s = nsplit[0]
                    nsplit[0] += 1
                    if s >= SPLIT_N:
                        act.wait_ge(weights_used, s - SPLIT_N + 1)
                    for half, (a, b) in enumerate(halves(units[s][1])):
                        c = slice(units[s][2] * a, units[s][2] * b)
                        r = slice(HALF * half, HALF * half + units[s][2] * (b - a))
                        act.wait_ge(raw_in[s % RAW_N][half], 16 * (s // RAW_N + 1))
                        act.activation(w_hi[:, s % SPLIT_N, c], raw[:, s % RAW_N, r], ACT.Copy).then_inc(hi_ready, 1)

            def after(name, n):
                split_to(ahead_of(name, n))
                act.wait_ge(weights_used, used(name, n))

            def rstd(n):
                nr[0] += 1
                act.wait_ge(var_ready, nr[0])
                y = st[:, ST_R, 0:n]
                act.activation(y, st[:, ST_VAR, 0:n], ACT.Sqrt).then_inc(sqrt_ready, 1)
                act.wait_ge(rstd_ready, nr[0])

            nss = [0]

            def squares(srcs, inc=True, new=None):
                if inc:
                    chain(act.activation(one_sqrt, ones[:, 0:1], ACT.Sqrt))
                for n, (src, col) in enumerate(srcs):
                    if new is not None:
                        act.wait_ge(h_new, new + n + 1)
                    w = src.shape[-1]
                    ins = act.activation(hn[:, 1, 0:w], src, ACT.Square, accum_out=st[:, ST_SUM, col:col + 1])
                    if n == len(srcs) - 1 and inc:
                        ins.then_inc(ss_ready, 1)
                        nss[0] += 1
                        act.wait_ge(ss_ready, nss[0])
                    else:
                        chain(ins)

            def u_half_and_high(n0, i, layer, which):
                s = 1 if i in LAT else 0
                act.wait_ge(norm_tr, n0 + i + 1)
                if i == 0:
                    act.wait_ge(u_half, n0 + 1)
                if i >= 2:
                    act.wait_ge(u_ready, n0 + i - 1)
                b = asrc()
                for k in range(4):
                    ins = act.activation(ub[i % 2][:, P * (4 + k):P * (4 + k) + P], b[:, P * k:P * k + P], ACT.Identity,
                                         bias=shift_of(layer, which)[:, 4 + k, s:s + 1],
                                         scale=Am[:, 2 * layer + which, 4 + k, s:s + 1])
                took(ins, then=True)
                act.wait_ge(u_half, n0 + i + 1)
                act.activation(uT_hi[:, :, P * i:P * i + P], ub[i % 2][:, :].rearrange("p (k t) -> p k t", k=KD),
                               ACT.Copy).then_inc(u_high, 1)

            def norm(n0, tiles, h_before, ahead=0, site=None):
                if n0 == 0:
                    act.wait_ge(h_in, 32)
                squares([(h[:, tl, :], i) for i, tl in enumerate(tiles)], new=h_before)
                rstd(len(tiles))
                split_to(ahead)
                for i, tl in enumerate(tiles):
                    if n0 + i >= 2:
                        act.wait_ge(norm_tr, n0 + i - 1)
                    act.activation(hn[:, (n0 + i) % 2, :], h[:, tl, :], ACT.Copy,
                                   scale=st[:, ST_R, i:i + 1]).then_inc(hn_ready, 1)
                    if site and i:
                        u_half_and_high(n0, i - 1, *site)
                if site:
                    u_half_and_high(n0, TILES - 1, *site)

            def gate_out(streams):
                for s in streams:
                    gn[0] += 1
                    act.wait_ge(gate_mm, gn[0])
                    took(act.activation(Gb[:, s, 0:512], asrc(), ACT.Copy))
                    took(act.activation(Gb[:, s, 512:D], asrc(), ACT.Copy), then=True)
                    act.sem_inc(gate_rows, 1)

            gn = [0]
            rows_in = [(K[:, :], consts[:, 0:C_KEEP]),
                       (rowsA[0:8, :], c_ctx.rearrange("(k p) -> k p", p=P)),
                       (rowsA[8:16, :], cond[0].rearrange("(k p) -> k p", p=P)),
                       (rowsA[16:80, :], norm_g.rearrange("l i (k p) -> (l i k) p", p=P)),
                       (rowsA[80:83, :], attn_q_norm[0].rearrange("(k p) -> k p", p=P)),
                       (rowsA[83:85, :], attn_kv_norm[0].rearrange("(k p) -> k p", p=P)),
                       (rowsB[0:96, :], mod_b.rearrange("l (k p) -> (l k) p", p=P)),
                       (rowC[0:1, 0:128], attn_qk_norm.rearrange("o a d -> o (a d)")),
                       (rowC[0:1, 128:384], gla_o_norm),
                       (rope[:, :, :], consts[:, C_ROPE:C_ROPE + 192].rearrange("p (j c) -> p j c", j=2))]
            for dst, src in rows_in:
                act.dma_start(dst, src).then_inc(const_in, 16)
            act.dma_start(h[:, 0:2, :], ctx[0].rearrange("(t p) d -> p t d", p=P)).then_inc(h_in, 16)
            act.dma_start(h[:, 2:4, :], x[0].rearrange("(t p) d -> p t d", p=P)).then_inc(h_in, 16)
            act.wait_ge(dve_took, 2)
            chain(act.activation(vecs[:, 0:16], vecs[:, 0:16], ACT.Silu))
            act.activation(cv[:, :, 0:2], vecs[:, 0:16].rearrange("p (s k) -> p k s", k=KD),
                           ACT.Copy).then_inc(c_silu, 1)
            split_to(2)
            norm(0, range(TILES), None, used("z", 0) + 2, (0, 0))

            for n in range(3):
                after("z", 2 * n + 2)
                for tl in (2, 3):
                    took(act.activation(z[:, tl, 480 * n:480 * n + 480], asrc()[:, 0:480], ACT.Copy))
            act.wait_ge(act_took, na[0])
            act.wait_ge(dve_took, dve_at["z"])
            squares([(z[:, tl, a:b], 12 * tl + c) for tl in range(TILES)
                     for c, (a, b) in enumerate(((0, Z_KV), (Z_KV, Z_ROPE)))])
            rstd(48)
            for tl in range(TILES):
                for c, (a, b) in enumerate(((0, Z_KV), (Z_KV, Z_ROPE))):
                    ins = act.activation(z[:, tl, a:b], z[:, tl, a:b], ACT.Copy,
                                         scale=st[:, ST_R, 12 * tl + c:12 * tl + c + 1])
                ins.then_inc(lat_scaled, 1)
            split_to(used("uq", 0) + 2)
            for n in range(2):
                after("uq", n + 1)
                for tl in (2, 3):
                    took(act.activation(qa[:, tl, 384 * n:384 * n + 384], asrc()[:, 0:384], ACT.Copy))
            split_to(used("mods", 0) + 2)

            def copy(dst, src):
                return act.activation(dst, src, ACT.Copy)

            for tl in (2, 3):
                for n in range(2):
                    if (tl, n) == (3, 1):
                        act.wait_ge(weights_used, used("ukv", 1))
                    else:
                        act.wait_ge(ukv_mm, 2 * tl + n + 1)
                    b = asrc().rearrange("p (h c) -> p h c", c=P)
                    copy(ka[:, tl, :].rearrange("p (h c) -> p h c", c=DQ)[:, 4 * n:4 * n + 4, 0:NOPE], b[:, :, 0:NOPE])
                    took(copy(va[:, tl, 256 * n:256 * n + 256].rearrange("p (h c) -> p h c", c=DV), b[:, :, NOPE:P]))

            def q_out(hd):
                w = DQ if hd < HEADS else GD
                act.wait_ge(q_tr, hd + 1)
                took(act.activation(qT[0:w, hd % 2, :], asrc()[0:w, :], ACT.Copy), then=True)
                act.sem_inc(q_sb, 1)

            q_out(0)
            for n in range(NI + 2):
                if n < NI:
                    hd, tl = ITEMS[n]
                    w = P * keys(tl)
                    if n % 4 == 1 and n // 4 + 1 < HEADS + GQ:
                        act.wait_ge(s_done, n)
                        q_out(n // 4 + 1)
                    act.wait_ge(nb_ready, n + 1)
                    if n >= 4:
                        act.wait_ge(p_tr, n - 3)
                    c = n % 8
                    took(act.activation(Pr[:, n % 4, 0:w], asrc()[:, 0:w], ACT.Exp, bias=sm[:, 8 + c:9 + c],
                                        scale=float(DQ if hd < HEADS else GD) ** -0.5,
                                        accum_out=sm[:, 16 + c:17 + c]), then=True)
                    act.sem_inc(exp_done, 1)
                if n >= 2:
                    hd, tl = ITEMS[n - 2]
                    act.wait_ge(p_tr, n - 1)
                    if hd >= 2:
                        act.wait_ge(pv_done, hd - 1)
                    blocks = slice(2, 6) if tl in LAT else slice(0, 2)
                    dst = PT[:, hd % 2, blocks, P * (tl % 2):P * (tl % 2) + P]
                    b = asrc()[:, 0:P * keys(tl)].rearrange("p (k t) -> p k t", k=keys(tl))
                    took(act.activation(dst, b, ACT.Copy), then=True)
                    act.sem_inc(pt_sb, 1)
                if mod_turn(n):
                    split_to(ahead_of("mods", 2 * (mod_turn(n) - MG0) + 2))
            split_to(used("wo", 0) + SPLIT_N - 1)
            act.wait_ge(dve_took, dve_at["attention"])
            for kk in range(KD):
                act.activation(uT_hi[:, kk, :], oT(kk), ACT.Copy).then_inc(o_hi, 1)

            def project_out(name, y, tiles, streams):
                for n in range(2):
                    after(name, 2 * n + 2)
                    for tl in tiles:
                        took(act.activation(y[:, tl, 512 * n:512 * n + 512], asrc(), ACT.Copy), then=(n == 1))
                    if n == 0:
                        gate_out(streams)

            project_out("wo", y_attn, (2, 3), (0, 1))
            act.wait_ge(dve_took, dve_at["wo"])
            squares([(y_attn[:, tl, :], tl) for tl in range(TILES)])
            rstd(TILES)
            norm(4, range(TILES), 0, used("gu", 0) + 2, (0, 1))

            for j in range(NF // 2):
                after("gu", 4 * j + 1)
                for fc in range(2):
                    f = 2 * j + fc
                    if f >= 2:
                        act.wait_ge(dve_took, dve_at["ffn"] + f - 1 + (f - 2) // 2)
                    elif f == 0:
                        act.wait_ge(norm_tr, 8)
                    took(act.activation(sil[:, f % 2, :], asrc(), ACT.Silu), then=True)
                    act.sem_inc(silu_ready, 1)
                split_to(ahead_of("gu", 4 * j + 4))
            split_to(ahead_of("gu", 4 * (NF // 2) + 2))
            for n in range(2):
                for d in range(len(DOWN)):
                    after("down", n * len(DOWN) + d + 1)
                for tl in (2, 3):
                    took(act.activation(y_ffn[:, tl, 512 * n:512 * n + 512], asrc(), ACT.Copy), then=(n == 1))
                if n == 0:
                    gate_out((0, 1))
            act.wait_ge(dve_took, dve_at["down"])
            squares([(y_ffn[:, tl, :], tl) for tl in range(TILES)])
            rstd(TILES)
            norm(8, range(TILES), 4, used("gin", 0) + 2, (1, 0))

            for n, (dst, c0) in enumerate(((g_k, 0), (g_v, 0), (g_v, 512))):
                after("gin", 2 * n + 3)
                for tl in (2, 3):
                    took(act.activation(dst[:, tl, c0:c0 + 512], asrc(), ACT.Copy))
                if n < 2:
                    for i in range(4 * n, 4 * n + 4):
                        act.wait_ge(dve_took, dve_at["gate", i])
                        ins = act.activation(ebuf[:, i % 4, :], ebuf[:, i % 4, :], ACT.Exp)
                    chain(ins)
                    for i in range(4 * n, 4 * n + 4):
                        act.activation(ebuf[:, i % 4, :], ebuf[:, i % 4, :], ACT.Ln, bias=1.0).then_inc(e_ln, 1)
            after("gin", 9)
            took(act.activation(g_q[:, 1, :], asrc(), ACT.Copy))
            for n in range(2):
                after("gin", 11 + 2 * n)
                for j in range(2):
                    took(act.activation(g_g[:, j, 512 * n:512 * n + 512], asrc(), ACT.Silu))
            def decays(it):
                hd, dr = it // 2, it % 2
                act.wait_ge(cum_sb, it + 1)
                if hd >= 2:
                    act.wait_ge(go_mm, hd - 1)
                act.activation(g_qd[:, dr, :], g_qd[:, dr, :], ACT.Exp, scale=1.0 / 16)
                act.activation(g_qf[:, hd % 2, dr, :], g_C[:, dr, :], ACT.Exp, scale=1.0 / 16)
                for i in range(8):
                    at, a, b = kx(dr, i)
                    s0 = a + (128 if dr == 1 and i >= 4 else 0)
                    ins = act.activation(g_KX[:, dr, at + a:at + b], g_C[:, dr, s0:s0 + b - a], ACT.Exp,
                                         bias=bt[:, dr, 1, i:i + 1], scale=-1.0 / 16)
                ins.then_inc(dec_exp, 1)

            def head_out(hd):
                act.wait_ge(go_mm, hd + 1)
                b = asrc().rearrange("p (j v) -> p j v", j=2)
                took(act.activation(g_o[:, :, GDV * hd:GDV * hd + GDV], b, ACT.Copy), then=True)
                squares([(g_o[:, j, GDV * hd:GDV * hd + GDV], 4 * j + hd) for j in range(2)], inc=(hd == GH - 1))

            act.wait_ge(kx_zero, 1)
            decays(0)
            decays(1)
            for dr in range(2):
                act.wait_ge(dve_took, dve_at["tail", dr])
                act.activation(g_a[:, 0:2, dr, :], g_a[:, 0:2, dr, :], ACT.Exp, scale=1.0 / 16).then_inc(tail_exp, 1)
            for it in range(2, 2 * GH):
                decays(it)
                if it == 2:
                    for n in range(4):
                        dr, hp = n // 2, n % 2
                        act.wait_ge(s0_mm, n + 1)
                        dst = g_S[:, dr, 2 * hp:2 * hp + 2, :].rearrange("p h v -> p (h v)")
                        took(act.activation(dst, asrc(), ACT.Copy))
                if it % 2 == 1 and it >= 3:
                    head_out(it // 2 - 1)
            head_out(GH - 1)
            rstd(8)
            split_to(used("gout", 0) + 2)
            project_out("gout", y_gla, (1,), (1,))
            act.wait_ge(dve_took, dve_at["gout"])
            squares([(y_gla[:, j, :], j) for j in range(2)])
            rstd(2)
            norm(12, LAT, 8)
            act.wait_ge(lg_ready, 1)
            act.activation(lg, lg, ACT.Exp).then_inc(lg_exp, 1)

            act.wait_ge(tab_ready, 1)
            act.sem_inc(y_took_a, 1)
            with act.Fori(0, E_N) as e:
                ms = e * M_ALL + M_ALL

                def e_hi(u):
                    s = N_PRE + u
                    act.wait_ge(weights_used, e * PER_E + (s - SPLIT_N + 1))
                    for half in range(2):
                        c = slice(HALF * half, HALF * (half + 1))
                        act.wait_ge(raw_in[s % RAW_N][half], e * (16 * PER_E // RAW_N) + 16 * (s // RAW_N + 1))
                        act.activation(w_hi[:, s % SPLIT_N, c], raw[:, s % RAW_N, c], ACT.Copy).then_inc(hi_ready, 1)

                def expert(T):
                    def e_silus(j):
                        act.wait_ge(weights_used, e * PER_E + (N_PRE + 4 * j + 2))
                        act.wait_ge(gu_took, e * EJ + gu_free(T, j))
                        for tt in range(T):
                            b = h_at(T, j, tt)
                            ins = act.activation(e_sil[:, b, :], banks[:, 2 * b, :], ACT.Silu)
                        ins.then_inc(e_silu, 1)

                    def h_hi(j):
                        for tt in range(T):
                            n = M_H + T * j + tt
                            act.wait_ge(m_ready, ms + (n + 1))
                            b = banks[:, 4 + n % 2, :].rearrange("p (k t) -> p k t", k=4)
                            act.activation(eT_hi[:, 4 * j:4 * j + 4, P * tt:P * tt + P], b, ACT.Copy)\
                                .then_inc(m_hi, 2 // T)

                    for j in range(1, EJ + 1):
                        for u in range(4 * j, 4 * j + 3):
                            e_hi(u)
                        e_silus(j - 1)
                        if j >= 2:
                            h_hi(j - 2)
                        e_hi(4 * j + 3)
                    e_hi(LAST_H + 1)
                    h_hi(EJ - 1)
                    for u in range(LAST_H + 2, PER_E):
                        e_hi(u)
                    act.wait_ge(weights_used, e * PER_E + (N_PRE + PER_E))
                    act.wait_ge(m_ready, ms + (M_S + 4))
                    for tt in range(T):
                        ins = act.activation(y_e[:, tt, 0:512], banks[:, 6 if tt == 0 else 0, :], ACT.Copy)
                    ins.then_inc(y_took_a, 1)

                for u in range(4):
                    e_hi(u)
                chosen = act.value_load(cnt[0:1, bass.ds(e + 1, 1)], min_val=0, max_val=2 * P)
                with act.If(chosen > P):
                    expert(2)
                with act.Else():
                    expert(1)
            act.wait_ge(m_took, (E_N + 1) * M_ALL + 4)
            squares([(y_acc[:, j, :], j) for j in range(2)])
            gate_out((1,))
            rstd(2)

        @block.gpsimd
        def _(pool):
            def diagonals(site, streams):
                for s in streams:
                    for k in range(KD):
                        ins = pool.tensor_scalar(diagonal(site, s)[:, P * k:P * k + P], ident, Gm[:, site, k, s:s + 1],
                                                 None, ALU.mult)
                    ins.then_inc(diag_ready, 1)

            pool.wait_ge(mods_ready, 1)
            diagonals(0, (0, 1))
            pool.wait_ge(weights_used, used("down", 1))
            diagonals(1, (0, 1))
            pool.wait_ge(h_new, 8)
            pool.dma_start(mask[:, :, :], consts[:, C_MASK:C_MASK + 768].rearrange("p (d c) -> p d c", d=2))\
                .then_inc(late_in, 16)
            pool.dma_start(wg2[0:GRANK, :, :], gla_w_gate2[0].rearrange("d r n -> r d n")).then_inc(late_in, 16)
            pool.dma_start(wg2[GRANK:GRANK + 1, :, :], gla_b_gate).then_inc(late_in, 16)
            pool.wait_ge(u_ready, 12)
            pool.memset(rT[0:32, :, :], 1.0).then_inc(rt_one, 1)
            pool.wait_ge(z2_mm, 8)
            pool.wait_ge(mods_ready, 2)
            diagonals(2, (1,))
            pool.wait_ge(weights_used, used("gin", 13))
            pool.memset(g_KX[:, :, :], 0.0).then_inc(kx_zero, 1)
            pool.wait_ge(at_mm, 2 * GH)
            pool.dma_start(wr, moe_w_router[0].rearrange("(k p) e -> p k e", p=P)).then_inc(late_in, 16)
            pool.dma_start(brow[0:1, :], moe_b_router).then_inc(late_in, 16)
            pool.dma_start(iota[:, :], consts[:, C_IOTA:C_IOTA + 256]).then_inc(late_in, 16)
            with pool.Fori(0, E_N) as e:
                for u in range(PER_E):
                    s = N_PRE + u
                    c = slice(HALF, UNIT)
                    pool.wait_ge(weights_used, e * PER_E + (s - SPLIT_N + 1))
                    pool.wait_ge(hi_ready, e * (2 * PER_E) + (2 * s + 2))
                    pool.wait_ge(raw_in[s % RAW_N][1], e * (16 * PER_E // RAW_N) + 16 * (s // RAW_N + 1))
                    pool.tensor_tensor(w_lo[:, s % SPLIT_N, c], raw[:, s % RAW_N, c],
                                       w_hi[:, s % SPLIT_N, c].bitcast(F32), ALU.subtract).then_inc(lo_ready[1], 1)
            pool.wait_ge(ug_ready, E_N + 1)
            diagonals(3, (1,))


def _constants(np):
    k = np.zeros((P, C_ALL), np.float32)
    k[:, C_ID:C_ID + P] = np.eye(P)
    k[:, C_ONE:C_ONE + P] = 1
    k[0:4, C_PAIR:C_PAIR + 2] = np.tile(np.eye(2), (2, 1))
    s, t = np.arange(256)[:, None], np.arange(256)[None, :]
    tri = [(s <= t).astype(np.float32), (s >= t).astype(np.float32)]
    for at, m in zip((C_TRI_F, C_TRI_B), tri):
        k[:, at:at + 512] = m.reshape(2, P, 256).transpose(1, 0, 2).reshape(P, 512)
    blocks = ([(0, 0), (1, 0), (1, 1)], [(0, 0), (0, 1), (1, 1)])
    for d in range(2):
        for n, (tt, j) in enumerate(blocks[d]):
            at = C_MASK + 384 * d + P * n
            k[:, at:at + P] = tri[d][P * j:P * j + P, P * tt:P * tt + P]
    k[:, C_IOTA:C_IOTA + 256] = np.arange(256)
    tok = np.arange(256)
    pos = np.stack([tok // 64, tok % 64]).astype(np.float32)
    for at, n in ((0, 16), (64, 8)):
        freq = (np.float32(10000.0) ** (-np.arange(0, 2 * n, 2, dtype=np.float32) / np.float32(2 * n)))
        ang = pos[:, :, None] * freq[None, None, :].astype(np.float32)
        for f, fn in enumerate((np.cos, np.sin)):
            v = fn(ang.astype(np.float32)).astype(np.float32).transpose(1, 0, 2).reshape(256, 2 * n)
            for j in range(2):
                c0 = C_ROPE + 96 * j + at + 2 * n * f
                k[:, c0:c0 + 2 * n] = v[P * j:P * j + P]
    return k


_INS = ['x', 'c', 'ctx', 'c_ctx', 'mod_w', 'mod_b', 'norm_g', 'attn_w_in', 'attn_q_norm', 'attn_w_uq', 'attn_kv_norm',
        'attn_w_ukv', 'attn_qk_norm', 'attn_w_out', 'gla_w_in', 'gla_w_gate2', 'gla_b_gate', 'gla_o_norm',
        'gla_w_out', 'ffn_w_gate', 'ffn_w_up', 'ffn_w_down', 'moe_w_router', 'moe_b_router', 'moe_w_gate',
        'moe_w_up', 'moe_w_down']


def kernel(**inputs):
    import numpy as _np
    import concourse.bacc as _bacc
    from concourse import mybir as _mybir
    from concourse.bass_utils import run_bass_kernel_spmd as _run

    nc = _bacc.Bacc("TRN2", target_bir_lowering=False, num_devices=1)
    arrays, args = {}, []
    for name in _INS:
        a = _np.ascontiguousarray(inputs[name])
        arrays[f"in_{name}_dram"] = a
        args.append(nc.dram_tensor(f"in_{name}_dram", a.shape, _mybir.dt.from_np(a.dtype), kind="ExternalInput").ap())
    k = _constants(_np)
    arrays["in_consts_dram"] = k
    args.append(nc.dram_tensor("in_consts_dram", k.shape, _mybir.dt.from_np(k.dtype), kind="ExternalInput").ap())
    args.append(nc.dram_tensor("out_0_dram", (1, 256, D), _mybir.dt.float32, kind="ExternalOutput").ap())
    hybrid_block(nc, *args)
    r = _run(nc, [arrays], core_ids=[0])
    return r.results[0]["out_0_dram"]
```
